# Optimizing a Trainium2 kernel written in Bass

```python
import math
import jax, jax.numpy as jnp
from jax import lax
import numpy as np

D_MODEL = 1024
BATCH = 1
SEQ = 512
DEPTH = 2

GRID_W = 64
CTX_LEN = 256
EPS = 1e-6
ADA_SCALE = 0.5
HEAD_DIM = 128
BLOCK = 128
A_Q_HEADS = 8
A_KV_HEADS = 2
A_REP = A_Q_HEADS // A_KV_HEADS
WINDOW = 128
B_Q_HEADS = 8
B_KV_HEADS = 2
B_REP = B_Q_HEADS // B_KV_HEADS
ROPE_THETA = 10000.0
A_Q = A_Q_HEADS * HEAD_DIM
A_KV = A_KV_HEADS * HEAD_DIM
B_Q = B_Q_HEADS * HEAD_DIM
B_KV = B_KV_HEADS * HEAD_DIM
ATTN_SPLITS = [A_Q, A_KV, A_KV, A_Q, B_Q, B_KV, B_KV, B_Q]
ATTN_IN = sum(ATTN_SPLITS)
ATTN_WIDTH = A_Q + B_Q
D_INNER = 2 * D_MODEL
SSM_HEAD_DIM = 64
SSM_HEADS = D_INNER // SSM_HEAD_DIM
SSM_GROUPS = 8
D_STATE = 128
D_CONV = 3
SSM_CHUNK = 128
CONV_DIM = D_INNER + 2 * SSM_GROUPS * D_STATE
SSM_SPLITS = [D_INNER, CONV_DIM, 2 * SSM_HEADS]
SSM_IN = sum(SSM_SPLITS)

kernel_name = "hybrid_ctx_prefix_attn_ssd_backbone"

def split_cols(t, sizes):
    idx = np.cumsum(sizes)[:-1].tolist()
    return jnp.split(t, idx, axis=-1)

def rms_norm(x, w):
    xf = x.astype(jnp.float32)
    y = xf * lax.rsqrt(jnp.mean(xf * xf, axis=-1, keepdims=True) + EPS)
    return (y * w.astype(jnp.float32)).astype(x.dtype)

def axial_rope_tables(n_rows):
    row = jnp.repeat(jnp.arange(n_rows), GRID_W).astype(jnp.float32)
    col = jnp.tile(jnp.arange(GRID_W), n_rows).astype(jnp.float32)
    n_freq = HEAD_DIM // 4
    inv = 1.0 / (ROPE_THETA ** (jnp.arange(n_freq, dtype=jnp.float32) / n_freq))
    ang = jnp.concatenate([row[:, None] * inv, col[:, None] * inv], axis=-1)
    return jnp.cos(ang), jnp.sin(ang)

def apply_rope(x, cos, sin):
    xp = x.astype(jnp.float32).reshape(*x.shape[:-1], HEAD_DIM // 2, 2)
    x0, x1 = xp[..., 0], xp[..., 1]
    c = cos[None, :, None, :]
    s = sin[None, :, None, :]
    out = jnp.stack([x0 * c - x1 * s, x0 * s + x1 * c], axis=-1)
    return out.reshape(x.shape).astype(x.dtype)

def to_heads(t, n):
    return t.reshape(*t.shape[:-1], n, HEAD_DIM)

def group_q(q, n_kv):
    return q.reshape(q.shape[0], q.shape[1], n_kv, q.shape[2] // n_kv, HEAD_DIM)

def gqa_softmax(q, segments, sink):
    scale = HEAD_DIM ** -0.5
    logits = []
    for k, v, mask in segments:
        s = jnp.einsum('bqgrd,bkgd->bgrqk', q, k).astype(jnp.float32) * scale
        if mask is not None:
            s = jnp.where(mask, s, -jnp.inf)
        logits.append(s)
    if sink is not None:
        sk = sink.astype(jnp.float32)[None, :, :, None, None]
        logits.append(jnp.broadcast_to(sk, logits[-1].shape[:-1] + (1,)))
    p = jax.nn.softmax(jnp.concatenate(logits, axis=-1), axis=-1)
    out = None
    off = 0
    for k, v, _ in segments:
        n = k.shape[1]
        o = jnp.einsum('bgrqk,bkgd->bqgrd', p[..., off:off + n].astype(v.dtype), v)
        out = o if out is None else out + o
        off += n
    return out

def windowed_attn(q, k, v, kc, vc, sink):
    b, T = q.shape[:2]
    nb = T // BLOCK
    pad = ((0, 0), (BLOCK, BLOCK), (0, 0), (0, 0))
    kp = jnp.pad(k, pad)
    vp = jnp.pad(v, pad)
    qoff = jnp.arange(BLOCK)
    koff = jnp.arange(3 * BLOCK) - BLOCK

    def block(i):
        s = i * BLOCK
        qi = lax.dynamic_slice_in_dim(q, s, BLOCK, axis=1)
        ki = lax.dynamic_slice_in_dim(kp, s, 3 * BLOCK, axis=1)
        vi = lax.dynamic_slice_in_dim(vp, s, 3 * BLOCK, axis=1)
        qpos = s + qoff
        kpos = s + koff
        mask = (jnp.abs(qpos[:, None] - kpos[None, :]) <= WINDOW) & (kpos >= 0)[None, :] & (kpos < T)[None, :]
        return gqa_softmax(qi, [(ki, vi, mask), (kc, vc, None)], sink)

    out = lax.map(block, jnp.arange(nb))
    return jnp.moveaxis(out, 0, 1).reshape(b, T, -1)

def dense_attn(q, k, v, kc, vc):
    b, T = q.shape[:2]
    nb = T // BLOCK

    def block(i):
        qi = lax.dynamic_slice_in_dim(q, i * BLOCK, BLOCK, axis=1)
        return gqa_softmax(qi, [(k, v, None), (kc, vc, None)], None)

    out = lax.map(block, jnp.arange(nb))
    return jnp.moveaxis(out, 0, 1).reshape(b, T, -1)

def attn_mixer(h, hc, w_in, w_out, sink, q_norm, k_norm, cos, sin, need_ctx):
    qa, ka, va, ga, qb, kb, vb, gb = split_cols(h @ w_in, ATTN_SPLITS)
    qac, kac, vac, gac, qbc, kbc, vbc, gbc = split_cols(hc @ w_in, ATTN_SPLITS)
    sink_g = sink.reshape(A_KV_HEADS, A_REP)
    qa = apply_rope(to_heads(qa, A_Q_HEADS), cos, sin)
    ka = apply_rope(to_heads(ka, A_KV_HEADS), cos, sin)
    va = to_heads(va, A_KV_HEADS)
    kac = to_heads(kac, A_KV_HEADS)
    vac = to_heads(vac, A_KV_HEADS)
    ya = windowed_attn(group_q(qa, A_KV_HEADS), ka, va, kac, vac, sink_g)
    qb = apply_rope(rms_norm(to_heads(qb, B_Q_HEADS), q_norm), cos, sin)
    kb = apply_rope(rms_norm(to_heads(kb, B_KV_HEADS), k_norm), cos, sin)
    vb = to_heads(vb, B_KV_HEADS)
    kbc = rms_norm(to_heads(kbc, B_KV_HEADS), k_norm)
    vbc = to_heads(vbc, B_KV_HEADS)
    yb = dense_attn(group_q(qb, B_KV_HEADS), kb, vb, kbc, vbc)
    y = jnp.concatenate([ya * jax.nn.silu(ga), yb * jax.nn.silu(gb)], axis=-1) @ w_out
    if not need_ctx:
        return y, None
    b, C = hc.shape[:2]
    yac = gqa_softmax(group_q(to_heads(qac, A_Q_HEADS), A_KV_HEADS), [(kac, vac, None)], sink_g).reshape(b, C, A_Q)
    qbc = rms_norm(to_heads(qbc, B_Q_HEADS), q_norm)
    ybc = gqa_softmax(group_q(qbc, B_KV_HEADS), [(kbc, vbc, None)], None).reshape(b, C, B_Q)
    yc = jnp.concatenate([yac * jax.nn.silu(gac), ybc * jax.nn.silu(gbc)], axis=-1) @ w_out
    return y, yc

def dwconv_centered(u, w, bias):
    L = u.shape[1]
    p = D_CONV // 2
    up = jnp.pad(u, ((0, 0), (p, p), (0, 0)))
    out = bias
    for j in range(D_CONV):
        out = out + w[j] * up[:, j:j + L]
    return out

def ssd_chunked(x, dt, A, Bm, Cm, h0):
    b, L, H, P = x.shape
    G, N = Bm.shape[2], Bm.shape[3]
    R = H // G
    Q = SSM_CHUNK
    nc = L // Q
    f32 = jnp.float32
    xdt = x.astype(f32) * dt[..., None]
    a = dt * A
    tri = jnp.tril(jnp.ones((Q, Q), dtype=bool))

    def chunks(t):
        return jnp.moveaxis(t.reshape(b, nc, Q, *t.shape[2:]), 1, 0)

    def step(h, inp):
        xc, ac, Bc, Cc = inp
        acum = jnp.cumsum(ac, axis=1)
        seg = acum[:, :, None, :] - acum[:, None, :, :]
        Lm = jnp.exp(jnp.where(tri[None, :, :, None], seg, -jnp.inf)).reshape(b, Q, Q, G, R)
        CB = jnp.einsum('blgn,bsgn->bgls', Cc, Bc)
        xg = xc.reshape(b, Q, G, R, P)
        y_diag = jnp.einsum('bgls,blsgr,bsgrp->blgrp', CB, Lm, xg)
        hg = h.reshape(b, G, R, P, N)
        y_off = jnp.einsum('blgn,bgrpn->blgrp', Cc, hg) * jnp.exp(acum).reshape(b, Q, G, R)[..., None]
        w_end = jnp.exp(acum[:, -1:, :] - acum).reshape(b, Q, G, R)
        h_new = jnp.exp(acum[:, -1])[:, :, None, None] * h + jnp.einsum('bsgn,bsgr,bsgrp->bgrpn', Bc, w_end, xg).reshape(b, H, P, N)
        return h_new, (y_diag + y_off).reshape(b, Q, H, P)

    h_fin, ys = lax.scan(step, h0.astype(f32), (chunks(xdt), chunks(a), chunks(Bm.astype(f32)), chunks(Cm.astype(f32))))
    y = jnp.moveaxis(ys, 0, 1).reshape(b, L, H, P)
    return y.astype(x.dtype), h_fin

def gated_rms_norm(y, z, w):
    g = (y * jax.nn.silu(z)).astype(jnp.float32)
    gr = g.reshape(*g.shape[:-1], SSM_GROUPS, D_INNER // SSM_GROUPS)
    gr = gr * lax.rsqrt(jnp.mean(gr * gr, axis=-1, keepdims=True) + EPS)
    return (gr.reshape(g.shape) * w.astype(jnp.float32)).astype(y.dtype)

def ssm_mixer(h, hc, w_in, conv_w, conv_b, dt_bias, a_log, d_skip, norm_w, w_out, need_ctx):
    def prep(u):
        bsz, L = u.shape[:2]
        z, xbc, dt = split_cols(u @ w_in, SSM_SPLITS)
        xbc = jax.nn.silu(dwconv_centered(xbc, conv_w, conv_b))
        xs, Bm, Cm = split_cols(xbc, [D_INNER, SSM_GROUPS * D_STATE, SSM_GROUPS * D_STATE])
        xs = xs.reshape(bsz, L, SSM_HEADS, SSM_HEAD_DIM)
        Bm = Bm.reshape(bsz, L, SSM_GROUPS, D_STATE)
        Cm = Cm.reshape(bsz, L, SSM_GROUPS, D_STATE)
        dt = jax.nn.softplus(dt.astype(jnp.float32).reshape(bsz, L, 2, SSM_HEADS) + dt_bias.astype(jnp.float32))
        return z, xs, Bm, Cm, dt

    rev = lambda t: t[:, ::-1]
    A = -jnp.exp(a_log.astype(jnp.float32))
    zc, xc, Bc, Cc, dtc = prep(hc)
    z, xl, Bl, Cl, dtl = prep(h)
    h0 = jnp.zeros((h.shape[0], SSM_HEADS, SSM_HEAD_DIM, D_STATE), jnp.float32)
    yc_f, sc_f = ssd_chunked(xc, dtc[:, :, 0], A[0], Bc, Cc, h0)
    yc_b, sc_b = ssd_chunked(rev(xc), rev(dtc[:, :, 1]), A[1], rev(Bc), rev(Cc), h0)
    y_f, _ = ssd_chunked(xl, dtl[:, :, 0], A[0], Bl, Cl, sc_f)
    y_b, _ = ssd_chunked(rev(xl), rev(dtl[:, :, 1]), A[1], rev(Bl), rev(Cl), sc_b)

    def finish(yf, yb_rev, xs, zz):
        y = yf + rev(yb_rev) + d_skip[:, None] * xs
        y = gated_rms_norm(y.reshape(*xs.shape[:2], D_INNER), zz, norm_w)
        return y @ w_out

    out = finish(y_f, y_b, xl, z)
    out_c = finish(yc_f, yc_b, xc, zc) if need_ctx else None
    return out, out_c

def setup_inputs(seed: int = 0) -> dict:
    key = jax.random.key(seed)
    ks = jax.random.split(key, 24)
    na = (DEPTH + 1) // 2
    ns = DEPTH // 2
    nrm = lambda k, shape, scale: jax.random.normal(k, shape, jnp.float32) * scale
    dt0 = jnp.exp(jax.random.uniform(ks[16], (ns, 2, SSM_HEADS), jnp.float32, math.log(1e-3), math.log(1e-1)))
    return {
        "x": nrm(ks[0], (BATCH, SEQ, D_MODEL), 1.0),
        "c": nrm(ks[1], (BATCH, D_MODEL), 1.0),
        "ctx": nrm(ks[2], (BATCH, CTX_LEN, D_MODEL), 1.0),
        "c_ctx": nrm(ks[3], (D_MODEL,), 1.0),
        "w_ada": nrm(ks[4], (DEPTH, D_MODEL, 3 * D_MODEL), ADA_SCALE * D_MODEL ** -0.5),
        "b_ada": nrm(ks[5], (DEPTH, 3 * D_MODEL), 0.01),
        "norm_pre": 1.0 + nrm(ks[6], (DEPTH, D_MODEL), 0.05),
        "norm_post": 1.0 + nrm(ks[7], (DEPTH, D_MODEL), 0.05),
        "attn_w_in": nrm(ks[8], (na, D_MODEL, ATTN_IN), D_MODEL ** -0.5),
        "attn_w_out": nrm(ks[9], (na, ATTN_WIDTH, D_MODEL), ATTN_WIDTH ** -0.5),
        "attn_sink": nrm(ks[10], (na, A_Q_HEADS), 0.5),
        "attn_q_norm": 1.0 + nrm(ks[11], (na, HEAD_DIM), 0.05),
        "attn_k_norm": 1.0 + nrm(ks[12], (na, HEAD_DIM), 0.05),
        "ssm_w_in": nrm(ks[13], (ns, D_MODEL, SSM_IN), D_MODEL ** -0.5),
        "ssm_conv_w": nrm(ks[14], (ns, D_CONV, CONV_DIM), D_CONV ** -0.5),
        "ssm_conv_b": nrm(ks[15], (ns, CONV_DIM), 0.01),
        "ssm_dt_bias": dt0 + jnp.log(-jnp.expm1(-dt0)),
        "ssm_a_log": jnp.log(jax.random.uniform(ks[17], (ns, 2, SSM_HEADS), jnp.float32, 1.0, 16.0)),
        "ssm_d": 1.0 + nrm(ks[18], (ns, SSM_HEADS), 0.1),
        "ssm_norm": 1.0 + nrm(ks[19], (ns, D_INNER), 0.05),
        "ssm_w_out": nrm(ks[20], (ns, D_INNER, D_MODEL), D_INNER ** -0.5),
    }

def reference(x, c, ctx, c_ctx, w_ada, b_ada, norm_pre, norm_post, attn_w_in, attn_w_out, attn_sink,
              attn_q_norm, attn_k_norm, ssm_w_in, ssm_conv_w, ssm_conv_b, ssm_dt_bias, ssm_a_log, ssm_d,
              ssm_norm, ssm_w_out):
    T = x.shape[1]
    ROWS = T // GRID_W
    cos, sin = axial_rope_tables(ROWS)
    silu_c = jax.nn.silu(c)
    silu_cc = jax.nn.silu(c_ctx)
    for l in range(DEPTH):
        need_ctx = l < DEPTH - 1
        sh, sc, gt = jnp.split(silu_c @ w_ada[l] + b_ada[l], 3, axis=-1)
        shc, scc, gtc = jnp.split(silu_cc @ w_ada[l] + b_ada[l], 3, axis=-1)
        h = rms_norm(x, norm_pre[l]) * (1.0 + sc[:, None, :]) + sh[:, None, :]
        hc = rms_norm(ctx, norm_pre[l]) * (1.0 + scc) + shc
        i = l // 2
        if l % 2 == 0:
            y, yc = attn_mixer(h, hc, attn_w_in[i], attn_w_out[i], attn_sink[i], attn_q_norm[i],
                               attn_k_norm[i], cos, sin, need_ctx)
        else:
            y, yc = ssm_mixer(h, hc, ssm_w_in[i], ssm_conv_w[i], ssm_conv_b[i], ssm_dt_bias[i],
                              ssm_a_log[i], ssm_d[i], ssm_norm[i], ssm_w_out[i], need_ctx)
        x = x + gt[:, None, :] * rms_norm(y, norm_post[l])
        if need_ctx:
            ctx = ctx + gtc * rms_norm(yc, norm_post[l])
    return x


_drawn_inputs = setup_inputs


def setup_inputs(seed=0):
    import zlib

    import numpy as np

    out = dict(_drawn_inputs(seed))
    spreads = {}
    factors = {'b_ada': 2.812,
     'norm_post': 2.793,
     'attn_sink': 8.0,
     'attn_q_norm': 8.0,
     'attn_k_norm': 8.0,
     'ssm_conv_b': 8.0,
     'ssm_d': 4.044,
     'ssm_norm': 4.054}
    for name, (base, spread) in spreads.items():
        noise = np.random.default_rng([zlib.crc32(name.encode()), seed]).standard_normal(out[name].shape)
        drawn = base * np.exp(spread * noise) if base else spread * noise
        out[name] = __import__('jax').numpy.asarray(drawn.astype(out[name].dtype))
    for name, factor in factors.items():
        out[name] = (out[name] * factor).astype(out[name].dtype)
    return out
```

```python
import concourse.bass as bass
from concourse import mybir
from contextlib import ExitStack

P = 128
D_MODEL, SEQ, CTX = 1024, 512, 256
TOK = CTX + SEQ
TT = TOK // P
CT = CTX // P
KT = D_MODEL // P
EPS = 1e-6
HEADS = 16
GROUPS = 4
SCALE = P ** -0.5
NR = 4
ADA = 3 * KT
ADA_EARLY = 2 * KT
MASKED = -float(2 ** 100)
SSM_GROUPS = 8
SSM_HEADS = 32
GH = SSM_HEADS // SSM_GROUPS
HD = 64
GW = GH * HD
LT = SEQ // P
DIRS = 2


def column_places():
    at, where = 0, {}
    for name, n in (("b_ada", 2 * ADA), ("pre", 2 * KT), ("post", 2 * KT), ("conv_w", 3 * 32), ("conv_b", 32),
                    ("ssm_norm", 16), ("q_norm", 1), ("k_norm", 1)):
        where[name] = (at, at + n)
        at += n
    return where, at


COLS, NCOLS = column_places()
R_DT, R_NACU, R_EA, R_WE, R_DEC, R_D = 0, 4, 8, 12, 17, 22
TAB_ROWS = 23
STEPS = 5
FWD, BWD = (0, 1, 2, 3, 4), (1, 0, 5, 4, 3)
ROWS = {"sink": (0, 8), "a_log": (8, 72), "dt_bias": (72, 136), "d": (136, 168)}
NROWS = 168


def build(nc, io):
    f32, f32r = mybir.dt.float32, mybir.dt.float32r
    ALU, ACT, AX = mybir.AluOpType, mybir.ActivationFunctionType, mybir.AxisListType
    PE_, V_, A_, G_ = nc.tensor, nc.vector, nc.scalar, nc.gpsimd
    ds = bass.ds

    keep = ExitStack()

    def sbuf(stack, name, shape, dt=f32):
        return stack.enter_context(nc.sbuf_tensor(name, shape, dt))

    def psum(name, shape):
        return keep.enter_context(nc.psum_tensor(name, shape, f32))

    def sem(name):
        return keep.enter_context(nc.semaphore(name))

    def f(ap):
        return ap.bitcast(f32)

    wraw = sbuf(keep, "wraw", [P, NR, KT, P])
    whi = sbuf(keep, "whi", [P, 2, KT, P], f32r)
    wlo = sbuf(keep, "wlo", [P, 2, KT, P], f32r)
    cols = sbuf(keep, "cols", [P, NCOLS])
    cvec = sbuf(keep, "cvec", [P, KT, 2])
    cth = sbuf(keep, "cth", [P, KT, 2])
    csilu = sbuf(keep, "csilu", [P, KT, 2])
    ident = sbuf(keep, "ident", [P, P])
    identr = sbuf(keep, "identr", [P, P], f32r)
    ones = sbuf(keep, "ones", [P, P])
    mod = sbuf(keep, "mod", [P, 2 * ADA, 2])
    gain = sbuf(keep, "gain", [P, 2, KT, 2])
    ssq = sbuf(keep, "ssq", [P, 4, 8])
    vvar = sbuf(keep, "vvar", [P, 4, 8])
    rstd = sbuf(keep, "rstd", [P, 4, 8])
    half = sbuf(keep, "half", [P, 8])
    nothing = sbuf(keep, "nothing", [P, 1])
    gcolx = sbuf(keep, "gcolx", [P, 2, KT, 2])

    psL = [psum("psL0", [P, 512]), psum("psL1", [P, 512])]
    psC = psum("psC", [P, 512])
    psS = psum("psS", [P, 1024])
    psT = psum("psT", [P, 1024])
    psV = psum("psV", [P, 512])
    tok_bank = [psL[0][:, :], psL[1][:, :], psC[:, :], psS[:, 0:512], psS[:, 512:1024], psV[:, :]]

    ph = ExitStack()
    hhi = sbuf(ph, "hhi", [P, KT, TOK], f32r)
    hlo = sbuf(ph, "hlo", [P, KT, TOK], f32r)
    with ExitStack() as s:
        X0 = sbuf(s, "X0", [P, TT, D_MODEL])
        HS0 = sbuf(s, "HS0", [P, 2, TOK])
        junk0 = sbuf(s, "junk0", [P, D_MODEL])
    with ExitStack() as s:
        rowt = sbuf(s, "rowt", [P, 8])
        nsink = sbuf(s, "nsink", [P, 8])
        costab = sbuf(s, "costab", [P, SEQ])
        sintab = sbuf(s, "sintab", [P, SEQ])
        maskr = sbuf(s, "maskr", [P, 2, P], f32r)
        Khi = sbuf(s, "Khi", [P, GROUPS, TOK], f32r)
        Klo = sbuf(s, "Klo", [P, GROUPS, TOK], f32r)
        Vhi = sbuf(s, "Vhi", [P, TT, GROUPS * P], f32r)
        Vlo = sbuf(s, "Vlo", [P, TT, GROUPS * P], f32r)
        PThi = sbuf(s, "PThi", [P, TT, 2 * P], f32r)
        PTlo = sbuf(s, "PTlo", [P, TT, 2 * P], f32r)
        QR = sbuf(s, "QR", [P, TOK])
        SQ = sbuf(s, "SQ", [P, TOK])
        T1 = sbuf(s, "T1", [P, SEQ])
        T2 = sbuf(s, "T2", [P, SEQ])
        Qhi = sbuf(s, "Qhi", [P, 2, TOK], f32r)
        Qlo = sbuf(s, "Qlo", [P, 2, TOK], f32r)
        TH = sbuf(s, "TH", [P, TOK])
        SG = sbuf(s, "SG", [P, 2, TOK])
        PR = sbuf(s, "PR", [P, 2, TOK])
        Yst = sbuf(s, "Yst", [P, 2, TOK])
        smax = sbuf(s, "smax", [P, 2])
        nmax = sbuf(s, "nmax", [P, 2])
        esum = sbuf(s, "esum", [P, 2])
        esink = sbuf(s, "esink", [P, 2])
        eall = sbuf(s, "eall", [P, 2])
        rinv = sbuf(s, "rinv", [P, 2])
        vq = sbuf(s, "vq", [P, TT])
        rq = sbuf(s, "rq", [P, 2, TT])
        dgk = sbuf(s, "dgk", [P, TT, P])
    ph.close()
    ph = ExitStack()
    X1 = sbuf(ph, "X1", [P, TT, D_MODEL])
    with ExitStack() as s:
        Yhi = sbuf(s, "Yhi", [P, HEADS, TOK], f32r)
        Ylo = sbuf(s, "Ylo", [P, HEADS, TOK], f32r)
        Yraw = sbuf(s, "Yraw", [P, 2, TOK])
        Yo = sbuf(s, "Yo", [P, TT, D_MODEL])
        grow = sbuf(s, "grow", [P, 2, D_MODEL])
        dg = sbuf(s, "dg", [P, KT, P])
        junk1 = sbuf(s, "junk1", [P, 512])
    h1hi = sbuf(ph, "h1hi", [P, KT, TOK], f32r)
    h1lo = sbuf(ph, "h1lo", [P, KT, TOK], f32r)
    with ExitStack() as s:
        XN = sbuf(s, "XN", [P, TT, D_MODEL])
        HS1 = sbuf(s, "HS1", [P, 2, TOK])
        junk2 = sbuf(s, "junk2", [P, D_MODEL])
    x1flat = X1[:, :, :].rearrange("p t d -> p (t d)")
    places = {}
    UEND = 3 * TOK + SEQ
    at = 0
    for name, n in (("U", 3 * TOK + SEQ), ("sz", LT * GW), ("E", DIRS * GH * P), ("y1", 2 * GW), ("y2", GW),
                    ("y3", GW), ("yg", GW)):
        places[name] = x1flat[:, at:at + n]
        at += n
    U, sz, E, y1, y2, y3, yg = places.values()
    U = [U[:, i * TOK:min((i + 1) * TOK, 3 * TOK + SEQ)] for i in range(4)]
    with ExitStack() as s:
        rows1 = sbuf(s, "rows1", [P, NROWS - 8])
        TAB = sbuf(s, "TAB", [P, TAB_ROWS, 2 * SSM_HEADS])
        GP = sbuf(s, "GP", [P, TAB_ROWS, DIRS, GH])
        acu = sbuf(s, "acu", [P, TT, 2 * SSM_HEADS])
        ahi = sbuf(s, "ahi", [P, TT, 2 * SSM_HEADS], f32r)
        alo = sbuf(s, "alo", [P, TT, 2 * SSM_HEADS], f32r)
        aghi = sbuf(s, "aghi", [P, LT, DIRS, GH], f32r)
        aglo = sbuf(s, "aglo", [P, LT, DIRS, GH], f32r)
        trir = sbuf(s, "trir", [P, DIRS, P], f32r)
        onesr = sbuf(s, "onesr", [P, P], f32r)
        negr = sbuf(s, "negr", [P, DIRS, P], f32r)
        convh = sbuf(s, "convh", [P, 4 * 32])
        normh = sbuf(s, "normh", [P, 16])
        gtap = sbuf(s, "gtap", [P, 4, 4])
        gnorm = sbuf(s, "gnorm", [P, 2])
        xt = sbuf(s, "xt", [P, TT, GW])
        xthi = sbuf(s, "xthi", [P, LT, GW], f32r)
        xtlo = sbuf(s, "xtlo", [P, LT, GW], f32r)
        bthi = sbuf(s, "bthi", [P, TT, P], f32r)
        btlo = sbuf(s, "btlo", [P, TT, P], f32r)
        bfhi = sbuf(s, "bfhi", [P, 2, SEQ], f32r)
        bflo = sbuf(s, "bflo", [P, 2, SEQ], f32r)
        xw = sbuf(s, "xw", [P, DIRS * GW])
        xwhi = sbuf(s, "xwhi", [P, DIRS * GW], f32r)
        xwlo = sbuf(s, "xwlo", [P, DIRS * GW], f32r)
        hcur = sbuf(s, "hcur", [P, DIRS * GW])
        hdec = sbuf(s, "hdec", [P, DIRS * GW])
        Hhi = sbuf(s, "Hhi", [P, LT, DIRS, GW], f32r)
        Hlo = sbuf(s, "Hlo", [P, LT, DIRS, GW], f32r)
        Wm = sbuf(s, "Wm", [P, GH * P])
        Mf = sbuf(s, "Mf", [P, GH * P])
        Mhi = sbuf(s, "Mhi", [P, GH * P], f32r)
        Mlo = sbuf(s, "Mlo", [P, GH * P], f32r)
        xD = sbuf(s, "xD", [P, GW])
        thz = sbuf(s, "thz", [P, LT * GW])
        CTH = sbuf(s, "CTH", [P, TOK])
        yss = sbuf(s, "yss", [P, 2])
        ynm = sbuf(s, "ynm", [P, GW])
        yvv = sbuf(s, "yvv", [P, 2])
        yrs = sbuf(s, "yrs", [P, 2])
        YT = sbuf(s, "YT", [P, 2, SEQ])
    ph.close()
    ph = ExitStack()
    X2 = sbuf(ph, "X2", [P, TT, D_MODEL])
    with ExitStack() as s:
        Y1hi = sbuf(s, "Y1hi", [P, HEADS, SEQ], f32r)
        Y1lo = sbuf(s, "Y1lo", [P, HEADS, SEQ], f32r)
        Y1raw = sbuf(s, "Y1raw", [P, 2, SEQ])
        Yo1 = sbuf(s, "Yo1", [P, LT, D_MODEL])
        grow1 = sbuf(s, "grow1", [P, D_MODEL])
        junk3 = sbuf(s, "junk3", [P, 512])
        dg1 = sbuf(s, "dg1", [P, KT, P])

    s_small = sem("small_loaded")
    s_x = [sem(f"x_loaded{t}") for t in range(TT)]
    s_w = [sem(f"raw_weights_loaded{i}") for i in range(NR)]
    s_const = sem("constants_made")
    s_whi, s_wlo, s_wused = sem("weight_hi"), sem("weight_lo"), sem("weight_used")
    s_ada = sem("modulation_tile_done")
    s_c = sem("silu_c_step")
    s_mod = sem("modulation_columns")
    s_gain = sem("gain_columns")
    s_ssq, s_var, s_rstd = sem("sum_of_squares"), sem("variance"), sem("rstd")
    s_xn = sem("x_normed")
    s_xt, s_hs, s_hh, s_hl = sem("x_transposed"), sem("h_scaled"), sem("h_hi"), sem("h_lo")
    s_qc, s_ql, s_gc, s_gl = sem("q_ctx_proj"), sem("q_lat_proj"), sem("g_ctx_proj"), sem("g_lat_proj")
    s_rope = sem("rope_step")
    s_qhi, s_qlo = sem("q_hi"), sem("q_lo")
    s_nq, s_vq, s_rq = sem("qk_square_sums"), sem("qk_variance"), sem("qk_rstd")
    s_dgk, s_rkb, s_kn = sem("k_rstd_diag"), sem("k_rstd_rows"), sem("k_normed")
    s_vt, s_vhi, s_vlo = sem("v_transposed"), sem("v_hi"), sem("v_lo")
    s_sc, s_mx, s_nm, s_ex, s_es = sem("scores"), sem("score_max"), sem("neg_max"), sem("probs"), sem("sink_exp")
    s_ea, s_ri, s_pn = sem("denominator"), sem("inv_denominator"), sem("probs_normed")
    s_pt, s_pth, s_ptl = sem("probs_transposed"), sem("probs_t_hi"), sem("probs_t_lo")
    s_pv, s_y, s_yst = sem("pv_done"), sem("y_gated"), sem("y_stored")
    s_adal = sem("late_modulation_columns")
    s_yld = [sem(f"y_loaded{i}") for i in range(2)]
    s_yh, s_yl = sem("y_hi"), sem("y_lo")
    s_half, s_yo, s_sq2 = sem("out_half"), sem("out_evacuated"), sem("out_squares")
    s_gate, s_dg, s_gre = sem("gate_columns"), sem("gate_diag"), sem("gate_rows_out")
    s_res, s_out = sem("residual"), sem("out_stored")
    s_xr = sem("x_reloaded")
    s_gr4 = sem("gate_diag_used")
    s_tab, s_nsink, s_mask = sem("tables_loaded"), sem("neg_sink"), sem("band_masks")
    s_t1, s_t2 = sem("rope_cos_part"), sem("rope_sin_part")
    s_qcev, s_qlev = sem("q_ctx_evacuated"), sem("q_lat_evacuated")
    s_thc, s_thl, s_sgc, s_sgl = sem("tanh_ctx"), sem("tanh_lat"), sem("gate_ctx"), sem("gate_lat")

    NW_KV = 2 * GROUPS
    W_HEAD0 = NW_KV
    W_OUT0 = NW_KV + 2 * HEADS
    USES_ADA = ADA_EARLY // NR
    USES_HEAD0 = USES_ADA + NW_KV // NR
    USES_OUT0 = USES_HEAD0 + HEADS
    LATE_PER = 2 * GROUPS
    STORED = 32

    W_DT = W_OUT0 + 2 * KT
    W_SSM = W_DT + 1
    W_OUT1 = W_SSM + 4 + 6 * SSM_GROUPS - 4
    USES_SSM = USES_OUT0 + 2 * KT // NR
    TRI_STEPS = 11
    Q_OUT1 = W_OUT1 - W_SSM
    USES_OUT1 = USES_SSM + Q_OUT1 // 3

    BLOCKS = TT
    PAIRS = TT // 2
    SLOTS = GROUPS * BLOCKS
    LATEC = TOK

    def col(name, i=0, n=1):
        a = COLS[name][0] + i
        return cols[:, a:a + n]

    s_x1s = sem("x1_stored")
    s_dt, s_dtp, s_rows1, s_tri = sem("dt_step"), sem("dt_projected"), sem("rows_loaded"), sem("triangles")
    s_aa, s_cum = sem("a_split"), sem("running_sums")
    s_pc, s_pl = sem("tile_ctx_projected"), sem("tile_lat_projected")
    s_cmc, s_cml = sem("conv_mid_ctx"), sem("conv_mid_lat")
    s_cvc, s_cvl, s_cth, s_u = sem("conv_ctx"), sem("conv_lat"), sem("conv_tanh"), sem("conv_done")
    s_gp, s_gpa = sem("group_columns"), sem("group_a")
    s_tx, s_txe, s_txh, s_txl = sem("tokens_transposed"), sem("tokens_out"), sem("tokens_hi"), sem("tokens_lo")
    s_bfh, s_bfl = sem("bc_hi"), sem("bc_lo")
    s_tz, s_sz = sem("z_tanh"), sem("z_silu")
    s_xw, s_xwh, s_xwl = sem("x_weighted"), sem("x_weighted_hi"), sem("x_weighted_lo")
    s_st, s_hd, s_hc, s_Hh, s_Hl = (sem("state_added"), sem("state_decayed"), sem("state_new"), sem("state_hi"),
                                    sem("state_lo"))
    s_r, s_e, s_ed, s_wm, s_m, s_mh, s_ml = (sem("log_decays"), sem("decays"), sem("decays_dt"), sem("decays_summed"),
                                             sem("cb_decayed"), sem("cb_decayed_hi"), sem("cb_decayed_lo"))
    s_yd, s_y1, s_y2, s_y3, s_yy = sem("y_chunk"), sem("y_off_scaled"), sem("y_diag_d"), sem("y_off_sum"), sem("y_sum")
    s_xD, s_yg, s_yq, s_yv, s_yr, s_yn = (sem("x_d"), sem("y_gated1"), sem("y_squares"), sem("y_variance"),
                                          sem("y_rstd"), sem("y_normed"))
    s_yt, s_yte, s_y1st = sem("y_transposed"), sem("y_out"), sem("y1_stored")
    s_y1ld = [sem(f"y1_loaded{i}") for i in range(2)]
    s_dg1, s_gr1, s_gre1, s_x2 = sem("gate1_diag"), sem("gate1_rows"), sem("gate1_rows_out"), sem("x1_reloaded")
    s_zc, s_cv1, s_cv2, s_btl, s_nh = (sem("z_weight_used"), sem("conv_ctx_step"), sem("conv_lat_step"),
                                       sem("b_tokens_lo"), sem("halved_columns"))
    s_cb, s_yof = sem("cb_done"), sem("y_off_done")
    s_ny, s_gn = sem("dt_correction"), sem("group_norm_columns")
    dt_x, dt_nx, dt_e, dt_u, dt_l, dt_a = (
        x1flat[:, UEND + i * TT * 2 * SSM_HEADS:UEND + (i + 1) * TT * 2 * SSM_HEADS].rearrange(
            "p (t h) -> p t h", t=TT) for i in range(6))
    ybank = (psS[:, 0:512], psS[:, 512:1024])

    def tap(j, i):
        return gtap[:, j, i:i + 1]

    def ssm_w(q):
        return W_SSM + q

    def bcast2(ap, n):
        return ap.unsqueeze(2).broadcast_to([P, n, 2])

    block = keep.enter_context(nc.Block())

    @block.sync
    def _(sp):
        sp.dma_start(cvec[:], io["cvec"]).then_inc(s_small, 16)
        sp.dma_start(cols[:], io["cols"]).then_inc(s_small, 16)
        for t in range(NR):
            sp.dma_start(wraw[:, t], io["w_ada"][0, t]).then_inc(s_w[t], 16)
        for t in range(TT):
            sp.dma_start(X0[:, t, :], io["xc"][t]).then_inc(s_x[t], 16)
        for t in range(NR, ADA_EARLY):
            sp.wait_ge(s_ada, t - NR + 1)
            sp.dma_start(wraw[:, t % NR], io["w_ada"][0, t]).then_inc(s_w[t % NR], 16)
        sp.wait_ge(s_hl, KT)
        sp.dma_start(costab[:], io["cos"]).then_inc(s_tab, 16)
        sp.dma_start(sintab[:], io["sin"]).then_inc(s_tab, 16)
        sp.dma_start(rowt[:], io["rows"][ROWS["sink"][0]:ROWS["sink"][1]].partition_broadcast(P)).then_inc(s_tab, 16)
        for u in range(NW_KV):
            if u < NR:
                sp.wait_ge(s_ada, ADA_EARLY - NR + u + 1)
            else:
                sp.wait_ge(s_wlo, u - NR + 1)
            sp.dma_start(wraw[:, u % NR], io["w_in"][u]).then_inc(s_w[u % NR], 16)

        def head_loads(j, first):
            for c in range(2):
                sp.wait_ge(s_wlo, 5 + c if first else W_HEAD0 + 2 * (j - 1) + c + 1)
                sp.dma_start(wraw[:, c], io["w_in"][NW_KV + 2 * j + c]).then_inc(s_w[c], 16)
            for c in range(2):
                if first:
                    sp.wait_ge(s_wlo, 7 + c)
                else:
                    sp.wait_ge(s_ada, ADA_EARLY + 2 * (j - 1) + c + 1)
                sp.dma_start(wraw[:, 2 + c], io["w_ada_late"][2 * j + c]).then_inc(s_w[2 + c], 16)

        def y_store(j, par):
            sp.wait_ge(s_y, 3 * j + 3)
            sp.wait_ge(s_yst, 16 * j + STORED)
            sp.dma_start(io["y_spill"][j], Yst[:, par, :]).then_inc(s_yst, 16)

        head_loads(0, True)
        head_loads(1, False)
        with sp.Fori(0, (HEADS - 2) // 2) as i:
            for e in range(2):
                head_loads(2 * i + 2 + e, False)
                y_store(2 * i + e, e)
        for c in range(NR):
            if c < 2:
                sp.wait_ge(s_wlo, W_OUT0 - 2 + c + 1)
            else:
                sp.wait_ge(s_ada, ADA_EARLY + 2 * HEADS - 2 + c - 1)
            sp.dma_start(wraw[:, c], io["w_out0"][c]).then_inc(s_w[c], 16)
            if c == 1:
                y_store(HEADS - 2, 0)
        y_store(HEADS - 1, 1)
        sp.wait_ge(s_pv, 3 * HEADS)
        sp.wait_ge(s_y, 3 * HEADS)
        for t in range(TT):
            sp.dma_start(X1[:, t, :], io["xc"][t]).then_inc(s_xr, 16)
        for c in range(NR, 2 * KT):
            sp.wait_ge(s_wlo, W_OUT0 + c - NR + 1)
            sp.dma_start(wraw[:, c % NR], io["w_out0"][c]).then_inc(s_w[c % NR], 16)
        sp.wait_ge(s_wlo, W_OUT0 + 2 * KT)
        sp.dma_start(wraw[:, NR - 1, :, 0:2 * SSM_HEADS], io["w_dt"]).then_inc(s_w[NR - 1], 16)

        def tile_load(q, q3):
            sp.wait_ge(s_wlo, W_SSM + q - 2 if not (isinstance(q, int) and q < 3) else W_OUT0 + 2 * KT - 3 + q)
            sp.dma_start(wraw[:, q3], io["w_ssm"][q]).then_inc(s_w[q3], 16)

        tile_load(0, 0)
        tile_load(1, 1)
        sp.wait_ge(s_res, 2 * TT)
        for t in range(LT):
            sp.dma_start(io["x1_spill"][t], X1[:, CT + t, :]).then_inc(s_x1s, 16)
        tile_load(2, 2)
        sp.wait_ge(s_hl, KT + KT)
        sp.dma_start(rows1[:], io["rows"][8:NROWS].partition_broadcast(P)).then_inc(s_rows1, 16)
        tile_load(3, 0)

        def group_loads(g, last):
            for c in range(2 if last else 6):
                tile_load(6 * g + 4 + c, (4 + c) % 3)

        def y1_store(g):
            sp.wait_ge(s_yte, LT * (g + 1))
            sp.wait_ge(s_y1st, 16 * g + 16)
            sp.dma_start(io["y1_spill"][g], YT[:]).then_inc(s_y1st, 16)

        group_loads(0, False)
        with sp.Fori(0, SSM_GROUPS - 2) as g:
            group_loads(g + 1, False)
            y1_store(g)
        group_loads(SSM_GROUPS - 1, True)
        y1_store(SSM_GROUPS - 2)

        def out1_load(c):
            if c < NR - 1:
                sp.wait_ge(s_wlo, W_OUT1 - 2 + c)
            elif c == NR - 1:
                sp.wait_ge(s_wlo, W_DT + 1)
            else:
                sp.wait_ge(s_wlo, W_OUT1 + c - NR + 1)
            sp.dma_start(wraw[:, c % NR], io["w_out1"][c]).then_inc(s_w[c % NR], 16)

        for c in range(NR):
            out1_load(c)
        y1_store(SSM_GROUPS - 1)
        sp.wait_ge(s_y1st, 16 * SSM_GROUPS + 16)
        for t in range(LT):
            sp.dma_start(X2[:, t, :], io["x1_spill"][t]).then_inc(s_x2, 16)
        for c in range(NR, 2 * KT):
            out1_load(c)
        for t in range(LT):
            sp.wait_ge(s_res, 2 * TT + 2 * t + 2)
            sp.dma_start(io["out"][t], X2[:, t, :]).then_inc(s_out, 16)
        sp.wait_ge(s_out, 16 * LT)

    def window(b, banded):
        if b < CT:
            lo = hi = 0
        elif banded:
            lo, hi = max(0, b - CT - 1), min(LT, b - CT + 2)
        else:
            lo, hi = 0, LT
        return lo, hi, SEQ - (hi - lo) * P

    def due(s, light, heavy):
        for hs in range(GROUPS):
            if s == hs * BLOCKS + (heavy if hs == GROUPS - 1 else light):
                return hs
        return None

    def out_chunk_done(eng, c):
        if c % KT == KT - 1:
            eng.wait_ge(s_half, TT * (c // KT + 1))
        else:
            eng.wait_ge(s_wused, c - c // KT + 1)

    def out1_chunk_done(eng, c):
        if c % KT == KT - 1:
            eng.wait_ge(s_half, 2 * TT + LT * (c // KT + 1))
        else:
            eng.wait_ge(s_wused, 2 * (KT - 1) + c - c // KT + 1)

    def lat(u, i):
        return u if i == 3 else u[:, CTX:TOK]

    def free_hi_lo(eng, w, par, tile):
        if isinstance(w, int) and w < 2:
            return
        if isinstance(w, int) and W_DT + 2 > w >= W_OUT0 + 2:
            out_chunk_done(eng, w - 2 - W_OUT0)
        else:
            eng.wait_ge((s_ql, s_gl)[par], tile)
    @block.scalar
    def _(act):
        def weight_hi(tile, par, slot, use):
            w = 2 * tile + par
            act.wait_ge(s_w[slot], 16 * use)
            free_hi_lo(act, w, par, tile)
            A_.activation(whi[:, par], wraw[:, slot], ACT.Copy).then_inc(s_whi, 1)

        act.wait_ge(s_small, 32)
        A_.activation(cth[:], cvec[:], ACT.Tanh, scale=0.5).then_inc(s_c, 1)
        for t in range(TT):
            act.wait_ge(s_x[t], 16)
            if t:
                act.wait_ge(s_ssq, t)
            A_.activation(junk0[:], X0[:, t, :], ACT.Square, accum_out=ssq[:, 0, t:t + 1]).then_inc(s_ssq, 1)
        act.wait_ge(s_rstd, 1)
        for t in range(TT):
            A_.activation(X0[:, t, :], X0[:, t, :], ACT.Copy, scale=rstd[:, 0, t:t + 1]).then_inc(s_xn, 1)
        act.wait_ge(s_gain, 1)
        for k in range(KT):
            act.wait_ge(s_xt, k + 1)
            if k >= 2:
                act.wait_ge(s_hl, k - 1)
            ps = (psS, psT)[k % 2]
            A_.activation(HS0[:, k % 2, 0:CTX], ps[:, 0:CTX], ACT.Identity, bias=mod[:, k, 1:2],
                          scale=gain[:, 0, k, 1:2])
            A_.activation(HS0[:, k % 2, CTX:TOK], ps[:, CTX:TOK], ACT.Identity, bias=mod[:, k, 0:1],
                          scale=gain[:, 0, k, 0:1]).then_inc(s_hs, 1)

        def q_ctx(e, norm, scale):
            act.wait_ge(s_qc, e + 1)
            if not (isinstance(e, int) and e == 0):
                act.wait_ge(s_qlo, e)
            if norm:
                A_.activation(SQ[:, 0:CTX], psC[:, 0:CTX], ACT.Square)
            A_.activation(QR[:, 0:CTX], psC[:, 0:CTX], ACT.Identity, scale=scale).then_inc(s_qcev, 1)

        def q_lat(e, norm, scale):
            act.wait_ge(s_ql, e + 1)
            if norm:
                A_.activation(SQ[:, CTX:TOK], psL[0][:, :], ACT.Square)
            A_.activation(QR[:, CTX:TOK], psL[0][:, :], ACT.Identity, scale=scale).then_inc(s_qlev, 1)

        def q_hi(e, par):
            act.wait_ge(s_rope, e + 1)
            A_.activation(Qhi[:, par, :], QR[:], ACT.Copy).then_inc(s_qhi, 1)

        def gate_ctx(e):
            act.wait_ge(s_gc, e + 1)
            A_.activation(TH[:, 0:CTX], psC[:, 0:CTX], ACT.Tanh, scale=0.5).then_inc(s_thc, 1)

        def gate_lat(e):
            act.wait_ge(s_gl, e + 1)
            A_.activation(TH[:, CTX:TOK], psL[1][:, :], ACT.Tanh, scale=0.5).then_inc(s_thl, 1)

        act.wait_ge(s_hl, KT)
        for w in range(2):
            weight_hi(0, w, w, USES_ADA + 1)
        for g in range(GROUPS):
            norm = g >= 2
            scale = col("k_norm") if norm else 1.0
            q_ctx(g, norm, scale)
            q_lat(g, norm, scale)
            act.wait_ge(s_gc, g + 1)
            if g:
                act.wait_ge(s_vt, g)
            A_.activation(TH[:, 0:CTX], psC[:, 0:CTX], ACT.Copy).then_inc(s_thc, 1)
            act.wait_ge(s_gl, g + 1)
            A_.activation(TH[:, CTX:TOK], psL[1][:, :], ACT.Copy).then_inc(s_thl, 1)
            for w in (2 * g + 2, 2 * g + 3):
                weight_hi(w // 2, w % 2, w % NR, USES_ADA + w // NR + 1)
            act.wait_ge(s_vt, g + 1)
            A_.activation(Vhi[:, :, g * P:(g + 1) * P], psT[:, 0:TOK].rearrange("p (t d) -> p t d", t=TT),
                          ACT.Copy).then_inc(s_vhi, 1)
            if norm:
                act.wait_ge(s_kn, g - 1)
            else:
                act.wait_ge(s_rope, g + 1)
            A_.activation(Khi[:, g, :], QR[:], ACT.Copy).then_inc(s_qhi, 1)
        q_ctx(GROUPS, False, 1.0)
        q_lat(GROUPS, False, 1.0)
        gate_ctx(GROUPS)
        gate_lat(GROUPS)
        q_hi(GROUPS, 0)
        for c in range(2):
            weight_hi(W_HEAD0 // 2 + 1, c, c, USES_HEAD0 + 2)

        def attention(r, last):
            for s in range(SLOTS + 3):
                n = SLOTS * r + s
                if (hs := due(s, 6, 8)) is not None and not (last and hs == GROUPS - 1):
                    gate_lat(GROUPS + GROUPS * r + hs + 1)
                if s < SLOTS:
                    hs, b = s // BLOCKS, s % BLOCKS
                    banded, (lo, hi, a) = hs < 2, window(b, hs < 2)
                    act.wait_ge(s_nm, n + 1)
                    if s >= 2:
                        act.wait_ge(s_pt, n - 1)
                        act.wait_ge(s_ri, n - 1)
                    A_.activation(PR[:, s % 2, a:TOK], psS[:, a:TOK], ACT.Exp, bias=nmax[:, s % 2:s % 2 + 1],
                                  scale=SCALE if banded else rq[:, hs % 2, b:b + 1],
                                  accum_out=esum[:, s % 2:s % 2 + 1]).then_inc(s_ex, 1)
                    if banded:
                        A_.activation(esink[:, s % 2:s % 2 + 1], rowt[:, ds(2 * r + hs, 1)], ACT.Exp,
                                      bias=nmax[:, s % 2:s % 2 + 1]).then_inc(s_es, 1)
                if 1 <= s <= SLOTS:
                    pb = (s - 1) % BLOCKS
                    lo, hi, a = window(pb, (s - 1) // BLOCKS < 2)
                    act.wait_ge(s_pt, n)
                    if pb % 2 == 0 and s > 1:
                        act.wait_ge(s_pv, PAIRS * GROUPS * r + (s - 1) // 2)
                    A_.activation(PThi[:, a // P:TT, (pb % 2) * P:(pb % 2 + 1) * P],
                                  psT[:, a:TOK].rearrange("p (t q) -> p t q", q=P), ACT.Copy).then_inc(s_pth, 1)
                if (hs := due(s, 2, 2)) is not None and not (last and hs == GROUPS - 1):
                    norm = (hs + 1) % GROUPS >= 2
                    q_ctx(GROUPS + GROUPS * r + hs + 1, norm, col("q_norm") if norm else 1.0)
                if (hs := due(s, 3, 4)) is not None and not (last and hs == GROUPS - 1):
                    norm = (hs + 1) % GROUPS >= 2
                    q_lat(GROUPS + GROUPS * r + hs + 1, norm, col("q_norm") if norm else 1.0)
                if (hs := due(s, 4, 5)) is not None and not (last and hs == GROUPS - 1):
                    gate_ctx(GROUPS + GROUPS * r + hs + 1)
                    q_hi(GROUPS + GROUPS * r + hs + 1, (hs + 1) % 2)
                    weight_hi(W_HEAD0 // 2 + GROUPS * r + hs + 2, 0, 0, USES_HEAD0 + GROUPS * r + hs + 3)
                if (hs := due(s, 7, 8)) is not None and not (last and hs == GROUPS - 1):
                    weight_hi(W_HEAD0 // 2 + GROUPS * r + hs + 2, 1, 1, USES_HEAD0 + GROUPS * r + hs + 3)

        with act.Fori(0, HEADS // GROUPS - 1) as r:
            attention(r, False)
        attention(HEADS // GROUPS - 1, True)

        def y_load(k):
            if k >= 2:
                act.wait_ge(s_yl, k - 1)
            act.wait_ge(s_yst, 16 * (k + 1) + STORED)
            act.dma_start(Yraw[:, k % 2, :], io["y_spill"][k]).then_inc(s_yld[k % 2], 16)

        act.wait_ge(s_y, PAIRS * HEADS)
        act.wait_ge(s_yst, 16 * HEADS + STORED)
        y_load(0)
        y_load(1)
        for nh in range(2):
            for c in range(KT):
                w = W_OUT0 + nh * KT + c
                if w >= W_OUT0 + 2:
                    weight_hi(w // 2, w % 2, (w - W_OUT0) % NR, USES_OUT0 + (w - W_OUT0) // NR + 1)
                if nh == 0:
                    for k in (2 * c, 2 * c + 1):
                        act.wait_ge(s_yld[k % 2], 16 * (k // 2 + 1))
                        A_.activation(Yhi[:, k, :], Yraw[:, k % 2, :], ACT.Copy).then_inc(s_yh, 1)
                        if 1 <= k < HEADS - 1:
                            y_load(k + 1)
                if nh == 0 and c in (5, 7):
                    v = (c - 5) // 2
                    act.wait_ge(s_gr4, KT * (v + 1))
                    A_.activation(grow[:, v, :], psT[:, :], ACT.Copy).then_inc(s_gre, 1)
            for t in range(TT):
                act.wait_ge(s_yo, nh * TT + t + 1)
                if nh or t:
                    act.wait_ge(s_sq2, nh * TT + t)
                A_.activation(junk1[:], Yo[:, t, nh * 512:(nh + 1) * 512], ACT.Square, accum_out=ssq[:, 1 + nh, t:t + 1]).then_inc(s_sq2, 1)

        for t in range(TT):
            act.wait_ge(s_res, 2 * t + 2)
            if t:
                act.wait_ge(s_ssq, TT + t)
            A_.activation(junk2[:], X1[:, t, :], ACT.Square, accum_out=ssq[:, 0, t:t + 1]).then_inc(s_ssq, 1)
        act.wait_ge(s_rstd, 3)
        act.wait_ge(s_gain, 2)
        for t in range(TT):
            A_.activation(XN[:, t, :], X1[:, t, :], ACT.Copy, scale=rstd[:, 2, t:t + 1]).then_inc(s_xn, 1)
        for k in range(KT):
            act.wait_ge(s_xt, KT + k + 1)
            if k >= 2:
                act.wait_ge(s_hl, KT + k - 1)
            ps = (psS, psT)[k % 2]
            A_.activation(HS1[:, k % 2, 0:CTX], ps[:, 0:CTX], ACT.Identity, bias=mod[:, ADA + k, 1:2],
                          scale=gain[:, 1, k, 1:2])
            A_.activation(HS1[:, k % 2, CTX:TOK], ps[:, CTX:TOK], ACT.Identity, bias=mod[:, ADA + k, 0:1],
                          scale=gain[:, 1, k, 0:1]).then_inc(s_hs, 1)

        H2_ = 2 * SSM_HEADS

        def ssm_hi(q, q3, q2):
            act.wait_ge(s_w[q3], 16 * (USES_SSM + 1) + 16 * q)
            A_.activation(whi[:, q2], wraw[:, q3], ACT.Copy).then_inc(s_whi, 1)

        act.wait_ge(s_w[NR - 1], 16 * (USES_SSM + 1))
        out_chunk_done(act, 2 * KT - 2)
        A_.activation(whi[:, 0, :, 0:H2_], wraw[:, NR - 1, :, 0:H2_], ACT.Copy).then_inc(s_whi, 1)
        out_chunk_done(act, 2 * KT - 1)
        ssm_hi(0, 0, 1)
        act.wait_ge(s_dt, 2)
        A_.activation(dt_e, dt_nx, ACT.Exp).then_inc(s_dt, 1)
        act.wait_ge(s_dt, 4)
        A_.activation(dt_l, dt_u, ACT.Ln).then_inc(s_dt, 1)
        act.wait_ge(s_rows1, 16)
        A_.activation(rows1[:, 0:H2_], rows1[:, 0:H2_], ACT.Exp).then_inc(s_dt, 1)
        act.wait_ge(s_aa, 1)
        A_.activation(ahi[:], dt_a, ACT.Copy).then_inc(s_aa, 1)
        act.wait_ge(s_cum, 1)
        cF = psL[1][:, 0:TT * H2_].rearrange("p (t h) -> p t h", t=TT)
        cT = psS[:, 0:TT * H2_].rearrange("p (t h) -> p t h", t=TT)
        A_.activation(acu[:], cF, ACT.Copy)
        A_.activation(TAB[:, R_EA:R_EA + LT, :], cF[:, CT:TT, :], ACT.Exp)
        A_.activation(TAB[:, R_NACU:R_NACU + LT, :], cF[:, CT:TT, :], ACT.Copy, scale=-1.0)
        for i in range(STEPS):
            A_.activation(TAB[:, R_DEC + i, 0:SSM_HEADS], cT[:, FWD[i], 0:SSM_HEADS], ACT.Exp)
            last = A_.activation(TAB[:, R_DEC + i, SSM_HEADS:H2_], cT[:, BWD[i], SSM_HEADS:H2_], ACT.Exp)
        last.then_inc(s_cum, 1)
        act.wait_ge(s_cum, 3)
        A_.activation(dt_l, dt_nx, ACT.Exp).then_inc(s_cum, 1)

        def conv_ctx(g, i):
            act.wait_ge(s_pc, 3 * g + i + 1)
            A_.activation(U[i][:, 0:CTX], psC[:, 0:CTX], ACT.Identity, bias=tap(3, i),
                          scale=tap(1, i)).then_inc(s_cmc, 1)

        def conv_lat(g, i):
            act.wait_ge(s_pl, 4 * g + i + 1)
            A_.activation(lat(U[i], i), psL[i % 2][:, :], ACT.Identity, bias=tap(3, i),
                          scale=tap(1, i)).then_inc(s_cml, 1)

        def conv_tanh(g, i, first=False):
            act.wait_ge(s_cvl, 4 * g + i + 1)
            act.wait_ge(s_cvc, 3 * g + min(i, 2) + 1)
            if not first:
                act.wait_ge(s_u, 4 * g + i)
            A_.activation(CTH[:, 0:SEQ if i == 3 else TOK], U[i], ACT.Tanh).then_inc(s_cth, 1)

        act.wait_ge(s_nh, 3)
        act.wait_ge(s_dtp, 1)
        ssm_hi(0, 1, 0)
        for i in range(4):
            if i < 3:
                conv_ctx(0, i)
            conv_lat(0, i)
            if i < 2:
                ssm_hi(0 if i == 0 else 1, (2 + i) % 3, (1 + i) % 2)
            elif i == 2:
                ssm_hi(1, 1, 1)
            else:
                ssm_hi(1, 2, 0)
            conv_tanh(0, i, first=i == 0)

        def squares(g, c):
            act.wait_ge(s_yg, LT * g + c + 1)
            A_.activation(y1[:, 0:GW], yg, ACT.Square, accum_out=yss[:, 0:1]).then_inc(s_yq, 1)

        def y_norm(g, c):
            act.wait_ge(s_yr, LT * g + c + 1)
            A_.activation(ynm[:], yg, ACT.Copy, scale=yrs[:, 0:1]).then_inc(s_yn, 1)

        def y_out(g, c):
            act.wait_ge(s_yt, LT * g + c + 1)
            if c == 0:
                act.wait_ge(s_gn, g + 1)
                act.wait_ge(s_y1st, 16 * g + 16)
            for i in range(2):
                last = A_.activation(YT[:, i, c * P:(c + 1) * P], psV[:, i * P:(i + 1) * P], ACT.Copy,
                                     scale=gnorm[:, i:i + 1])
            last.then_inc(s_yte, 1)

        def decays(g, c):
            act.wait_ge(s_r, LT * g + c + 1)
            if c:
                act.wait_ge(s_wm, LT * g + c)
            for d in range(DIRS):
                for h in range(GH):
                    x = slice((d * GH + h) * P, (d * GH + h + 1) * P)
                    last = A_.activation(E[:, x], psT[:, x], ACT.Exp, bias=GP[:, R_NACU + c, d, h:h + 1])
            last.then_inc(s_e, 1)

        def ssd(g, last):
            G = g + 1
            act.wait_ge(s_u, 4 * g + 4)
            A_.activation(bfhi[:, 0, :], U[2][:, CTX:TOK], ACT.Copy)
            A_.activation(bfhi[:, 1, :], U[3], ACT.Copy).then_inc(s_bfh, 1)
            ps = psT[:, 0:TOK].rearrange("p (t d) -> p t d", t=TT)
            for i in range(3):
                act.wait_ge(s_tx, 3 * g + i + 1)
                A_.activation(xt[:, :, i * P:(i + 1) * P] if i < 2 else bthi[:], ps, ACT.Copy).then_inc(s_txe, 1)
            act.wait_ge(s_txe, 3 * g + 2)
            A_.activation(xthi[:], xt[:, CT:TT, :], ACT.Copy).then_inc(s_txh, 1)
            act.wait_ge(s_zc, 2 * g + 1)
            if not last:
                ssm_hi(2 * g + 2, 0, 1)
            act.wait_ge(s_zc, 2 * g + 2)
            A_.activation(thz[:], psS[:, :], ACT.Tanh, scale=0.5).then_inc(s_tz, 1)
            if not last:
                ssm_hi(2 * g + 2, 1, 0)
            else:
                for c in range(2):
                    act.wait_ge(s_w[c], 16 * (USES_OUT1 + 1))
                    A_.activation(whi[:, (W_OUT1 + c) % 2], wraw[:, c], ACT.Copy).then_inc(s_whi, 1)
            act.wait_ge(s_gp, g + 1)
            decays(g, 0)
            for i in range(STEPS):
                act.wait_ge(s_xw, STEPS * g + i + 1)
                if i:
                    act.wait_ge(s_st, STEPS * g + i)
                A_.activation(xwhi[:], xw[:], ACT.Copy).then_inc(s_xwh, 1)
                if i == 2 and not last:
                    act.wait_ge(s_nh, G + 3)
                    conv_ctx(G, 0)
                if i == 4 and not last:
                    conv_lat(G, 0)
                if i:
                    act.wait_ge(s_hc, STEPS * g + i + 1)
                    A_.activation(Hhi[:, i - 1, 0, :], hcur[:, 0:GW], ACT.Copy)
                    A_.activation(Hhi[:, LT - i, 1, :], hcur[:, GW:2 * GW], ACT.Copy).then_inc(s_Hh, 1)
            if not last:
                conv_ctx(G, 1)
                conv_tanh(G, 0)
                ssm_hi(2 * g + 2, 2, 1)
            for c in range(LT):
                act.wait_ge(s_m, LT * g + c + 1)
                if c:
                    act.wait_ge(s_yd, LT * g + c)
                A_.activation(Mhi[:], Mf[:], ACT.Copy).then_inc(s_mh, 1)
                if c < LT - 1:
                    decays(g, c + 1)
                if c == 1 and not last:
                    conv_lat(G, 1)
                    ssm_hi(2 * g + 3, 0, 0)
                if c == 2 and not last:
                    conv_ctx(G, 2)
                    conv_tanh(G, 1)
                if c == 3 and not last:
                    conv_lat(G, 2)
                    ssm_hi(2 * g + 3, 1, 1)
                if c:
                    y_out(g, c - 1)
                squares(g, c)
                y_norm(g, c)
            if not last:
                conv_tanh(G, 2)
                conv_lat(G, 3)
            y_out(g, LT - 1)
            if not last:
                ssm_hi(2 * g + 3, 2, 0)
                conv_tanh(G, 3)

        with act.Fori(0, SSM_GROUPS - 1) as g:
            ssd(g, False)
        ssd(SSM_GROUPS - 1, True)

        def y1_load(k):
            if k >= 2:
                act.wait_ge(s_yl, HEADS + k - 1)
            act.wait_ge(s_y1st, 16 * (k // 2 + 1) + 16)
            act.dma_start(Y1raw[:, k % 2, :], io["y1_spill"][k // 2, :, k % 2, :]).then_inc(s_y1ld[k % 2], 16)

        act.wait_ge(s_y1st, 16 * SSM_GROUPS + 16)
        y1_load(0)
        y1_load(1)
        for nh in range(2):
            for c in range(KT):
                i = nh * KT + c
                if i >= 2:
                    act.wait_ge(s_w[i % NR], 16 * ((USES_OUT1 if i % NR < 3 else USES_SSM + 1) + i // NR + 1))
                    out1_chunk_done(act, i - 2)
                    A_.activation(whi[:, (W_OUT1 + i) % 2], wraw[:, i % NR], ACT.Copy).then_inc(s_whi, 1)
                if nh == 0:
                    for k in (2 * c, 2 * c + 1):
                        act.wait_ge(s_y1ld[k % 2], 16 * (k // 2 + 1))
                        A_.activation(Y1hi[:, k, :], Y1raw[:, k % 2, :], ACT.Copy).then_inc(s_yh, 1)
                        if 1 <= k < HEADS - 1:
                            y1_load(k + 1)
                if nh == 0 and c == 5:
                    act.wait_ge(s_gr1, KT)
                    A_.activation(grow1[:], psT[:, :], ACT.Copy).then_inc(s_gre1, 1)
            for t in range(LT):
                act.wait_ge(s_yo, 2 * TT + nh * LT + t + 1)
                if nh or t:
                    act.wait_ge(s_sq2, 2 * TT + nh * LT + t)
                A_.activation(junk3[:], Yo1[:, t, nh * 512:(nh + 1) * 512], ACT.Square,
                              accum_out=ssq[:, 1 + nh, t:t + 1]).then_inc(s_sq2, 1)

    @block.vector
    def _(dve):
        dve.wait_ge(s_c, 1)
        V_.scalar_tensor_tensor(csilu[:], cth[:], 1.0, cvec[:], ALU.add, ALU.mult).then_inc(s_c, 1)
        dve.wait_ge(s_c, 2)
        V_.tensor_scalar(csilu[:], csilu[:], 0.5, None, ALU.mult).then_inc(s_c, 1)
        dve.wait_ge(s_ssq, TT)
        V_.tensor_scalar(vvar[:, 0, 0:TT], ssq[:, 0, 0:TT], 1.0 / D_MODEL, EPS, ALU.mult, ALU.add).then_inc(s_var, 1)
        dve.wait_ge(s_ada, ADA_EARLY)
        V_.tensor_tensor(mod[:, 0:ADA_EARLY, :], psV[:, 0:2 * ADA_EARLY].rearrange("p (t v) -> p t v", v=2),
                         bcast2(col("b_ada", 0, ADA_EARLY), ADA_EARLY), ALU.add).then_inc(s_mod, 1)
        dve.wait_ge(s_mod, 1)
        V_.scalar_tensor_tensor(gain[:, 0], mod[:, KT:2 * KT, :], 1.0, bcast2(col("pre", 0, KT), KT),
                                ALU.add, ALU.mult).then_inc(s_gain, 1)
        for k in range(KT):
            dve.wait_ge(s_hs, k + 1)
            V_.tensor_copy(hhi[:, k, :], HS0[:, k % 2, :]).then_inc(s_hh, 1)
            dve.wait_ge(s_hh, k + 1)
            V_.tensor_tensor(hlo[:, k, :], HS0[:, k % 2, :], f(hhi[:, k, :]), ALU.subtract).then_inc(s_hl, 1)

        H2 = P // 2

        def rope(e):
            dve.wait_ge(s_qlev, e + 1)
            x = QR[:, CTX:TOK]
            V_.tensor_tensor(T1[:], x, costab[:], ALU.mult).then_inc(s_t1, 1)
            V_.tensor_tensor(T2[0:H2, :], x[H2:P, :], sintab[H2:P, :], ALU.mult)
            V_.tensor_tensor(T2[H2:P, :], x[0:H2, :], sintab[0:H2, :], ALU.mult).then_inc(s_t2, 1)
            dve.wait_ge(s_t1, e + 1)
            dve.wait_ge(s_t2, e + 1)
            V_.tensor_tensor(x, T1[:], T2[:], ALU.add).then_inc(s_rope, 1)

        def variance(u, factor=1.0):
            dve.wait_ge(s_nq, u + 1)
            V_.tensor_scalar(vq[:], psV[:, 0:TT], factor / P, factor * EPS, ALU.mult,
                             ALU.add).then_inc(s_vq, 1)

        def gate(e, par, part):
            if part == 0:
                dve.wait_ge(s_thc, e + 1)
                V_.scalar_tensor_tensor(SG[:, par, 0:CTX], TH[:, 0:CTX], 1.0, psC[:, 0:CTX], ALU.add,
                                        ALU.mult).then_inc(s_sgc, 1)
            else:
                dve.wait_ge(s_thl, e + 1)
                V_.scalar_tensor_tensor(SG[:, par, CTX:TOK], TH[:, CTX:TOK], 1.0, psL[1][:, :], ALU.add,
                                        ALU.mult).then_inc(s_sgl, 1)

        dve.wait_ge(s_tab, 48)
        V_.tensor_scalar(nsink[:], rowt[:], -1.0, None, ALU.mult).then_inc(s_nsink, 1)
        for g in range(GROUPS):
            vals = slice(g * P, (g + 1) * P)
            rope(g)
            if g >= 2:
                variance(g - 2)
                dve.wait_ge(s_rq, g - 1)
                for t in range(TT):
                    last = V_.tensor_scalar(dgk[:, t, :], ident[:], rq[:, g % 2, t:t + 1], None, ALU.mult)
                last.then_inc(s_dgk, 1)
            dve.wait_ge(s_vhi, g + 1)
            V_.tensor_tensor(Vlo[:, :, vals], psT[:, 0:TOK].rearrange("p (t d) -> p t d", t=TT),
                             f(Vhi[:, :, vals]), ALU.subtract).then_inc(s_vlo, 1)
            if g >= 2:
                dve.wait_ge(s_rkb, g - 1)
                dve.wait_ge(s_rope, g + 1)
                V_.tensor_tensor(QR[:], QR[:], psT[:, 0:TOK], ALU.mult).then_inc(s_kn, 1)
            dve.wait_ge(s_qhi, g + 1)
            V_.tensor_tensor(Klo[:, g, :], QR[:], f(Khi[:, g, :]), ALU.subtract).then_inc(s_qlo, 1)
        rope(GROUPS)
        gate(GROUPS, 0, 0)
        gate(GROUPS, 0, 1)

        def attention(r, last):
            for s in range(SLOTS + 3):
                n = SLOTS * r + s
                skip = lambda hs: hs is None or (last and hs == GROUPS - 1)
                tile = lambda hs: GROUPS + GROUPS * r + hs + 1
                if not skip(hs := due(s, 5, 6)):
                    gate(tile(hs), (hs + 1) % 2, 0)
                if not skip(hs := due(s, 6, 8)):
                    gate(tile(hs), (hs + 1) % 2, 1)
                if s < SLOTS:
                    hs, b = s // BLOCKS, s % BLOCKS
                    banded, (lo, hi, a) = hs < 2, window(b, hs < 2)
                    p = slice(s % 2, s % 2 + 1)
                    dve.wait_ge(s_sc, n + 1)
                    V_.reduce_max(smax[:, p], psS[:, a:TOK], AX.X).then_inc(s_mx, 1)
                    dve.wait_ge(s_mx, n + 1)
                    if banded:
                        V_.tensor_scalar(nmax[:, p], smax[:, p], -SCALE, nsink[:, ds(2 * r + hs, 1)], ALU.mult,
                                         ALU.min).then_inc(s_nm, 1)
                    else:
                        if b == 0:
                            dve.wait_ge(s_rq, 2 * r + hs + 1)
                        V_.tensor_scalar(nmax[:, p], smax[:, p], rq[:, hs % 2, b:b + 1], -1.0, ALU.mult,
                                         ALU.mult).then_inc(s_nm, 1)
                if s < SLOTS:
                    hs, b = s // BLOCKS, s % BLOCKS
                    if hs < 2:
                        dve.wait_ge(s_es, 2 * BLOCKS * r + s + 1)
                        dve.wait_ge(s_ex, n + 1)
                        V_.tensor_tensor(eall[:, p], esum[:, p], esink[:, p], ALU.add).then_inc(s_ea, 1)
                        dve.wait_ge(s_ea, 2 * BLOCKS * r + s + 1)
                        V_.reciprocal(rinv[:, p], eall[:, p]).then_inc(s_ri, 1)
                    else:
                        dve.wait_ge(s_ex, n + 1)
                        V_.reciprocal(rinv[:, p], esum[:, p]).then_inc(s_ri, 1)
                    dve.wait_ge(s_ri, n + 1)
                    V_.tensor_scalar(PR[:, s % 2, a:TOK], PR[:, s % 2, a:TOK], rinv[:, p], 0.5, ALU.mult,
                                     ALU.mult).then_inc(s_pn, 1)
                if not skip(hs := due(s, 4, 5)):
                    rope(tile(hs))
                if 1 <= s <= SLOTS:
                    pb = (s - 1) % BLOCKS
                    lo, hi, a = window(pb, (s - 1) // BLOCKS < 2)
                    q = slice((pb % 2) * P, (pb % 2 + 1) * P)
                    dve.wait_ge(s_pth, n)
                    V_.tensor_tensor(PTlo[:, a // P:TT, q], psT[:, a:TOK].rearrange("p (t q) -> p t q", q=P),
                                     f(PThi[:, a // P:TT, q]), ALU.subtract).then_inc(s_ptl, 1)
                if s >= 3 and s % 2:
                    pair = (s - 3) // 2
                    hs, q = pair // PAIRS, pair % PAIRS
                    dve.wait_ge(s_pv, PAIRS * GROUPS * r + pair + 1)
                    if q == 0:
                        dve.wait_ge(s_yst, 16 * (GROUPS * r + hs + 1))
                    V_.tensor_tensor(Yst[:, hs % 2, q * 2 * P:(q + 1) * 2 * P], psV[:, 0:2 * P],
                                     SG[:, hs % 2, q * 2 * P:(q + 1) * 2 * P], ALU.mult).then_inc(s_y, 1)
                if not skip(hs := due(s, 4, 5)) and (hs + 1) % GROUPS >= 2:
                    variance(2 * r + hs + 1, P)
                if s == SLOTS + 1:
                    dve.wait_ge(s_ada, ADA_EARLY + LATE_PER * (r + 1))
                    V_.tensor_tensor(mod[:, ds(LATE_PER * r + ADA_EARLY, LATE_PER), :],
                                     psT[:, LATEC:LATEC + 2 * LATE_PER].rearrange("p (t v) -> p t v", v=2),
                                     bcast2(cols[:, ds(LATE_PER * r + ADA_EARLY + COLS["b_ada"][0], LATE_PER)], LATE_PER),
                                     ALU.add).then_inc(s_adal, 1)

        with dve.Fori(0, HEADS // GROUPS - 1) as r:
            attention(r, False)
        attention(HEADS // GROUPS - 1, True)

        def gate_columns(layer):
            V_.tensor_tensor(gcolx[:, layer], mod[:, layer * ADA + 2 * KT:layer * ADA + 3 * KT, :],
                             bcast2(col("post", layer * KT, KT), KT), ALU.mult).then_inc(s_gate, 1)

        def gate_diag(layer, v, first):
            for k in range(KT):
                u = first + v * KT + k
                if u >= KT:
                    dve.wait_ge(s_gr4, u - KT + 1)
                V_.tensor_scalar(dg[:, k, :], ident[:], gcolx[:, layer, k, v:v + 1], None,
                                 ALU.mult).then_inc(s_dg, 1)

        dve.wait_ge(s_adal, HEADS // GROUPS)
        gate_columns(0)
        dve.wait_ge(s_gate, 1)
        for k in range(HEADS):
            dve.wait_ge(s_yh, k + 1)
            V_.tensor_tensor(Ylo[:, k, :], Yraw[:, k % 2, :], f(Yhi[:, k, :]), ALU.subtract).then_inc(s_yl, 1)
            if k in (7, 11):
                gate_diag(0, (k - 7) // 4, 0)
        for nh in range(2):
            for t in range(TT):
                dve.wait_ge(s_half, nh * TT + t + 1)
                V_.tensor_copy(Yo[:, t, nh * 512:(nh + 1) * 512], tok_bank[t]).then_inc(s_yo, 1)
        dve.wait_ge(s_sq2, 2 * TT)
        V_.tensor_tensor(ssq[:, 3, 0:TT], ssq[:, 1, 0:TT], ssq[:, 2, 0:TT], ALU.add).then_inc(s_var, 1)
        dve.wait_ge(s_var, 2)
        V_.tensor_scalar(vvar[:, 1, 0:TT], ssq[:, 3, 0:TT], 1.0 / D_MODEL, EPS, ALU.mult, ALU.add).then_inc(s_var, 1)
        dve.wait_ge(s_rstd, 2)
        dve.wait_ge(s_gre, 2)
        dve.wait_ge(s_yo, 2 * TT)
        for t in range(TT):
            V_.scalar_tensor_tensor(Yo[:, t, :], Yo[:, t, :], rstd[:, 1, t:t + 1], grow[:, int(t < CT), :],
                                    ALU.mult, ALU.mult).then_inc(s_res, 1)
            if t == 0:
                dve.wait_ge(s_xr, 16 * TT)
            dve.wait_ge(s_res, 2 * t + 1)
            V_.tensor_tensor(X1[:, t, :], X1[:, t, :], Yo[:, t, :], ALU.add).then_inc(s_res, 1)

        dve.wait_ge(s_ssq, TT + TT)
        V_.tensor_scalar(vvar[:, 2, 0:TT], ssq[:, 0, 0:TT], 1.0 / D_MODEL, EPS, ALU.mult, ALU.add).then_inc(s_var, 1)
        V_.scalar_tensor_tensor(gain[:, 1], mod[:, ADA + KT:ADA + 2 * KT, :], 1.0, bcast2(col("pre", KT, KT), KT),
                                ALU.add, ALU.mult).then_inc(s_gain, 1)
        gate_columns(1)
        for k in range(KT):
            dve.wait_ge(s_hs, KT + k + 1)
            V_.tensor_copy(h1hi[:, k, :], HS1[:, k % 2, :]).then_inc(s_hh, 1)
            dve.wait_ge(s_hh, KT + k + 1)
            V_.tensor_tensor(h1lo[:, k, :], HS1[:, k % 2, :], f(h1hi[:, k, :]), ALU.subtract).then_inc(s_hl, 1)
        dve.wait_ge(s_hl, KT + KT)
        V_.tensor_scalar(convh[:], cols[:, COLS["conv_w"][0]:COLS["conv_b"][1]], 0.5, None, ALU.mult).then_inc(s_nh, 1)
        V_.tensor_scalar(normh[:], col("ssm_norm", 0, 16), 0.5, None, ALU.mult).then_inc(s_nh, 1)
        H2_ = 2 * SSM_HEADS

        def rows_b(ap):
            return ap.unsqueeze(1).broadcast_to([P, TT, H2_])

        dve.wait_ge(s_rows1, 16)
        dve.wait_ge(s_x1s, 16 * LT)
        dve.wait_ge(s_dtp, 1)
        V_.tensor_tensor(dt_x, psL[0][:, 0:TT * H2_].rearrange("p (t h) -> p t h", t=TT), rows_b(rows1[:, H2_:2 * H2_]),
                         ALU.add).then_inc(s_dt, 1)
        dve.wait_ge(s_dt, 1)
        V_.scalar_tensor_tensor(dt_nx, dt_x, -1.0, dt_x, ALU.mult, ALU.min).then_inc(s_dt, 1)
        dve.wait_ge(s_dt, 3)
        V_.tensor_scalar(dt_u, dt_e, 1.0, None, ALU.add).then_inc(s_dt, 1)
        dve.wait_ge(s_dt, 5)
        V_.scalar_tensor_tensor(dt_e, dt_u, -1.0, dt_e, ALU.add, ALU.subtract).then_inc(s_ny, 1)
        V_.reciprocal(dt_nx, dt_u).then_inc(s_ny, 1)
        dve.wait_ge(s_ny, 2)
        V_.tensor_tensor(dt_e, dt_e, dt_nx, ALU.mult).then_inc(s_ny, 1)
        dve.wait_ge(s_ny, 3)
        V_.tensor_tensor(dt_l, dt_l, dt_e, ALU.subtract).then_inc(s_ny, 1)
        dve.wait_ge(s_ny, 4)
        V_.scalar_tensor_tensor(dt_x, dt_x, 0.0, dt_l, ALU.max, ALU.add).then_inc(s_ny, 1)
        dve.wait_ge(s_ny, 5)
        dve.wait_ge(s_dt, 6)
        V_.tensor_copy(TAB[:, R_DT:R_DT + LT, :], dt_x[:, CT:TT, :])
        V_.tensor_copy(TAB[:, R_D, 0:SSM_HEADS], rows1[:, 2 * H2_:2 * H2_ + SSM_HEADS])
        V_.memset(TAB[:, R_D, SSM_HEADS:H2_], 0.0)
        V_.scalar_tensor_tensor(dt_a, dt_x, -1.0, rows_b(rows1[:, 0:H2_]), ALU.mult, ALU.mult).then_inc(s_aa, 1)
        dve.wait_ge(s_aa, 2)
        V_.tensor_tensor(alo[:], dt_a, f(ahi[:]), ALU.subtract).then_inc(s_aa, 1)
        dve.wait_ge(s_cum, 2)
        V_.tensor_tensor(dt_nx, psS[:, 0:TT * H2_].rearrange("p (t h) -> p t h", t=TT), acu[:],
                         ALU.subtract).then_inc(s_cum, 1)
        dve.wait_ge(s_cum, 4)
        for i in range(STEPS):
            V_.tensor_tensor(TAB[:, R_WE + i, 0:SSM_HEADS], dt_l[:, FWD[i], 0:SSM_HEADS], dt_x[:, FWD[i], 0:SSM_HEADS],
                             ALU.mult)
            last = V_.tensor_tensor(TAB[:, R_WE + i, SSM_HEADS:H2_], dt_l[:, BWD[i], SSM_HEADS:H2_],
                                    dt_x[:, BWD[i], SSM_HEADS:H2_], ALU.mult)
        last.then_inc(s_cum, 1)

        def outer_taps(g, i, u, ps, n, mid, step, done, k):
            dve.wait_ge(mid, k + 1)
            V_.scalar_tensor_tensor(u[:, 1:n], ps[:, 0:n - 1], tap(0, i), u[:, 1:n], ALU.mult, ALU.add).then_inc(step, 1)
            dve.wait_ge(step, k + 1)
            V_.scalar_tensor_tensor(u[:, 0:n - 1], ps[:, 1:n], tap(2, i), u[:, 0:n - 1], ALU.mult,
                                    ALU.add).then_inc(done, 1)

        def taps_ctx(g, i):
            outer_taps(g, i, U[i], psC, CTX, s_cmc, s_cv1, s_cvc, 3 * g + i)

        def taps_lat(g, i):
            outer_taps(g, i, lat(U[i], i), psL[i % 2], SEQ, s_cml, s_cv2, s_cvl, 4 * g + i)

        def silu(g, i):
            dve.wait_ge(s_cth, 4 * g + i + 1)
            V_.scalar_tensor_tensor(U[i], CTH[:, 0:SEQ if i == 3 else TOK], 1.0, U[i], ALU.add, ALU.mult).then_inc(s_u, 1)

        def group_taps(g):
            at = convh[:].rearrange("p (j b g) -> p j b g", j=4, b=4)
            V_.tensor_copy(gtap[:, :, 0:2], convh[:].rearrange("p (j b) -> p j b", j=4)[:, :, ds(2 * g, 2)])
            V_.tensor_copy(gtap[:, :, 2:4], at[:, :, 2:4, ds(g, 1)].rearrange("p j b g -> p j (b g)")).then_inc(s_nh, 1)

        dve.wait_ge(s_nh, 2)
        group_taps(0)
        for i in range(4):
            if i < 3:
                taps_ctx(0, i)
            taps_lat(0, i)
            silu(0, i)

        def variance1(g, c):
            dve.wait_ge(s_yq, LT * g + c + 1)
            V_.tensor_scalar(yvv[:, 0:1], yss[:, 0:1], 0.25 / GW, EPS, ALU.mult, ALU.add).then_inc(s_yv, 1)

        def by_head(ap, n):
            return ap.rearrange("p (h x) -> p h x", x=n)

        def per_head(ap, d0, d1, n):
            return ap.rearrange("p d h -> p (d h)")[:, d0 * GH:d1 * GH].unsqueeze(2).broadcast_to([P, (d1 - d0) * GH, n])

        dve.wait_ge(s_cum, 5)

        def ssd(g, last):
            G = g + 1
            if not last:
                group_taps(G)
            V_.tensor_copy(GP[:], TAB[:].rearrange("p r (d h) -> p r d h", d=DIRS)[:, :, :, ds(GH * g, GH)]).then_inc(s_gp, 1)
            V_.tensor_copy(aghi[:], f(ahi[:]).rearrange("p t (d h) -> p t d h", d=DIRS)[:, CT:TT, :, ds(GH * g, GH)])
            V_.tensor_copy(aglo[:], f(alo[:]).rearrange("p t (d h) -> p t d h", d=DIRS)[:, CT:TT, :, ds(GH * g, GH)]).then_inc(s_gpa, 1)
            dve.wait_ge(s_bfh, g + 1)
            V_.tensor_tensor(bflo[:, 0, :], U[2][:, CTX:TOK], f(bfhi[:, 0, :]), ALU.subtract)
            V_.tensor_tensor(bflo[:, 1, :], U[3], f(bfhi[:, 1, :]), ALU.subtract).then_inc(s_bfl, 1)
            dve.wait_ge(s_txe, 3 * g + 3)
            V_.tensor_tensor(btlo[:], psT[:, 0:TOK].rearrange("p (t d) -> p t d", t=TT), f(bthi[:]), ALU.subtract).then_inc(s_btl, 1)
            dve.wait_ge(s_txh, g + 1)
            V_.tensor_tensor(xtlo[:], xt[:, CT:TT, :], f(xthi[:]), ALU.subtract).then_inc(s_txl, 1)
            dve.wait_ge(s_tz, g + 1)
            V_.scalar_tensor_tensor(sz, thz[:], 1.0, psS[:, :], ALU.add, ALU.mult).then_inc(s_sz, 1)
            dve.wait_ge(s_gp, g + 1)
            for i in range(STEPS):
                if i == STEPS - 1:
                    dve.wait_ge(s_y1st, 16 * g + 16)
                dve.wait_ge(s_xwh, STEPS * g + i + 1)
                V_.tensor_tensor(xwlo[:], xw[:], f(xwhi[:]), ALU.subtract).then_inc(s_xwl, 1)
                if i == STEPS - 1:
                    V_.tensor_copy(gnorm[:], normh[:, ds(2 * g, 2)]).then_inc(s_gn, 1)
                if i == 3 and not last:
                    taps_ctx(G, 0)
                if i:
                    dve.wait_ge(s_hc, STEPS * g + i)
                    V_.tensor_tensor(by_head(hdec[:], HD), by_head(hcur[:], HD), per_head(GP[:, R_DEC + i], 0, DIRS, HD),
                                     ALU.mult).then_inc(s_hd, 1)
                    dve.wait_ge(s_hd, (STEPS - 1) * g + i)
                dve.wait_ge(s_st, STEPS * g + i + 1)
                if i == 0:
                    V_.tensor_copy(hcur[:], ybank[0]).then_inc(s_hc, 1)
                else:
                    if i > 1:
                        dve.wait_ge(s_Hl, LT * g + i - 1)
                    V_.tensor_tensor(hcur[:], hdec[:], ybank[0], ALU.add).then_inc(s_hc, 1)
            if not last:
                taps_lat(G, 0)
                taps_ctx(G, 1)
            for c in range(LT):
                n = LT * g + c
                dve.wait_ge(s_ed, n + 1)
                V_.tensor_tensor(Wm[:], E[:, 0:GH * P], E[:, GH * P:2 * GH * P], ALU.add).then_inc(s_wm, 1)
                dve.wait_ge(s_wm, n + 1)
                dve.wait_ge(s_cb, n + 1)
                V_.tensor_tensor(by_head(Mf[:], P), by_head(Wm[:], P),
                                 ybank[1][:, 0:P].unsqueeze(1).broadcast_to([P, GH, P]), ALU.mult).then_inc(s_m, 1)
                dve.wait_ge(s_mh, n + 1)
                V_.tensor_tensor(Mlo[:], Mf[:], f(Mhi[:]), ALU.subtract).then_inc(s_ml, 1)
                if c == 0 and not last:
                    silu(G, 0)
                if c == 2 and not last:
                    taps_lat(G, 1)
                    silu(G, 1)
                    taps_ctx(G, 2)
                dve.wait_ge(s_xD, n + 1)
                dve.wait_ge(s_yd, n + 1)
                V_.tensor_tensor(y2, ybank[1][:, P:P + GW], xD[:], ALU.add).then_inc(s_y2, 1)
                dve.wait_ge(s_yof, n + 1)
                V_.tensor_tensor(by_head(y1, HD), by_head(ybank[0], HD), per_head(GP[:, R_EA + c], 0, DIRS, HD),
                                 ALU.mult).then_inc(s_y1, 1)
                dve.wait_ge(s_y1, n + 1)
                V_.tensor_tensor(y3, y1[:, 0:GW], y1[:, GW:2 * GW], ALU.add).then_inc(s_y3, 1)
                dve.wait_ge(s_y3, n + 1)
                V_.tensor_tensor(y2, y2, y3, ALU.add).then_inc(s_yy, 1)
                dve.wait_ge(s_yy, n + 1)
                V_.tensor_tensor(yg, y2, sz[:, c * GW:(c + 1) * GW], ALU.mult).then_inc(s_yg, 1)
                variance1(g, c)
            if not last:
                taps_lat(G, 2)
                silu(G, 2)
                taps_lat(G, 3)
                silu(G, 3)

        with dve.Fori(0, SSM_GROUPS - 1) as g:
            ssd(g, False)
        ssd(SSM_GROUPS - 1, True)

        for k in range(HEADS):
            dve.wait_ge(s_yh, HEADS + k + 1)
            V_.tensor_tensor(Y1lo[:, k, :], Y1raw[:, k % 2, :], f(Y1hi[:, k, :]), ALU.subtract).then_inc(s_yl, 1)
            if k == 7:
                for j in range(KT):
                    V_.tensor_scalar(dg1[:, j, :], ident[:], gcolx[:, 1, j, 0:1], None, ALU.mult).then_inc(s_dg1, 1)
        for nh in range(2):
            for t in range(LT):
                dve.wait_ge(s_half, 2 * TT + nh * LT + t + 1)
                V_.tensor_copy(Yo1[:, t, nh * 512:(nh + 1) * 512], tok_bank[t]).then_inc(s_yo, 1)
        dve.wait_ge(s_sq2, 2 * TT + 2 * LT)
        V_.tensor_tensor(ssq[:, 3, 0:LT], ssq[:, 1, 0:LT], ssq[:, 2, 0:LT], ALU.add).then_inc(s_var, 1)
        dve.wait_ge(s_var, 5)
        V_.tensor_scalar(vvar[:, 3, 0:LT], ssq[:, 3, 0:LT], 1.0 / D_MODEL, EPS, ALU.mult, ALU.add).then_inc(s_var, 1)
        dve.wait_ge(s_rstd, 4)
        dve.wait_ge(s_gre1, 1)
        dve.wait_ge(s_yo, 2 * TT + 2 * LT)
        dve.wait_ge(s_x2, 16 * LT)
        for t in range(LT):
            V_.scalar_tensor_tensor(Yo1[:, t, :], Yo1[:, t, :], rstd[:, 3, t:t + 1], grow1[:], ALU.mult,
                                    ALU.mult).then_inc(s_res, 1)
            dve.wait_ge(s_res, 2 * TT + 2 * t + 1)
            V_.tensor_tensor(X2[:, t, :], X2[:, t, :], Yo1[:, t, :], ALU.add).then_inc(s_res, 1)

    @block.gpsimd
    def _(pool):
        G_.memset(half[:], -0.5).then_inc(s_yst, STORED)
        G_.memset(ones[:], 1.0).then_inc(s_const, 1)
        G_.memset(ident[:], 0.0).then_inc(s_const, 1)
        G_.memset(nothing[:], 0.0).then_inc(s_y1st, 16)
        pool.wait_ge(s_const, 2)
        G_.affine_select(out=ident[:], in_=ident[:], compare_op=ALU.not_equal, fill=1.0, base=0,
                         pattern=[[-1, P]], channel_multiplier=1).then_inc(s_const, 1)
        pool.wait_ge(s_const, 3)
        G_.tensor_copy(identr[:], ident[:]).then_inc(s_const, 1)

        def inv_sqrt(dst, src, n, done):
            G_.tensor_tensor(dst, src, half[:, 0:n], ALU.pow).then_inc(done, 1)

        def weight_lo(w, par, slot):
            pool.wait_ge(s_whi, w + 1)
            G_.tensor_tensor(wlo[:, par], wraw[:, slot], f(whi[:, par]), ALU.subtract).then_inc(s_wlo, 1)

        pool.wait_ge(s_yst, STORED)
        pool.wait_ge(s_var, 1)
        inv_sqrt(rstd[:, 0, 0:TT], vvar[:, 0, 0:TT], TT, s_rstd)
        pool.wait_ge(s_hl, KT)
        for m in range(2):
            sign = 1 - 2 * m
            G_.memset(T2[:, m * P:(m + 1) * P], 0.0).then_inc(s_mask, 1)
            pool.wait_ge(s_mask, 3 * m + 1)
            G_.affine_select(out=T2[:, m * P:(m + 1) * P], in_=T2[:, m * P:(m + 1) * P], compare_op=ALU.is_ge,
                             fill=MASKED, base=0, pattern=[[sign, P]], channel_multiplier=-sign).then_inc(s_mask, 1)
            pool.wait_ge(s_mask, 3 * m + 2)
            G_.tensor_copy(maskr[:, m, :], T2[:, m * P:(m + 1) * P]).then_inc(s_mask, 1)
        weight_lo(0, 0, 0)
        weight_lo(1, 1, 1)

        def qk_rstd(u, par):
            pool.wait_ge(s_vq, u + 1)
            inv_sqrt(rq[:, par, :], vq[:], TT, s_rq)

        def q_lo(e, par):
            pool.wait_ge(s_qhi, e + 1)
            G_.tensor_tensor(Qlo[:, par, :], QR[:], f(Qhi[:, par, :]), ALU.subtract).then_inc(s_qlo, 1)

        for g in range(GROUPS):
            weight_lo(2 * g + 2, 0, (2 * g + 2) % NR)
            weight_lo(2 * g + 3, 1, (2 * g + 3) % NR)
            if g >= 2:
                qk_rstd(g - 2, g % 2)
        q_lo(GROUPS, 0)
        for c in range(2):
            weight_lo(W_HEAD0 + 2 + c, c, c)

        def attention(r, last):
            for s in range(SLOTS + 3):
                n = SLOTS * r + s
                skip = lambda hs: hs is None or (last and hs == GROUPS - 1)
                if not skip(hs := due(s, 4, 5)):
                    q_lo(GROUPS + GROUPS * r + hs + 1, (hs + 1) % 2)
                if not skip(hs := due(s, 5, 6)) and (hs + 1) % GROUPS >= 2:
                    qk_rstd(2 * r + hs + 1, (hs + 1) % 2)
                if not skip(hs := due(s, 4, 5)):
                    weight_lo(W_HEAD0 + 2 * (GROUPS * r + hs + 2), 0, 0)
                if not skip(hs := due(s, 7, 8)):
                    weight_lo(W_HEAD0 + 2 * (GROUPS * r + hs + 2) + 1, 1, 1)

        with pool.Fori(0, HEADS // GROUPS - 1) as r:
            attention(r, False)
        attention(HEADS // GROUPS - 1, True)
        for w in range(W_OUT0 + 2, W_OUT0 + 2 * KT):
            weight_lo(w, w % 2, (w - W_OUT0) % NR)
        pool.wait_ge(s_var, 3)
        inv_sqrt(rstd[:, 1, 0:TT], vvar[:, 1, 0:TT], TT, s_rstd)

        pool.wait_ge(s_var, 4)
        inv_sqrt(rstd[:, 2, 0:TT], vvar[:, 2, 0:TT], TT, s_rstd)
        H2_ = 2 * SSM_HEADS
        pool.wait_ge(s_whi, W_DT + 1)
        G_.tensor_tensor(wlo[:, 0, :, 0:H2_], wraw[:, NR - 1, :, 0:H2_], f(whi[:, 0, :, 0:H2_]),
                         ALU.subtract).then_inc(s_wlo, 1)
        weight_lo(W_SSM, 1, 0)
        pool.wait_ge(s_hl, KT + KT)
        G_.tensor_copy(onesr[:], ones[:]).then_inc(s_tri, 1)
        tri = xt[:, 0, 0:P]
        n = 1
        for d in range(DIRS):
            sign = 1 - 2 * d
            for base, fill, dst in ((ones[:], 0.0, trir[:, d, :]), (None, MASKED, negr[:, d, :])):
                if base is None:
                    pool.wait_ge(s_tri, n)
                    G_.memset(tri, 0.0).then_inc(s_tri, 1)
                    n += 1
                    base = tri
                pool.wait_ge(s_tri, n)
                G_.affine_select(out=tri, in_=base, compare_op=ALU.is_ge, fill=fill, base=0, pattern=[[sign, P]],
                                 channel_multiplier=-sign).then_inc(s_tri, 1)
                pool.wait_ge(s_tri, n + 1)
                G_.tensor_copy(dst, tri).then_inc(s_tri, 1)
                n += 2
        for q in range(1, 6):
            weight_lo(W_SSM + q, (W_SSM + q) % 2, q % 3)

        def by_head(ap, n):
            return ap.rearrange("p (h x) -> p h x", x=n)

        def per_head(ap, n):
            return ap.unsqueeze(2).broadcast_to([P, ap.shape[1], n])

        def ssd(g, last):
            w = W_SSM + 6 + 6 * g
            G = g + 1
            pool.wait_ge(s_gp, g + 1)
            pool.wait_ge(s_txe, 3 * g + 2)
            for i in range(STEPS):
                if i:
                    pool.wait_ge(s_xwl, STEPS * g + i)
                for d, u in ((0, FWD[i]), (1, BWD[i])):
                    done = G_.tensor_tensor(by_head(xw[:, d * GW:(d + 1) * GW], HD), by_head(xt[:, u, :], HD),
                                            per_head(GP[:, R_WE + i, d, :], HD), ALU.mult)
                done.then_inc(s_xw, 1)
                if i == 0:
                    decays_dt(g, 0)
                    if not last:
                        weight_lo(w, 1, 0)
                    else:
                        weight_lo(W_OUT1, W_OUT1 % 2, 0)
                if i == 1:
                    if not last:
                        weight_lo(w + 1, 0, 1)
                    else:
                        weight_lo(W_OUT1 + 1, (W_OUT1 + 1) % 2, 1)
                if i >= 2:
                    state_lo(g, i - 1)
            state_lo(g, STEPS - 1)
            if not last:
                weight_lo(w + 2, 1, 2)
            for c in range(LT):
                n = LT * g + c
                if c:
                    pool.wait_ge(s_y2, n)
                G_.tensor_tensor(by_head(xD[:], HD), by_head(xt[:, CT + c, :], HD), per_head(GP[:, R_D, 0, :], HD),
                                 ALU.mult).then_inc(s_xD, 1)
                if c < LT - 1:
                    decays_dt(g, c + 1)
                if c == 1 and not last:
                    weight_lo(w + 3, 0, 0)
                if c == 3 and not last:
                    weight_lo(w + 4, 1, 1)
                pool.wait_ge(s_yv, n + 1)
                inv_sqrt(yrs[:, 0:1], yvv[:, 0:1], 1, s_yr)
            if not last:
                weight_lo(w + 5, 0, 2)

        def decays_dt(g, c):
            pool.wait_ge(s_e, LT * g + c + 1)
            e = by_head(E, P)
            G_.tensor_tensor(e, e, per_head(GP[:, R_DT + c].rearrange("p d h -> p (d h)"), P), ALU.mult).then_inc(s_ed, 1)

        def state_lo(g, i):
            pool.wait_ge(s_Hh, LT * g + i)
            G_.tensor_tensor(Hlo[:, i - 1, 0, :], hcur[:, 0:GW], f(Hhi[:, i - 1, 0, :]), ALU.subtract)
            G_.tensor_tensor(Hlo[:, LT - i, 1, :], hcur[:, GW:2 * GW], f(Hhi[:, LT - i, 1, :]),
                             ALU.subtract).then_inc(s_Hl, 1)

        with pool.Fori(0, SSM_GROUPS - 1) as g:
            ssd(g, False)
        ssd(SSM_GROUPS - 1, True)
        for c in range(2, 2 * KT):
            weight_lo(W_OUT1 + c, (W_OUT1 + c) % 2, c % NR)
        pool.wait_ge(s_var, 6)
        inv_sqrt(rstd[:, 3, 0:LT], vvar[:, 3, 0:LT], LT, s_rstd)

    @block.tensor
    def _(pe):
        def mm3(out, a_hi, a_lo, b_hi, b_lo, start, stop):
            PE_.matmul(out, a_hi, b_hi, start=start, stop=False, skip_group_check=True)
            PE_.matmul(out, a_hi, b_lo, start=False, stop=False, skip_group_check=True)
            return PE_.matmul(out, a_lo, b_hi, start=False, stop=stop, skip_group_check=True)

        def modulation(slot, out):
            for k in range(KT):
                last = PE_.matmul(out, wraw[:, slot, k, :], csilu[:, k, :], start=k == 0, stop=k == KT - 1,
                                  skip_group_check=True)
            last.then_inc(s_ada, 1)

        pe.wait_ge(s_c, 3)
        for t in range(ADA_EARLY):
            pe.wait_ge(s_w[t % NR], 16 * (t // NR + 1))
            modulation(t % NR, psV[:, 2 * t:2 * t + 2])
        pe.wait_ge(s_const, 4)
        pe.wait_ge(s_xn, TT)
        for k in range(KT):
            ps = (psS, psT)[k % 2]
            if k >= 2:
                pe.wait_ge(s_hs, k - 1)
            for t in range(TT):
                last = PE_.transpose(ps[:, t * P:(t + 1) * P], X0[:, t, k * P:(k + 1) * P], ident[:])
            last.then_inc(s_xt, 1)

        def project(e, kind, part, k0, k1, w, done):
            par = kind
            toks = slice(0, CTX) if part == 0 else slice(CTX, TOK)
            out = psC[:, 0:CTX] if part == 0 else psL[kind][:, :]
            for i in range(k0, k1):
                k, m = divmod(i, 3)
                a = (whi, whi, wlo)[m][:, par, k, :]
                b = (hhi, hlo, hhi)[m][:, k, toks]
                last = PE_.matmul(out, a, b, start=i == 0, stop=i == 3 * KT - 1, skip_group_check=True)
                if i == 3 * KT - 1:
                    last.then_inc(done, 1)

        def ctx_bank_free(e, kind):
            if kind == 0:
                if isinstance(e, int) and e <= GROUPS:
                    if e:
                        pe.wait_ge(s_thc, e)
                else:
                    pe.wait_ge(s_sgc, e - GROUPS)
            else:
                pe.wait_ge(s_qcev, e + 1)

        def lat_bank_free(e, kind):
            if kind == 0:
                if not (isinstance(e, int) and e == 0):
                    pe.wait_ge(s_qlev, e)
            elif isinstance(e, int) and e <= GROUPS:
                if e:
                    pe.wait_ge(s_thl, e)
            else:
                pe.wait_ge(s_sgl, e - GROUPS)

        def tile_ready(w):
            pe.wait_ge(s_whi, w + 1)
            pe.wait_ge(s_wlo, w + 1)

        def project_tile(e, kind, w):
            tile_ready(w)
            ctx_bank_free(e, kind)
            project(e, kind, 0, 0, 3 * KT, w, (s_qc, s_gc)[kind])
            lat_bank_free(e, kind)
            project(e, kind, 1, 0, 3 * KT, w, (s_ql, s_gl)[kind])

        def square_sums(u, e, pairs=None):
            pe.wait_ge(s_qlev, e + 1)
            if not (isinstance(u, int) and u == 0):
                pe.wait_ge(s_vq, u)
            if pairs is not None:
                pe.wait_ge(s_y, pairs)
            for t in range(TT):
                last = PE_.matmul(psV[:, t:t + 1], SQ[:, t * P:(t + 1) * P], ones[:, 0:1],
                                  start=True, stop=True, skip_group_check=True)
            last.then_inc(s_nq, 1)

        def finish_kv(g):
            if g >= 2:
                square_sums(g - 2, g)
            pe.wait_ge(s_thl, g + 1)
            if g >= 1:
                pe.wait_ge(s_vlo, g)
            if g >= 3:
                pe.wait_ge(s_kn, g - 2)
            for t in range(TT):
                last = PE_.transpose(psT[:, t * P:(t + 1) * P], TH[:, t * P:(t + 1) * P], ident[:])
            last.then_inc(s_vt, 1)
            if g >= 2:
                pe.wait_ge(s_dgk, g - 1)
                pe.wait_ge(s_vlo, g + 1)
                for t in range(TT):
                    last = PE_.matmul(psT[:, t * P:(t + 1) * P], ones[:], dgk[:, t, :], start=True, stop=True,
                                      skip_group_check=True)
                last.then_inc(s_rkb, 1)

        pe.wait_ge(s_hl, KT)
        for e in range(GROUPS + 1):
            project_tile(e, 0, 2 * e)
            if e:
                finish_kv(e - 1)
            project_tile(e, 1, 2 * e + 1)

        def scores(r, s):
            n = SLOTS * r + s
            hs, b = s // BLOCKS, s % BLOCKS
            banded, (lo, hi, a) = hs < 2, window(b, hs < 2)
            if b == 0:
                pe.wait_ge(s_qlo, GROUPS + GROUPS * r + hs + 1)
            if s:
                pe.wait_ge(s_ex, n)
            q = slice(b * P, (b + 1) * P)
            qh, ql = Qhi[:, hs % 2, q], Qlo[:, hs % 2, q]
            if hi > lo:
                keys = slice(CTX + lo * P, CTX + hi * P)
                i = b - CT
                mm3(psS[:, a:SEQ], qh, ql, Khi[:, hs, keys], Klo[:, hs, keys], True, not banded)
                if banded and i >= 1:
                    PE_.matmul(psS[:, a:a + P], identr[:], maskr[:, 0, :], start=False, stop=i == LT - 1,
                               skip_group_check=True)
                if banded and i < LT - 1:
                    PE_.matmul(psS[:, SEQ - P:SEQ], identr[:], maskr[:, 1, :], start=False, stop=True,
                               skip_group_check=True)
            mm3(psS[:, SEQ:TOK], qh, ql, Khi[:, hs, 0:CTX], Klo[:, hs, 0:CTX], True, True).then_inc(s_sc, 1)

        def transposes(r, s):
            n = SLOTS * r + s
            lo, hi, a = window(s % BLOCKS, s // BLOCKS < 2)
            pe.wait_ge(s_pn, n + 1)
            if s:
                pe.wait_ge(s_ptl, n)
            if s % BLOCKS in (0, 3):
                c = s % BLOCKS // 3
                pe.wait_ge(s_w[2 + c], 16 * (USES_HEAD0 + 1) + 16 * (GROUPS * r + s // BLOCKS))
                at = LATEC + 2 * (2 * (s // BLOCKS) + c)
                modulation(2 + c, psT[:, at:at + 2])
            for t in range(a // P, TT):
                last = PE_.transpose(psT[:, t * P:(t + 1) * P], PR[:, s % 2, t * P:(t + 1) * P], ident[:])
            last.then_inc(s_pt, 1)

        def values(r, pair):
            hs, q = pair // PAIRS, pair % PAIRS
            p = PAIRS * GROUPS * r + pair
            pe.wait_ge(s_ptl, 2 * p + 2)
            if pair:
                pe.wait_ge(s_y, p)
            if q == 1 and hs in (1, 2):
                pe.wait_ge(s_vq, 2 * r + hs + 2)
            todo = [(c, SEQ // P + c, 0, 2) for c in range(CT)]
            if q:
                b = 2 * q
                (lo0, hi0, a0), (lo1, hi1, a1) = window(b, hs < 2), window(b + 1, hs < 2)
                slot = lambda kt, lo, a: a // P + kt - lo
                for kt in range(min(lo0, lo1), max(hi0, hi1)):
                    in0, in1 = lo0 <= kt < hi0, lo1 <= kt < hi1
                    if in0 and in1 and slot(kt, lo0, a0) == slot(kt, lo1, a1):
                        todo.append((CT + kt, slot(kt, lo0, a0), 0, 2))
                    else:
                        if in0:
                            todo.append((CT + kt, slot(kt, lo0, a0), 0, 1))
                        if in1:
                            todo.append((CT + kt, slot(kt, lo1, a1), 1, 2))
            for i, (kt, sl, x0, x1) in enumerate(todo):
                x = slice(x0 * P, x1 * P)
                last = mm3(psV[:, x0 * P:x1 * P], Vhi[:, kt, hs * P:(hs + 1) * P],
                           Vlo[:, kt, hs * P:(hs + 1) * P], PThi[:, sl, x], PTlo[:, sl, x], i == 0,
                           i == len(todo) - 1)
            last.then_inc(s_pv, 1)

        def next_part(r, s, h, last):
            hs = min(s // BLOCKS, GROUPS - 1)
            if last and hs == GROUPS - 1:
                return
            e, w = GROUPS + GROUPS * r + hs + 1, W_HEAD0 + 2 * (GROUPS * r + hs + 1)
            at = 2 * (s - hs * BLOCKS) + h
            if hs < GROUPS - 1:
                i0, i1 = 8 * at, 8 * at + 8
            else:
                i0, i1 = (6 * at, 6 * at + 6) if at < 12 else (72 + 12 * ((at - 12) // 2), 72 + 12 * ((at - 12) // 2) + 12)
                if at >= 12 and h == 1:
                    return
            kind, part, i0 = i0 // 48, i0 // 24 % 2, i0 % 24
            i1 = i0 + (8 if hs < GROUPS - 1 else 6 if at < 12 else 12)
            if i0 == 0 and part == 0:
                tile_ready(w + kind)
                ctx_bank_free(e, kind)
            if i0 == 0 and part == 1:
                lat_bank_free(e, kind)
            project(e, kind, part, i0, i1, w + kind, ((s_qc, s_gc), (s_ql, s_gl))[part][kind])

        def attention(r, last):
            for s in range(SLOTS + 2):
                hs, b = s // BLOCKS, s % BLOCKS
                if s < SLOTS:
                    scores(r, s)
                if s >= 3 and s % 2 and s < SLOTS:
                    values(r, (s - 3) // 2)
                next_part(r, s, 0, last)
                if 1 <= s <= SLOTS:
                    transposes(r, s - 1)
                next_part(r, s, 1, last)
                if (h := due(s, 4, 5)) is not None and not (last and h == GROUPS - 1) and (h + 1) % GROUPS >= 2:
                    square_sums(2 * r + h + 1, GROUPS + GROUPS * r + h + 1, PAIRS * (GROUPS * r + h) + 1)
                if s == SLOTS + 1:
                    values(r, PAIRS * GROUPS - 1)

        with pe.Fori(0, HEADS // GROUPS - 1) as r:
            attention(r, False)
        attention(HEADS // GROUPS - 1, True)

        for nh in range(2):
            for c in range(KT):
                w = W_OUT0 + nh * KT + c
                tile_ready(w)
                for kk in range(2):
                    k = 2 * c + kk
                    wh = whi[:, w % 2, 4 * kk:4 * kk + 4, :].rearrange("p a b -> p (a b)")
                    wl = wlo[:, w % 2, 4 * kk:4 * kk + 4, :].rearrange("p a b -> p (a b)")
                    if nh == 0:
                        pe.wait_ge(s_yl, k + 1)
                    for t in range(TT):
                        if k == 0:
                            if nh == 0 and t == 0:
                                pe.wait_ge(s_y, PAIRS * HEADS)
                                pe.wait_ge(s_ptl, BLOCKS * HEADS)
                            if nh == 1:
                                pe.wait_ge(s_yo, t + 1)
                        q = slice(t * P, (t + 1) * P)
                        last = mm3(tok_bank[t], Yhi[:, k, q], Ylo[:, k, q], wh, wl, k == 0, k == HEADS - 1)
                        if k == HEADS - 1:
                            last.then_inc(s_half, 1)
                if c < KT - 1:
                    last.then_inc(s_wused, 1)
                if nh == 0 and c in (4, 6):
                    v = (c - 4) // 2
                    if v:
                        pe.wait_ge(s_gre, 1)
                    for k in range(KT):
                        pe.wait_ge(s_dg, v * KT + k + 1)
                        last = PE_.matmul(psT[:, k * P:(k + 1) * P], ones[:], dg[:, k, :], start=True,
                                          stop=True, skip_group_check=True)
                        last.then_inc(s_gr4, 1)

        pe.wait_ge(s_xn, TT + TT)
        pe.wait_ge(s_yo, 2 * TT)
        for k in range(KT):
            ps = (psS, psT)[k % 2]
            if k >= 2:
                pe.wait_ge(s_hs, KT + k - 1)
            for t in range(TT):
                last = PE_.transpose(ps[:, t * P:(t + 1) * P], XN[:, t, k * P:(k + 1) * P], ident[:])
            last.then_inc(s_xt, 1)
        H2_ = 2 * SSM_HEADS
        tile_ready(W_DT)
        pe.wait_ge(s_hl, KT + KT)
        for t in range(TT):
            for k in range(KT):
                q = slice(t * P, (t + 1) * P)
                last = mm3(psL[0][:, t * H2_:(t + 1) * H2_], h1hi[:, k, q], h1lo[:, k, q], whi[:, 0, k, 0:H2_],
                           wlo[:, 0, k, 0:H2_], k == 0, k == KT - 1)
        last.then_inc(s_dtp, 1)
        pe.wait_ge(s_aa, 3)
        pe.wait_ge(s_tri, TRI_STEPS)
        cF = psL[1][:, 0:TT * H2_].rearrange("p (t h) -> p t h", t=TT)
        for d in range(DIRS):
            h = slice(d * SSM_HEADS, (d + 1) * SSM_HEADS)
            PE_.matmul(cF[:, :, h], trir[:, d, :], ahi[:, :, h], start=True, stop=False, skip_group_check=True)
            PE_.matmul(cF[:, :, h], trir[:, d, :], alo[:, :, h], start=False, stop=True, skip_group_check=True)
        PE_.matmul(psS[:, 0:TT * H2_], onesr[:], ahi[:].rearrange("p t h -> p (t h)"), start=True, stop=False,
                   skip_group_check=True)
        PE_.matmul(psS[:, 0:TT * H2_], onesr[:], alo[:].rearrange("p t h -> p (t h)"), start=False, stop=True,
                   skip_group_check=True).then_inc(s_cum, 1)

        def project1(g, i, part, k0, k1, q2):
            toks = slice(0, CTX) if part == 0 else slice(CTX, TOK)
            out = psC[:, 0:CTX] if part == 0 else psL[i % 2][:, :]
            for j in range(k0, k1):
                k, m = divmod(j, 3)
                last = PE_.matmul(out, (whi, whi, wlo)[m][:, q2, k, :], (h1hi, h1lo, h1hi)[m][:, k, toks],
                                  start=j == 0, stop=j == 3 * KT - 1, skip_group_check=True)
            if k1 == 3 * KT:
                last.then_inc((s_pc, s_pl)[part], 1)

        def tile_start(g, i, part, w, first):
            if part == 0 or i == 3:
                tile_ready(w)
            if part == 0:
                if not (first and i == 0):
                    pe.wait_ge(s_cvc, 3 * g + i)
            elif not (first and i < 2):
                pe.wait_ge(s_cvl, 4 * g + i - 1)

        for i in range(4):
            for part in range(2):
                if i == 3 and part == 0:
                    continue
                tile_start(0, i, part, W_SSM + i, True)
                if i == 0 and part == 1:
                    pe.wait_ge(s_dt, 1)
                if i == 1 and part == 1:
                    pe.wait_ge(s_cum, 2)
                project1(0, i, part, 0, 3 * KT, (W_SSM + i) % 2)

        def ssd(g, last_group):
            G = g + 1
            def tokens(i):
                pe.wait_ge(s_u, 4 * g + i + 1)
                if i:
                    pe.wait_ge(s_txe, 3 * g + i)
                for t in range(TT):
                    last = PE_.transpose(psT[:, t * P:(t + 1) * P], U[i][:, t * P:(t + 1) * P], ident[:])
                last.then_inc(s_tx, 1)

            def z(half, cs):
                for c in cs:
                    q = slice((CT + c) * P, (CT + c + 1) * P)
                    for kk in range(KT // 2):
                        k = half * KT // 2 + kk
                        slot = (1, 0)[half]
                        wh = whi[:, slot, 2 * kk:2 * kk + 2, :].rearrange("p a b -> p (a b)")
                        wl = wlo[:, slot, 2 * kk:2 * kk + 2, :].rearrange("p a b -> p (a b)")
                        last = mm3(psS[:, c * GW:(c + 1) * GW], h1hi[:, k, q], h1lo[:, k, q], wh, wl,
                                   k == 0 and c % 2 == 0, k == KT - 1)
                return last

            def next_part(p):
                if last_group:
                    return
                i, part = ((0, 0), (0, 1), (1, 0), (1, 1), (2, 0), (2, 1), (3, 1))[p // 2]
                if p % 2 == 0:
                    tile_start(G, i, part, W_SSM + 6 + 6 * g + i, False)
                project1(G, i, part, 12 * (p % 2), 12 * (p % 2) + 12, (1, 0, 1, 0)[i])

            def log_decays(c):
                if c == 0:
                    pe.wait_ge(s_btl, g + 1)
                    pe.wait_ge(s_gpa, g + 1)
                else:
                    pe.wait_ge(s_e, LT * g + c)
                for d in range(DIRS):
                    bank = psT[:, d * 512:(d + 1) * 512]
                    PE_.matmul(bank, identr[:], negr[:, d, :].unsqueeze(1).broadcast_to([P, GH, P]), start=True,
                               stop=False, skip_group_check=True)
                    for h in range(GH):
                        for m, a in enumerate((aghi, aglo)):
                            last = PE_.matmul(bank[:, h * P:(h + 1) * P], a[:, c, d, h:h + 1].broadcast_to([P, P]),
                                              trir[:, d, :], start=False, stop=m == 1, skip_group_check=True)
                last.then_inc(s_r, 1)

            def cb(c):
                q = slice(c * P, (c + 1) * P)
                mm3(ybank[1][:, 0:P], bfhi[:, 0, q], bflo[:, 0, q], bfhi[:, 1, q], bflo[:, 1, q], True,
                    True).then_inc(s_cb, 1)

            tile_ready(W_SSM + 4 + 6 * g)
            tokens(0)
            z(0, (0, 1))
            tokens(1)
            z(0, (2, 3)).then_inc(s_zc, 1)
            tokens(2)
            tile_ready(W_SSM + 5 + 6 * g)
            z(1, (0, 1))
            z(1, (2, 3)).then_inc(s_zc, 1)
            log_decays(0)
            pe.wait_ge(s_sz, g + 1)
            pe.wait_ge(s_bfl, g + 1)
            cb(0)
            for i in range(STEPS):
                pe.wait_ge(s_xwl, STEPS * g + i + 1)
                if i:
                    pe.wait_ge(s_hc, STEPS * g + i)
                for d, u in ((0, FWD[i]), (1, BWD[i])):
                    x = slice(d * GW, (d + 1) * GW)
                    last = mm3(ybank[0][:, x], bthi[:, u, :], btlo[:, u, :], xwhi[:, x], xwlo[:, x], True, True)
                last.then_inc(s_st, 1)
                next_part(i)
            next_part(STEPS)
            pe.wait_ge(s_txl, g + 1)
            for c in range(LT):
                n = LT * g + c
                if c < LT - 1:
                    log_decays(c + 1)
                pe.wait_ge(s_ml, n + 1)
                for h in range(GH):
                    x, m = slice(h * HD, (h + 1) * HD), slice(h * P, (h + 1) * P)
                    last = mm3(ybank[1][:, P + h * HD:P + (h + 1) * HD], Mhi[:, m], Mlo[:, m], xthi[:, c, x],
                               xtlo[:, c, x], True, True)
                last.then_inc(s_yd, 1)
                if c == 0:
                    pe.wait_ge(s_hc, STEPS * (g + 1))
                    pe.wait_ge(s_Hl, LT * (g + 1))
                else:
                    pe.wait_ge(s_y1, n)
                q = slice(c * P, (c + 1) * P)
                mm3(ybank[0], bfhi[:, 1, q], bflo[:, 1, q], Hhi[:, c].rearrange("p d x -> p (d x)"),
                    Hlo[:, c].rearrange("p d x -> p (d x)"), True, True).then_inc(s_yof, 1)
                next_part(6 + 2 * c)
                if c:
                    y_transposed(g, c - 1)
                if c < LT - 1:
                    pe.wait_ge(s_y2, n + 1)
                    cb(c + 1)
                next_part(7 + 2 * c)
            y_transposed(g, LT - 1)

        def y_transposed(g, c):
            pe.wait_ge(s_yn, LT * g + c + 1)
            if c:
                pe.wait_ge(s_yte, LT * g + c)
            for i in range(2):
                last = PE_.transpose(psV[:, i * P:(i + 1) * P], ynm[:, i * P:(i + 1) * P], ident[:])
            last.then_inc(s_yt, 1)

        with pe.Fori(0, SSM_GROUPS - 1) as g:
            ssd(g, False)
        ssd(SSM_GROUPS - 1, True)

        for nh in range(2):
            for c in range(KT):
                i = nh * KT + c
                tile_ready(W_OUT1 + i)
                for kk in range(2):
                    k = 2 * c + kk
                    sl = (W_OUT1 + i) % 2
                    wh = whi[:, sl, 4 * kk:4 * kk + 4, :].rearrange("p a b -> p (a b)")
                    wl = wlo[:, sl, 4 * kk:4 * kk + 4, :].rearrange("p a b -> p (a b)")
                    if nh == 0:
                        pe.wait_ge(s_yl, HEADS + k + 1)
                    for t in range(LT):
                        if k == 0 and nh == 1:
                            pe.wait_ge(s_yo, 2 * TT + t + 1)
                        q = slice(t * P, (t + 1) * P)
                        last = mm3(tok_bank[t], Y1hi[:, k, q], Y1lo[:, k, q], wh, wl, k == 0, k == HEADS - 1)
                        if k == HEADS - 1:
                            last.then_inc(s_half, 1)
                if c < KT - 1:
                    last.then_inc(s_wused, 1)
                if nh == 0 and c == 4:
                    for k in range(KT):
                        pe.wait_ge(s_dg1, k + 1)
                        PE_.matmul(psT[:, k * P:(k + 1) * P], ones[:], dg1[:, k, :], start=True, stop=True,
                                   skip_group_check=True).then_inc(s_gr1, 1)


def kernel(**inputs):
    import numpy as np
    import concourse.bacc as bacc
    from concourse.bass_utils import run_bass_kernel_spmd as run
    a = {k: np.asarray(v) for k, v in inputs.items()}
    f32 = mybir.dt.float32

    def tiles(w, columns):
        w = w[:, columns].reshape(KT, P, -1, P)
        return np.ascontiguousarray(w.transpose(2, 1, 0, 3))

    def colvec(v):
        return v.reshape(-1, P).T

    def out_chunks(w):
        w = w.reshape(-1, 2, P, 2, 512)
        return np.ascontiguousarray(w.transpose(3, 0, 2, 1, 4).reshape(-1, P, KT, P))

    split = np.concatenate([np.arange(0, P, 2), np.arange(1, P, 2)])
    off = dict(zip(("qa", "ka", "va", "ga", "qb", "kb", "vb", "gb"), (0, 1024, 1280, 1536, 2560, 3584, 3840, 4096)))
    order, rows_out, sinks = [], [], []
    for g in range(GROUPS):
        t = "ab"[g // 2]
        order += [off["k" + t] + (g % 2) * P + split, off["v" + t] + (g % 2) * P + np.arange(P)]
    for r in range(HEADS // GROUPS):
        for g in range(GROUPS):
            t, h = "ab"[g // 2], (g % 2) * GROUPS + r
            order += [off["q" + t] + h * P + split, off["g" + t] + h * P + np.arange(P)]
            rows_out.append((g // 2) * 1024 + h * P + np.arange(P))
            if g < 2:
                sinks.append(h)
    order, rows_out = np.concatenate(order), np.concatenate(rows_out)

    inv = 1.0 / (np.float32(10000.0) ** (np.arange(32, dtype=np.float32) / np.float32(32)))
    row = np.repeat(np.arange(SEQ // 64), 64).astype(np.float32)
    colp = np.tile(np.arange(64), SEQ // 64).astype(np.float32)
    ang = np.concatenate([row[:, None] * inv, colp[:, None] * inv], -1).astype(np.float32).T
    cos, sin = np.cos(ang).astype(np.float32), np.sin(ang).astype(np.float32)

    cw = a["ssm_conv_w"][0]
    columns = [colvec(a["b_ada"].reshape(-1)), colvec(a["norm_pre"].reshape(-1)), colvec(a["norm_post"].reshape(-1)),
               colvec(cw.reshape(-1)), colvec(a["ssm_conv_b"][0]), colvec(a["ssm_norm"][0]),
               a["attn_q_norm"][0][split][:, None], a["attn_k_norm"][0][split][:, None]]
    wi = a["ssm_w_in"][0]
    ssm = []
    for g in range(SSM_GROUPS):
        x = [tiles(wi, 2048 + 256 * g + np.arange(256)), tiles(wi, 4096 + P * g + np.arange(P)),
             tiles(wi, 5120 + P * g + np.arange(P))]
        z = wi[:, 256 * g:256 * g + 256].reshape(2, 4, P, 256).transpose(0, 2, 1, 3).reshape(2, P, KT, P)
        ssm += x + [z]
    ada = [tiles(a["w_ada"][l], np.arange(3 * D_MODEL)) for l in range(2)]
    arrays = {
        "xc": np.concatenate([a["ctx"][0], a["x"][0]]).reshape(TT, P, D_MODEL),
        "cvec": np.stack([colvec(a["c"][0]), colvec(a["c_ctx"])], -1),
        "cols": np.concatenate(columns, 1),
        "rows": np.concatenate([a["attn_sink"][0][sinks], a["ssm_a_log"][0].reshape(-1),
                                a["ssm_dt_bias"][0].reshape(-1), a["ssm_d"][0]]),
        "w_ada": ada[0][None, :ADA_EARLY],
        "w_ada_late": np.concatenate([ada[0][ADA_EARLY:], ada[1]]),
        "w_in": tiles(a["attn_w_in"][0], order),
        "w_out0": out_chunks(a["attn_w_out"][0][rows_out]),
        "w_ssm": np.concatenate(ssm),
        "w_dt": wi[:, 6144:6208].reshape(KT, P, 64).transpose(1, 0, 2),
        "w_out1": out_chunks(a["ssm_w_out"][0]),
        "cos": np.concatenate([cos, cos]), "sin": np.concatenate([sin, -sin]),
    }
    arrays = {"in_" + k: np.ascontiguousarray(v) for k, v in arrays.items()}
    nc = bacc.Bacc("TRN2", target_bir_lowering=False, num_devices=1)
    io = {k[3:]: nc.dram_tensor(k, v.shape, f32, kind="ExternalInput").ap() for k, v in arrays.items()}
    io["out"] = nc.dram_tensor("out", (LT, P, D_MODEL), f32, kind="ExternalOutput").ap()
    io["y_spill"] = nc.dram_tensor("y_spill", (HEADS, P, TOK), f32, kind="Internal").ap()
    io["x1_spill"] = nc.dram_tensor("x1_spill", (LT, P, D_MODEL), f32, kind="Internal").ap()
    io["y1_spill"] = nc.dram_tensor("y1_spill", (SSM_GROUPS, P, 2, SEQ), f32, kind="Internal").ap()
    build(nc, io)
    r = run(nc, [arrays], core_ids=[0])
    return r.results[0]["out"].reshape(1, SEQ, D_MODEL)
```

```python
import concourse.bass as bass
from concourse import mybir
from contextlib import ExitStack

P = 128
D_MODEL, SEQ, CTX = 1024, 512, 256
TOK = CTX + SEQ
TT = TOK // P
CT = CTX // P
KT = D_MODEL // P
EPS = 1e-6
HEADS = 16
GROUPS = 4
SCALE = P ** -0.5
NR = 4
ADA = 3 * KT
ADA_EARLY = 2 * KT
MASKED = -float(2 ** 100)
SSM_GROUPS = 8
SSM_HEADS = 32
GH = SSM_HEADS // SSM_GROUPS
HD = 64
GW = GH * HD
LT = SEQ // P
DIRS = 2


def column_places():
    at, where = 0, {}
    for name, n in (("b_ada", 2 * ADA), ("pre", 2 * KT), ("post", 2 * KT), ("conv_w", 3 * 32), ("conv_b", 32),
                    ("ssm_norm", 16), ("q_norm", 1), ("k_norm", 1)):
        where[name] = (at, at + n)
        at += n
    return where, at


COLS, NCOLS = column_places()
R_LOG, R_EA, R_WE, R_DEC, R_D = 0, 4, 8, 13, 18
TAB_ROWS = 19
STEPS = 5
FWD, BWD = (0, 1, 2, 3, 4), (1, 0, 5, 4, 3)
ROWS = {"sink": (0, 8), "a_log": (8, 72), "dt_bias": (72, 136), "d": (136, 168)}
NROWS = 168


def build(nc, io):
    f32, f32r = mybir.dt.float32, mybir.dt.float32r
    ALU, ACT, AX = mybir.AluOpType, mybir.ActivationFunctionType, mybir.AxisListType
    PE_, V_, A_, G_ = nc.tensor, nc.vector, nc.scalar, nc.gpsimd
    ds = bass.ds

    keep = ExitStack()

    def sbuf(stack, name, shape, dt=f32):
        return stack.enter_context(nc.sbuf_tensor(name, shape, dt))

    def psum(name, shape):
        return keep.enter_context(nc.psum_tensor(name, shape, f32))

    def sem(name):
        return keep.enter_context(nc.semaphore(name))

    def f(ap):
        return ap.bitcast(f32)

    wraw = sbuf(keep, "wraw", [P, NR, KT, P])
    whi = sbuf(keep, "whi", [P, 2, KT, P], f32r)
    wlo = sbuf(keep, "wlo", [P, 2, KT, P], f32r)
    cols = sbuf(keep, "cols", [P, NCOLS])
    ident = sbuf(keep, "ident", [P, P])
    identr = sbuf(keep, "identr", [P, P], f32r)
    ones = sbuf(keep, "ones", [P, P])
    mod = sbuf(keep, "mod", [P, 2 * ADA, 2])
    modp = sbuf(keep, "modp", [P, GROUPS, 2])
    gain = sbuf(keep, "gain", [P, 2, KT, 2])
    ssq = sbuf(keep, "ssq", [P, 4, 8])
    vvar = sbuf(keep, "vvar", [P, 4, 8])
    rstd = sbuf(keep, "rstd", [P, 4, 8])
    half = sbuf(keep, "half", [P, 8])
    nothing = sbuf(keep, "nothing", [P, 1])
    gcolx = sbuf(keep, "gcolx", [P, 2, KT, 2])

    psL = [psum("psL0", [P, 512]), psum("psL1", [P, 512])]
    psC = psum("psC", [P, 512])
    psS = psum("psS", [P, 1024])
    psT = psum("psT", [P, 1024])
    psV = psum("psV", [P, 512])
    tok_bank = [psL[0][:, :], psL[1][:, :], psC[:, :], psS[:, 0:512], psS[:, 512:1024], psV[:, :]]

    ph = ExitStack()
    csilu = sbuf(ph, "csilu", [P, 2, D_MODEL])
    hhi = sbuf(ph, "hhi", [P, KT, TOK], f32r)
    hlo = sbuf(ph, "hlo", [P, KT, TOK], f32r)
    with ExitStack() as s:
        X0 = sbuf(s, "X0", [P, TT, D_MODEL])
        HS0 = sbuf(s, "HS0", [P, 2, TOK])
        junk0 = sbuf(s, "junk0", [P, D_MODEL])
        cth = sbuf(s, "cth", [P, 2, D_MODEL])
    with ExitStack() as s:
        rowt = sbuf(s, "rowt", [P, 8])
        nsink = sbuf(s, "nsink", [P, 8])
        costab = sbuf(s, "costab", [P, SEQ])
        sintab = sbuf(s, "sintab", [P, SEQ])
        maskr = sbuf(s, "maskr", [P, 2, P], f32r)
        Khi = sbuf(s, "Khi", [P, GROUPS, TOK], f32r)
        Klo = sbuf(s, "Klo", [P, GROUPS, TOK], f32r)
        Vhi = sbuf(s, "Vhi", [P, TT, GROUPS * P], f32r)
        Vlo = sbuf(s, "Vlo", [P, TT, GROUPS * P], f32r)
        PThi = sbuf(s, "PThi", [P, TT, 2 * P], f32r)
        PTlo = sbuf(s, "PTlo", [P, TT, 2 * P], f32r)
        QR = sbuf(s, "QR", [P, TOK])
        SQ = sbuf(s, "SQ", [P, TOK])
        T1 = sbuf(s, "T1", [P, SEQ])
        T2 = sbuf(s, "T2", [P, SEQ])
        Qhi = sbuf(s, "Qhi", [P, 2, TOK], f32r)
        Qlo = sbuf(s, "Qlo", [P, 2, TOK], f32r)
        TH = sbuf(s, "TH", [P, TOK])
        SG = sbuf(s, "SG", [P, 2, TOK])
        PR = sbuf(s, "PR", [P, 2, TOK])
        Yst = sbuf(s, "Yst", [P, 2, TOK])
        smax = sbuf(s, "smax", [P, 2])
        nmax = sbuf(s, "nmax", [P, 2])
        esum = sbuf(s, "esum", [P, 2])
        esink = sbuf(s, "esink", [P, 2])
        eall = sbuf(s, "eall", [P, 2])
        rinv = sbuf(s, "rinv", [P, 2])
        vq = sbuf(s, "vq", [P, TT])
        rq = sbuf(s, "rq", [P, 2, TT])
        dgk = sbuf(s, "dgk", [P, TT, P])
        product0 = sbuf(s, "product0", [P, D_MODEL])

    def flat(ap):
        return ap.rearrange("p a b -> p (a b)")[:, 0:D_MODEL]

    product = flat(Yst[:])
    products = (product0[:], flat(SG[:]))
    ph.close()
    ph = ExitStack()
    X1 = sbuf(ph, "X1", [P, TT, D_MODEL])
    with ExitStack() as s:
        Yhi = sbuf(s, "Yhi", [P, HEADS, TOK], f32r)
        Ylo = sbuf(s, "Ylo", [P, HEADS, TOK], f32r)
        Yraw = sbuf(s, "Yraw", [P, 2, TOK])
        Yo = sbuf(s, "Yo", [P, TT, D_MODEL])
        grow = sbuf(s, "grow", [P, 2, D_MODEL])
        dg = sbuf(s, "dg", [P, KT, P])
        junk1 = sbuf(s, "junk1", [P, 512])
    h1hi = sbuf(ph, "h1hi", [P, KT, TOK], f32r)
    h1lo = sbuf(ph, "h1lo", [P, KT, TOK], f32r)
    with ExitStack() as s:
        XN = sbuf(s, "XN", [P, TT, D_MODEL])
        HS1 = sbuf(s, "HS1", [P, 2, TOK])
        junk2 = sbuf(s, "junk2", [P, D_MODEL])
    x1flat = X1[:, :, :].rearrange("p t d -> p (t d)")
    places = {}
    UEND = 3 * TOK + SEQ
    at = 0
    for name, n in (("U", 3 * TOK + SEQ), ("sz", LT * GW), ("E", DIRS * GH * P), ("y1", 2 * GW), ("y2", GW),
                    ("y3", GW), ("yg", GW)):
        places[name] = x1flat[:, at:at + n]
        at += n
    U, sz, E, y1, y2, y3, yg = places.values()
    U = [U[:, i * TOK:min((i + 1) * TOK, 3 * TOK + SEQ)] for i in range(4)]
    with ExitStack() as s:
        rows1 = sbuf(s, "rows1", [P, NROWS - 8])
        TAB = sbuf(s, "TAB", [P, TAB_ROWS, 2 * SSM_HEADS])
        GP = sbuf(s, "GP", [P, TAB_ROWS, DIRS, GH])
        acu = sbuf(s, "acu", [P, TT, 2 * SSM_HEADS])
        ahi = sbuf(s, "ahi", [P, TT, 2 * SSM_HEADS], f32r)
        alo = sbuf(s, "alo", [P, TT, 2 * SSM_HEADS], f32r)
        aghi = sbuf(s, "aghi", [P, LT, DIRS, GH], f32r)
        aglo = sbuf(s, "aglo", [P, LT, DIRS, GH], f32r)
        trir = sbuf(s, "trir", [P, DIRS, P], f32r)
        onesr = sbuf(s, "onesr", [P, P], f32r)
        negr = sbuf(s, "negr", [P, DIRS, P], f32r)
        convh = sbuf(s, "convh", [P, 4 * 32])
        normh = sbuf(s, "normh", [P, 16])
        gtap = sbuf(s, "gtap", [P, 4, 4])
        gnorm = sbuf(s, "gnorm", [P, 2])
        xt = sbuf(s, "xt", [P, TT, GW])
        xthi = sbuf(s, "xthi", [P, LT, GW], f32r)
        xtlo = sbuf(s, "xtlo", [P, LT, GW], f32r)
        bthi = sbuf(s, "bthi", [P, TT, P], f32r)
        btlo = sbuf(s, "btlo", [P, TT, P], f32r)
        bfhi = sbuf(s, "bfhi", [P, 2, SEQ], f32r)
        bflo = sbuf(s, "bflo", [P, 2, SEQ], f32r)
        xw = sbuf(s, "xw", [P, 2, DIRS * GW])
        xwhi = sbuf(s, "xwhi", [P, 2, DIRS * GW], f32r)
        xwlo = sbuf(s, "xwlo", [P, 2, DIRS * GW], f32r)
        hcur = sbuf(s, "hcur", [P, DIRS * GW])
        hdec = sbuf(s, "hdec", [P, DIRS * GW])
        Hhi = sbuf(s, "Hhi", [P, LT, DIRS, GW], f32r)
        Hlo = sbuf(s, "Hlo", [P, LT, DIRS, GW], f32r)
        Wm = sbuf(s, "Wm", [P, GH * P])
        Mf = sbuf(s, "Mf", [P, GH * P])
        Mhi = sbuf(s, "Mhi", [P, GH * P], f32r)
        Mlo = sbuf(s, "Mlo", [P, GH * P], f32r)
        xD = sbuf(s, "xD", [P, 2, GW])
        thz = sbuf(s, "thz", [P, LT * GW])
        CTH = sbuf(s, "CTH", [P, TOK])
        yss = sbuf(s, "yss", [P, 2])
        ynm = sbuf(s, "ynm", [P, GW])
        yvv = sbuf(s, "yvv", [P, 2])
        yrs = sbuf(s, "yrs", [P, 2])
        YT = sbuf(s, "YT", [P, 2, SEQ])
    ph.close()
    ph = ExitStack()
    X2 = sbuf(ph, "X2", [P, TT, D_MODEL])
    with ExitStack() as s:
        Y1hi = sbuf(s, "Y1hi", [P, HEADS, SEQ], f32r)
        Y1lo = sbuf(s, "Y1lo", [P, HEADS, SEQ], f32r)
        Y1raw = sbuf(s, "Y1raw", [P, 2, SEQ])
        Yo1 = sbuf(s, "Yo1", [P, LT, D_MODEL])
        grow1 = sbuf(s, "grow1", [P, D_MODEL])
        junk3 = sbuf(s, "junk3", [P, 512])
        dg1 = sbuf(s, "dg1", [P, KT, P])

    s_small = sem("small_loaded")
    s_x = [sem(f"x_loaded{t}") for t in range(TT)]
    s_w = [sem(f"raw_weights_loaded{i}") for i in range(NR)]
    s_const = sem("constants_made")
    s_whi, s_wlo, s_wused = sem("weight_hi"), sem("weight_lo"), sem("weight_used")
    s_ada = sem("modulation_tile_done")
    s_adp, s_ads = sem("modulation_product"), sem("modulation_product_summed")
    s_wx = sem("modulation_tile_loaded")
    s_c = sem("silu_c_step")
    s_mod = sem("modulation_columns")
    s_gain = sem("gain_columns")
    s_ssq, s_var, s_rstd = sem("sum_of_squares"), sem("variance"), sem("rstd")
    s_xn = sem("x_normed")
    s_xt, s_hs, s_hh, s_hl = sem("x_transposed"), sem("h_scaled"), sem("h_hi"), sem("h_lo")
    s_qc, s_ql, s_gc, s_gl = sem("q_ctx_proj"), sem("q_lat_proj"), sem("g_ctx_proj"), sem("g_lat_proj")
    s_rope = sem("rope_step")
    s_qhi, s_qlo = sem("q_hi"), sem("q_lo")
    s_nq, s_vq, s_rq = sem("qk_square_sums"), sem("qk_variance"), sem("qk_rstd")
    s_dgk, s_rkb, s_kn = sem("k_rstd_diag"), sem("k_rstd_rows"), sem("k_normed")
    s_vt, s_vhi, s_vlo = sem("v_transposed"), sem("v_hi"), sem("v_lo")
    s_sc, s_mx, s_nm, s_ex, s_es = sem("scores"), sem("score_max"), sem("neg_max"), sem("probs"), sem("sink_exp")
    s_ea, s_ri, s_pn = sem("denominator"), sem("inv_denominator"), sem("probs_normed")
    s_pt, s_pth, s_ptl = sem("probs_transposed"), sem("probs_t_hi"), sem("probs_t_lo")
    s_pv, s_y, s_yst = sem("pv_done"), sem("y_gated"), sem("y_stored")
    s_adal = sem("late_modulation_columns")
    s_yld = [sem(f"y_loaded{i}") for i in range(2)]
    s_yh, s_yl = sem("y_hi"), sem("y_lo")
    s_half, s_yo, s_sq2 = sem("out_half"), sem("out_evacuated"), sem("out_squares")
    s_gate, s_dg, s_gre = sem("gate_columns"), sem("gate_diag"), sem("gate_rows_out")
    s_res, s_out = sem("residual"), sem("out_stored")
    s_xr = sem("x_reloaded")
    s_gr4 = sem("gate_diag_used")
    s_tab, s_nsink, s_mask = sem("tables_loaded"), sem("neg_sink"), sem("band_masks")
    s_t1, s_t2 = sem("rope_cos_part"), sem("rope_sin_part")
    s_qcev, s_qlev = sem("q_ctx_evacuated"), sem("q_lat_evacuated")
    s_thc, s_thl, s_sgc, s_sgl = sem("tanh_ctx"), sem("tanh_lat"), sem("gate_ctx"), sem("gate_lat")

    NW_KV = 2 * GROUPS
    W_HEAD0 = NW_KV
    W_OUT0 = NW_KV + 2 * HEADS
    USES_ADA = ADA_EARLY // NR
    ADA_LATE = HEADS
    ADA_LAST = 2 * ADA - ADA_EARLY - ADA_LATE
    assert ADA_LAST == HEADS
    LATE_AHEAD = 4
    LATE_SHARE = ((2, 1), (2, 1), (2, 1), (2, 1))
    LATE_START = [LATE_AHEAD + sum(sum(p) for p in LATE_SHARE[:g]) for g in range(GROUPS + 1)]
    assert LATE_START[GROUPS] == ADA_LATE
    USES_HEAD0 = USES_ADA + NW_KV // 2
    USES_LAST = (USES_ADA + 6, USES_ADA + 5)
    USES_OUT0 = [USES_HEAD0 + HEADS] * 2 + [n + HEADS // 2 for n in USES_LAST]
    STORED = 32

    W_DT = W_OUT0 + 2 * KT
    W_SSM = W_DT + 1
    W_OUT1 = W_SSM + 4 + 6 * SSM_GROUPS - 4
    USES_SSM = [n + 2 * KT // NR for n in USES_OUT0]
    TRI_STEPS = 11
    Q_OUT1 = W_OUT1 - W_SSM
    USES_OUT1 = [n + Q_OUT1 // 3 for n in USES_SSM[:3]] + [USES_SSM[3] + 1]

    BLOCKS = TT
    PAIRS = TT // 2
    SLOTS = GROUPS * BLOCKS

    def pool_sums(n):
        return n // 3

    def dve_sums(n):
        return n - n // 3

    POOL_LATE = (2 * ADA_EARLY + 2 * ADA_LATE) // 3

    def tile_summed(eng, tile):
        eng.wait_ge(s_ada, dve_sums(2 * tile + 2))
        if pool_sums(2 * tile + 2):
            eng.wait_ge(s_adp, pool_sums(2 * tile + 2))

    def ada_slot(tile):
        if tile < ADA_EARLY:
            return wraw[:, tile % NR].rearrange("p a b -> p (a b)"), s_w[tile % NR], 16 * (tile // NR + 1)
        n = tile - ADA_EARLY
        if n % 3 < 2:
            return wraw[:, 2 + n % 3].rearrange("p a b -> p (a b)"), s_w[2 + n % 3], 16 * (USES_ADA + n // 3 + 1)
        return flat(PR[:]), s_wx, 16 * (n // 3 + 1)

    def col(name, i=0, n=1):
        a = COLS[name][0] + i
        return cols[:, a:a + n]

    s_x1s = sem("x1_stored")
    s_dt, s_dtp, s_rows1, s_tri = sem("dt_step"), sem("dt_projected"), sem("rows_loaded"), sem("triangles")
    s_aa, s_cum = sem("a_split"), sem("running_sums")
    s_dtt = sem("dt_evacuated")
    s_pc, s_pl = sem("tile_ctx_projected"), sem("tile_lat_projected")
    s_cmc, s_cml = sem("conv_mid_ctx"), sem("conv_mid_lat")
    s_cvc, s_cvl, s_cth, s_u = sem("conv_ctx"), sem("conv_lat"), sem("conv_tanh"), sem("conv_done")
    s_gp, s_gpa = sem("group_columns"), sem("group_a")
    s_tx, s_txe, s_txh, s_txl = sem("tokens_transposed"), sem("tokens_out"), sem("tokens_hi"), sem("tokens_lo")
    s_bfh, s_bfl = sem("bc_hi"), sem("bc_lo")
    s_tz, s_sz = sem("z_tanh"), sem("z_silu")
    s_xw, s_xwh, s_xwl = sem("x_weighted"), sem("x_weighted_hi"), sem("x_weighted_lo")
    s_st, s_hd, s_hc, s_Hh, s_Hl = (sem("state_added"), sem("state_decayed"), sem("state_new"), sem("state_hi"),
                                    sem("state_lo"))
    s_r, s_e, s_ed, s_wm, s_m, s_mh, s_ml = (sem("log_decays"), sem("decays"), sem("decays_dt"), sem("decays_summed"),
                                             sem("cb_decayed"), sem("cb_decayed_hi"), sem("cb_decayed_lo"))
    s_yd, s_y1, s_y2, s_y3, s_yy = sem("y_chunk"), sem("y_off_scaled"), sem("y_diag_d"), sem("y_off_sum"), sem("y_sum")
    s_xD, s_yg, s_yq, s_yv, s_yr, s_yn = (sem("x_d"), sem("y_gated1"), sem("y_squares"), sem("y_variance"),
                                          sem("y_rstd"), sem("y_normed"))
    s_yt, s_yte, s_y1st = sem("y_transposed"), sem("y_out"), sem("y1_stored")
    s_y1ld = [sem(f"y1_loaded{i}") for i in range(2)]
    s_dg1, s_gr1, s_gre1, s_x2 = sem("gate1_diag"), sem("gate1_rows"), sem("gate1_rows_out"), sem("x1_reloaded")
    s_zc, s_cv1, s_cv2, s_btl, s_nh = (sem("z_weight_used"), sem("conv_ctx_step"), sem("conv_lat_step"),
                                       sem("b_tokens_lo"), sem("halved_columns"))
    s_cb, s_yof = sem("cb_done"), sem("y_off_done")
    s_ny, s_gn = sem("dt_correction"), sem("group_norm_columns")
    dt_x, dt_nx, dt_e, dt_u, dt_l, dt_a = (
        x1flat[:, UEND + i * TT * 2 * SSM_HEADS:UEND + (i + 1) * TT * 2 * SSM_HEADS].rearrange(
            "p (t h) -> p t h", t=TT) for i in range(6))
    ybank = (psS[:, 0:512], psS[:, 512:1024])

    def tap(j, i):
        return gtap[:, j, i:i + 1]

    def ssm_w(q):
        return W_SSM + q

    def bcast2(ap, n):
        return ap.unsqueeze(2).broadcast_to([P, n, 2])

    block = keep.enter_context(nc.Block())

    @block.sync
    def _(sp):
        for v in range(2):
            sp.dma_start(csilu[:, v], io["cvec"][v].partition_broadcast(P)).then_inc(s_small, 16)
        sp.dma_start(cols[:], io["cols"]).then_inc(s_small, 16)
        for t in range(NR):
            sp.dma_start(wraw[:, t], io["w_ada"][0, t]).then_inc(s_w[t], 16)
        for t in range(TT):
            sp.dma_start(X0[:, t, :], io["xc"][t]).then_inc(s_x[t], 16)
        for t in range(NR, ADA_EARLY):
            tile_summed(sp, t - NR)
            sp.dma_start(wraw[:, t % NR], io["w_ada"][0, t]).then_inc(s_w[t % NR], 16)
        def w_in_load(u):
            sp.dma_start(wraw[:, u % 2], io["w_in"][u]).then_inc(s_w[u % 2], 16)

        for u in range(2):
            tile_summed(sp, ADA_EARLY - NR + u)
            w_in_load(u)
        sp.wait_ge(s_hl, KT)
        sp.dma_start(costab[:], io["cos"]).then_inc(s_tab, 16)
        sp.dma_start(sintab[:], io["sin"]).then_inc(s_tab, 16)
        sp.dma_start(rowt[:], io["rows"][ROWS["sink"][0]:ROWS["sink"][1]].partition_broadcast(P)).then_inc(s_tab, 16)

        def late_load(n):
            if n < 2:
                tile_summed(sp, ADA_EARLY - 2 + n)
            elif n >= 3:
                tile_summed(sp, ADA_EARLY + n - 3)
            place, loaded, _ = ada_slot(ADA_EARLY + n)
            sp.dma_start(place, io["w_ada_late"][n].rearrange("p a b -> p (a b)")).then_inc(loaded, 16)

        for n in range(3):
            late_load(n)
        for g in range(GROUPS + 1):
            first, last = (LATE_START[g - 1] + 3, min(LATE_START[g] + 3, ADA_LATE)) if g else (3, LATE_AHEAD + 3)
            cut = first + (LATE_SHARE[g - 1][0] if g else 0)
            first = min(first, last)
            cut = (min(cut, last), min(cut + 2, last), last)
            for n in range(first, cut[0]):
                late_load(n)
            for c in range(2):
                u = 2 * g + 2 + c
                if u < 2 * GROUPS + 2:
                    sp.wait_ge(s_wlo, u - 1)
                    w_in_load(u)
                for n in range(cut[c], cut[c + 1]):
                    late_load(n)

        def head_loads(j):
            for c in range(2):
                sp.wait_ge(s_wlo, W_HEAD0 + 2 * (j - 1) + c + 1)
                sp.dma_start(wraw[:, c], io["w_in"][NW_KV + 2 * j + c]).then_inc(s_w[c], 16)

        def y_store(j, par):
            sp.wait_ge(s_y, 3 * j + 3)
            sp.wait_ge(s_yst, 16 * j + STORED)
            sp.dma_start(io["y_spill"][j], Yst[:, par, :]).then_inc(s_yst, 16)

        def modulation_load(j, par):
            if isinstance(j, int) and j < 2:
                tile_summed(sp, ADA_EARLY + ADA_LATE - 1)
            else:
                sp.wait_ge(s_adp, POOL_LATE + 2 * (j - 1))
            sp.dma_start(wraw[:, 2 + par], io["w_ada_late"][ADA_LATE + j]).then_inc(s_w[2 + par], 16)

        head_loads(1)
        modulation_load(0, 0)
        modulation_load(1, 1)
        with sp.Fori(0, (HEADS - 2) // 2) as i:
            for e in range(2):
                head_loads(2 * i + 2 + e)
                modulation_load(2 * i + 2 + e, e)
                y_store(2 * i + e, e)
        for c in range(2):
            sp.wait_ge(s_wlo, W_OUT0 - 2 + c + 1)
            sp.dma_start(wraw[:, c], io["w_out0"][c]).then_inc(s_w[c], 16)
        for c in range(2, NR):
            sp.wait_ge(s_adp, POOL_LATE + 2 * (HEADS - NR + c) + 2)
            sp.dma_start(wraw[:, c], io["w_out0"][c]).then_inc(s_w[c], 16)
        y_store(HEADS - 2, 0)
        y_store(HEADS - 1, 1)
        sp.wait_ge(s_pv, 3 * HEADS)
        sp.wait_ge(s_y, 3 * HEADS)
        for c in range(NR, 2 * KT):
            if c == KT:
                for t in range(TT):
                    sp.dma_start(X1[:, t, :], io["xc"][t]).then_inc(s_xr, 16)
            sp.wait_ge(s_wlo, W_OUT0 + c - NR + 1)
            sp.dma_start(wraw[:, c % NR], io["w_out0"][c]).then_inc(s_w[c % NR], 16)
        sp.wait_ge(s_wlo, W_OUT0 + 2 * KT)
        sp.dma_start(wraw[:, NR - 1, :, 0:2 * SSM_HEADS], io["w_dt"]).then_inc(s_w[NR - 1], 16)

        def tile_load(q, q3):
            sp.wait_ge(s_wlo, W_SSM + q - 2 if not (isinstance(q, int) and q < 3) else W_OUT0 + 2 * KT - 3 + q)
            sp.dma_start(wraw[:, q3], io["w_ssm"][q]).then_inc(s_w[q3], 16)

        tile_load(0, 0)
        tile_load(1, 1)
        sp.wait_ge(s_res, 2 * TT)
        for t in range(LT):
            sp.dma_start(io["x1_spill"][t], X1[:, CT + t, :]).then_inc(s_x1s, 16)
        tile_load(2, 2)
        sp.wait_ge(s_hl, KT + KT)
        sp.dma_start(rows1[:], io["rows"][8:NROWS].partition_broadcast(P)).then_inc(s_rows1, 16)
        tile_load(3, 0)

        def group_loads(g, last):
            for c in range(2 if last else 6):
                tile_load(6 * g + 4 + c, (4 + c) % 3)

        def y1_store(g):
            sp.wait_ge(s_yte, LT * (g + 1))
            sp.wait_ge(s_y1st, 16 * g + 16)
            sp.dma_start(io["y1_spill"][g], YT[:]).then_inc(s_y1st, 16)

        group_loads(0, False)
        with sp.Fori(0, SSM_GROUPS - 2) as g:
            group_loads(g + 1, False)
            y1_store(g)
        group_loads(SSM_GROUPS - 1, True)
        y1_store(SSM_GROUPS - 2)

        def out1_load(c):
            if c < NR - 1:
                sp.wait_ge(s_wlo, W_OUT1 - 2 + c)
            elif c == NR - 1:
                sp.wait_ge(s_wlo, W_DT + 1)
            else:
                sp.wait_ge(s_wlo, W_OUT1 + c - NR + 1)
            sp.dma_start(wraw[:, c % NR], io["w_out1"][c]).then_inc(s_w[c % NR], 16)

        for c in range(NR):
            out1_load(c)
        y1_store(SSM_GROUPS - 1)
        sp.wait_ge(s_y1st, 16 * SSM_GROUPS + 16)
        for t in range(LT):
            sp.dma_start(X2[:, t, :], io["x1_spill"][t]).then_inc(s_x2, 16)
        for c in range(NR, 2 * KT):
            out1_load(c)
        for t in range(LT):
            sp.wait_ge(s_res, 2 * TT + 2 * t + 2)
            sp.dma_start(io["out"][t], X2[:, t, :]).then_inc(s_out, 16)
        sp.wait_ge(s_out, 16 * LT)

    def window(b, banded):
        if b < CT:
            lo = hi = 0
        elif banded:
            lo, hi = max(0, b - CT - 1), min(LT, b - CT + 2)
        else:
            lo, hi = 0, LT
        return lo, hi, SEQ - (hi - lo) * P

    def due(s, light, heavy):
        for hs in range(GROUPS):
            if s == hs * BLOCKS + (heavy if hs == GROUPS - 1 else light):
                return hs
        return None

    OUT_TILES = (TT, LT)
    OUT_HALF, OUT_YO, OUT_WUSED = (0, 2 * TT), (0, TT), (0, 2 * KT - 3)
    OUT_VAR, OUT_RSTD, OUT_RES = (1, TT + 4), (1, TT + 3), (0, 2 * TT)
    NORM_BATCHES = ((0, 4), (4, TT))

    def chunk_done(eng, layer, c):
        if c in (KT - 1, 2 * KT - 2, 2 * KT - 1):
            eng.wait_ge(s_half, OUT_HALF[layer] + OUT_TILES[layer] * (c // KT + 1))
        else:
            eng.wait_ge(s_wused, OUT_WUSED[layer] + c - c // KT + 1)

    def lat(u, i):
        return u if i == 3 else u[:, CTX:TOK]

    def free_hi_lo(eng, w, par, tile):
        if isinstance(w, int) and w < 2:
            return
        if isinstance(w, int) and W_DT + 2 > w >= W_OUT0 + 2:
            chunk_done(eng, 0, w - 2 - W_OUT0)
        else:
            eng.wait_ge((s_ql, s_gl)[par], tile)
    @block.scalar
    def _(act):
        def weight_hi(tile, par, slot, use):
            w = 2 * tile + par
            act.wait_ge(s_w[slot], 16 * use)
            free_hi_lo(act, w, par, tile)
            A_.activation(whi[:, par], wraw[:, slot], ACT.Copy).then_inc(s_whi, 1)

        def product_sums(j0, j1):
            for j in range(j0, j1):
                n = 3 * j + 2
                act.wait_ge(s_adp, j + 1)
                A_.activation(products[j % 2], products[j % 2], ACT.Copy, scale=0.5,
                              accum_out=mod[:, n // 2, n % 2:n % 2 + 1]).then_inc(s_ads, 1)

        def late_sums(tile0, tile1):
            product_sums(pool_sums(2 * (ADA_EARLY + tile0)), pool_sums(2 * (ADA_EARLY + tile1)))

        act.wait_ge(s_small, 48)
        A_.activation(cth[:], csilu[:], ACT.Tanh, scale=0.5).then_inc(s_c, 1)
        for t in range(TT):
            act.wait_ge(s_x[t], 16)
            if t:
                act.wait_ge(s_ssq, t)
            A_.activation(junk0[:], X0[:, t, :], ACT.Square, accum_out=ssq[:, 0, t:t + 1]).then_inc(s_ssq, 1)
            if t >= TT - 3:
                product_sums(t - TT + 3, t - TT + 4)
        product_sums(3, pool_sums(ADA_EARLY + 4))
        act.wait_ge(s_rstd, 1)
        for t in range(TT):
            A_.activation(X0[:, t, :], X0[:, t, :], ACT.Copy, scale=rstd[:, 0, t:t + 1]).then_inc(s_xn, 1)
        product_sums(pool_sums(ADA_EARLY + 4), pool_sums(2 * ADA_EARLY))
        act.wait_ge(s_gain, 1)
        for k in range(KT):
            act.wait_ge(s_xt, k + 1)
            if k >= 2:
                act.wait_ge(s_hl, k - 1)
            ps = (psS, psT)[k % 2]
            A_.activation(HS0[:, k % 2, 0:CTX], ps[:, 0:CTX], ACT.Identity, bias=mod[:, k, 1:2],
                          scale=gain[:, 0, k, 1:2])
            A_.activation(HS0[:, k % 2, CTX:TOK], ps[:, CTX:TOK], ACT.Identity, bias=mod[:, k, 0:1],
                          scale=gain[:, 0, k, 0:1]).then_inc(s_hs, 1)

        def q_ctx(e, norm, scale):
            act.wait_ge(s_qc, e + 1)
            if not (isinstance(e, int) and e == 0):
                act.wait_ge(s_qlo, e)
            if norm:
                A_.activation(SQ[:, 0:CTX], psC[:, 0:CTX], ACT.Square)
            A_.activation(QR[:, 0:CTX], psC[:, 0:CTX], ACT.Identity, scale=scale).then_inc(s_qcev, 1)

        def q_lat(e, norm, scale):
            act.wait_ge(s_ql, e + 1)
            if norm:
                A_.activation(SQ[:, CTX:TOK], psL[0][:, :], ACT.Square)
            A_.activation(QR[:, CTX:TOK], psL[0][:, :], ACT.Identity, scale=scale).then_inc(s_qlev, 1)

        def q_hi(e, par):
            act.wait_ge(s_rope, e + 1)
            A_.activation(Qhi[:, par, :], QR[:], ACT.Copy).then_inc(s_qhi, 1)

        def gate_ctx(e):
            act.wait_ge(s_gc, e + 1)
            A_.activation(TH[:, 0:CTX], psC[:, 0:CTX], ACT.Tanh, scale=0.5).then_inc(s_thc, 1)

        def gate_lat(e):
            act.wait_ge(s_gl, e + 1)
            A_.activation(TH[:, CTX:TOK], psL[1][:, :], ACT.Tanh, scale=0.5).then_inc(s_thl, 1)

        for w in range(2):
            weight_hi(0, w, w, USES_ADA + 1)
        act.wait_ge(s_hl, KT)
        late_sums(0, LATE_AHEAD)
        for g in range(GROUPS):
            norm = g >= 2
            scale = col("k_norm") if norm else 1.0
            q_ctx(g, norm, scale)
            q_lat(g, norm, scale)
            weight_hi(g + 1, 0, 0, USES_ADA + g + 2)
            cut = LATE_START[g] + LATE_SHARE[g][0]
            act.wait_ge(s_gc, g + 1)
            if g:
                act.wait_ge(s_vt, g)
            A_.activation(TH[:, 0:CTX], psC[:, 0:CTX], ACT.Copy).then_inc(s_thc, 1)
            act.wait_ge(s_gl, g + 1)
            A_.activation(TH[:, CTX:TOK], psL[1][:, :], ACT.Copy).then_inc(s_thl, 1)
            weight_hi(g + 1, 1, 1, USES_ADA + g + 2)
            late_sums(LATE_START[g], cut)
            act.wait_ge(s_vt, g + 1)
            A_.activation(Vhi[:, :, g * P:(g + 1) * P], psT[:, 0:TOK].rearrange("p (t d) -> p t d", t=TT),
                          ACT.Copy).then_inc(s_vhi, 1)
            if norm:
                act.wait_ge(s_kn, g - 1)
            else:
                act.wait_ge(s_rope, g + 1)
            A_.activation(Khi[:, g, :], QR[:], ACT.Copy).then_inc(s_qhi, 1)
            late_sums(cut, LATE_START[g + 1])
        q_ctx(GROUPS, False, 1.0)
        q_lat(GROUPS, False, 1.0)
        gate_ctx(GROUPS)
        gate_lat(GROUPS)
        q_hi(GROUPS, 0)
        for c in range(2):
            weight_hi(W_HEAD0 // 2 + 1, c, c, USES_HEAD0 + 2)

        def attention(r, last):
            for s in range(SLOTS + 3):
                n = SLOTS * r + s
                if (hs := due(s, 6, 8)) is not None and not (last and hs == GROUPS - 1):
                    gate_lat(GROUPS + GROUPS * r + hs + 1)
                if s < SLOTS:
                    hs, b = s // BLOCKS, s % BLOCKS
                    banded, (lo, hi, a) = hs < 2, window(b, hs < 2)
                    act.wait_ge(s_nm, n + 1)
                    if s >= 2:
                        act.wait_ge(s_pt, n - 1)
                        act.wait_ge(s_ri, n - 1)
                    A_.activation(PR[:, s % 2, a:TOK], psS[:, a:TOK], ACT.Exp, bias=nmax[:, s % 2:s % 2 + 1],
                                  scale=SCALE if banded else rq[:, hs % 2, b:b + 1],
                                  accum_out=esum[:, s % 2:s % 2 + 1]).then_inc(s_ex, 1)
                    if banded:
                        A_.activation(esink[:, s % 2:s % 2 + 1], rowt[:, ds(2 * r + hs, 1)], ACT.Exp,
                                      bias=nmax[:, s % 2:s % 2 + 1]).then_inc(s_es, 1)
                if 1 <= s <= SLOTS:
                    pb = (s - 1) % BLOCKS
                    lo, hi, a = window(pb, (s - 1) // BLOCKS < 2)
                    act.wait_ge(s_pt, n)
                    if pb % 2 == 0 and s > 1:
                        act.wait_ge(s_pv, PAIRS * GROUPS * r + (s - 1) // 2)
                    A_.activation(PThi[:, a // P:TT, (pb % 2) * P:(pb % 2 + 1) * P],
                                  psT[:, a:TOK].rearrange("p (t q) -> p t q", q=P), ACT.Copy).then_inc(s_pth, 1)
                if s < SLOTS and s % BLOCKS in (2, 4):
                    hs, v = s // BLOCKS, s % BLOCKS // 2 - 1
                    act.wait_ge(s_adp, POOL_LATE + 2 * GROUPS * r + 2 * hs + v + 1)
                    if hs == 0 and v == 0 and not (isinstance(r, int) and r == 0):
                        act.wait_ge(s_adal, r + 1)
                    A_.activation(product0[:], product0[:], ACT.Copy, scale=0.5,
                                  accum_out=modp[:, hs, v:v + 1]).then_inc(s_ads, 1)
                if (hs := due(s, 2, 2)) is not None and not (last and hs == GROUPS - 1):
                    norm = (hs + 1) % GROUPS >= 2
                    q_ctx(GROUPS + GROUPS * r + hs + 1, norm, col("q_norm") if norm else 1.0)
                if (hs := due(s, 3, 4)) is not None and not (last and hs == GROUPS - 1):
                    norm = (hs + 1) % GROUPS >= 2
                    q_lat(GROUPS + GROUPS * r + hs + 1, norm, col("q_norm") if norm else 1.0)
                if (hs := due(s, 4, 5)) is not None and not (last and hs == GROUPS - 1):
                    gate_ctx(GROUPS + GROUPS * r + hs + 1)
                    q_hi(GROUPS + GROUPS * r + hs + 1, (hs + 1) % 2)
                    weight_hi(W_HEAD0 // 2 + GROUPS * r + hs + 2, 0, 0, USES_HEAD0 + GROUPS * r + hs + 3)
                if (hs := due(s, 7, 8)) is not None and not (last and hs == GROUPS - 1):
                    weight_hi(W_HEAD0 // 2 + GROUPS * r + hs + 2, 1, 1, USES_HEAD0 + GROUPS * r + hs + 3)

        with act.Fori(0, HEADS // GROUPS - 1) as r:
            attention(r, False)
        attention(HEADS // GROUPS - 1, True)

        def y_load(k):
            if k >= 2:
                act.wait_ge(s_yl, k - 1)
            act.wait_ge(s_yst, 16 * (k + 1) + STORED)
            act.dma_start(Yraw[:, k % 2, :], io["y_spill"][k]).then_inc(s_yld[k % 2], 16)

        act.wait_ge(s_y, PAIRS * HEADS)
        act.wait_ge(s_yst, 16 * HEADS + STORED)
        y_load(0)
        y_load(1)
        def out_squares(layer, nh, t, yo, junk):
            n = OUT_HALF[layer] + nh * OUT_TILES[layer] + t
            if nh == 0:
                act.wait_ge(s_yo, OUT_YO[layer] + t + 1)
            else:
                act.wait_ge(s_half, n + 1)
            if nh or t:
                act.wait_ge(s_sq2, n)
            A_.activation(junk[:], yo[:, t, 0:512] if nh == 0 else tok_bank[t], ACT.Square,
                          accum_out=ssq[:, 1 + nh, t:t + 1]).then_inc(s_sq2, 1)

        def x_squares(t):
            act.wait_ge(s_res, 2 * t + 2)
            if t:
                act.wait_ge(s_ssq, TT + t)
            A_.activation(psT[:, :], X1[:, t, :], ACT.Square, accum_out=ssq[:, 0, t:t + 1]).then_inc(s_ssq, 1)

        def out_hi(c):
            weight_hi((W_OUT0 + c) // 2, c % 2, c % NR, USES_OUT0[c % NR] + c // NR + 1)

        for nh in range(2):
            for c in range(KT):
                if 2 <= nh * KT + c and not (nh == 1 and c < 2):
                    out_hi(nh * KT + c)
                if nh == 0:
                    for k in (2 * c, 2 * c + 1):
                        act.wait_ge(s_yld[k % 2], 16 * (k // 2 + 1))
                        A_.activation(Yhi[:, k, :], Yraw[:, k % 2, :], ACT.Copy).then_inc(s_yh, 1)
                        if 1 <= k < HEADS - 1:
                            y_load(k + 1)
                if nh == 0 and c in (5, 7):
                    v = (c - 5) // 2
                    act.wait_ge(s_gr4, KT * (v + 1))
                    A_.activation(grow[:, v, :], psT[:, :], ACT.Copy).then_inc(s_gre, 1)
            if nh == 0:
                out_hi(KT)
                out_hi(KT + 1)
            for t in range(TT):
                out_squares(0, nh, t, Yo, junk1)
                if nh == 1 and t >= 2:
                    x_squares(t - 2)

        x_squares(TT - 2)
        act.wait_ge(s_half, 2 * TT)
        for b, (t0, t1) in enumerate(NORM_BATCHES):
            act.wait_ge(s_rstd, TT + 2 + b)
            for t in range(t0, t1):
                A_.activation(XN[:, t, :], X1[:, t, :], ACT.Copy, scale=rstd[:, 2, t:t + 1]).then_inc(s_xn, 1)
            if b == 0:
                x_squares(TT - 1)
        H2_ = 2 * SSM_HEADS

        def ssm_hi(q, q3, q2):
            act.wait_ge(s_w[q3], 16 * (USES_SSM[q3] + 1) + 16 * q)
            A_.activation(whi[:, q2], wraw[:, q3], ACT.Copy).then_inc(s_whi, 1)

        act.wait_ge(s_w[NR - 1], 16 * (USES_SSM[NR - 1] + 1))
        chunk_done(act, 0, 2 * KT - 2)
        A_.activation(whi[:, 0, :, 0:H2_], wraw[:, NR - 1, :, 0:H2_], ACT.Copy).then_inc(s_whi, 1)
        chunk_done(act, 0, 2 * KT - 1)
        ssm_hi(0, 0, 1)
        act.wait_ge(s_gain, 2)
        for k in range(KT):
            act.wait_ge(s_xt, KT + k + 1)
            if k >= 2:
                act.wait_ge(s_hl, KT + k - 1)
            ps = (psS, psT)[k % 2]
            A_.activation(HS1[:, k % 2, 0:CTX], ps[:, 0:CTX], ACT.Identity, bias=mod[:, ADA + k, 1:2],
                          scale=gain[:, 1, k, 1:2])
            A_.activation(HS1[:, k % 2, CTX:TOK], ps[:, CTX:TOK], ACT.Identity, bias=mod[:, ADA + k, 0:1],
                          scale=gain[:, 1, k, 0:1]).then_inc(s_hs, 1)

        act.wait_ge(s_dtp, 1)
        A_.activation(CTH[0:H2_, 0:CTX], psC[0:H2_, 0:CTX], ACT.Copy)
        A_.activation(CTH[0:H2_, CTX:TOK], psL[0][0:H2_, :], ACT.Copy).then_inc(s_dtt, 1)
        ssm_hi(0, 1, 0)
        act.wait_ge(s_dt, 2)
        A_.activation(dt_e, dt_nx, ACT.Exp).then_inc(s_dt, 1)
        act.wait_ge(s_dt, 4)
        A_.activation(dt_l, dt_u, ACT.Ln).then_inc(s_dt, 1)
        act.wait_ge(s_rows1, 16)
        A_.activation(rows1[:, 0:H2_], rows1[:, 0:H2_], ACT.Exp).then_inc(s_dt, 1)
        def conv_ctx(g, i):
            act.wait_ge(s_pc, 3 * g + i + 1)
            A_.activation(U[i][:, 0:CTX], psC[:, 0:CTX], ACT.Identity, bias=tap(3, i),
                          scale=tap(1, i)).then_inc(s_cmc, 1)

        act.wait_ge(s_aa, 1)
        A_.activation(ahi[:], dt_a, ACT.Copy).then_inc(s_aa, 1)
        act.wait_ge(s_nh, 3)
        conv_ctx(0, 0)
        A_.activation(dt_u, dt_u, ACT.Ln).then_inc(s_dt, 1)
        act.wait_ge(s_cum, 1)
        cF = psL[1][:, 0:TT * H2_].rearrange("p (t h) -> p t h", t=TT)
        cT = psS[:, 0:TT * H2_].rearrange("p (t h) -> p t h", t=TT)
        A_.activation(acu[:], cF, ACT.Copy)
        A_.activation(TAB[:, R_EA:R_EA + LT, :], cF[:, CT:TT, :], ACT.Exp)
        for i in range(STEPS):
            A_.activation(TAB[:, R_DEC + i, 0:SSM_HEADS], cT[:, FWD[i], 0:SSM_HEADS], ACT.Exp)
            last = A_.activation(TAB[:, R_DEC + i, SSM_HEADS:H2_], cT[:, BWD[i], SSM_HEADS:H2_], ACT.Exp)
        last.then_inc(s_cum, 1)
        act.wait_ge(s_cum, 3)
        A_.activation(dt_l, dt_nx, ACT.Exp).then_inc(s_cum, 1)

        def conv_lat(g, i):
            act.wait_ge(s_pl, 4 * g + i + 1)
            A_.activation(lat(U[i], i), psL[i % 2][:, :], ACT.Identity, bias=tap(3, i),
                          scale=tap(1, i)).then_inc(s_cml, 1)

        def conv_tanh(g, i, first=False):
            act.wait_ge(s_cvl, 4 * g + i + 1)
            act.wait_ge(s_cvc, 3 * g + min(i, 2) + 1)
            if not first:
                act.wait_ge(s_u, 4 * g + i)
            A_.activation(CTH[:, 0:SEQ if i == 3 else TOK], U[i], ACT.Tanh).then_inc(s_cth, 1)

        for i in range(4):
            if 0 < i < 3:
                conv_ctx(0, i)
            conv_lat(0, i)
            if i < 2:
                ssm_hi(0 if i == 0 else 1, (2 + i) % 3, (1 + i) % 2)
            elif i == 2:
                ssm_hi(1, 1, 1)
            else:
                ssm_hi(1, 2, 0)
            conv_tanh(0, i, first=i == 0)

        def squares(g, c):
            act.wait_ge(s_yg, LT * g + c + 1)
            A_.activation(y1[:, 0:GW], yg, ACT.Square, accum_out=yss[:, 0:1]).then_inc(s_yq, 1)

        def y_norm(g, c):
            act.wait_ge(s_yr, LT * g + c + 1)
            A_.activation(ynm[:], yg, ACT.Copy, scale=yrs[:, 0:1]).then_inc(s_yn, 1)

        def y_out(g, c):
            act.wait_ge(s_yt, LT * g + c + 1)
            if c == 0:
                act.wait_ge(s_gn, g + 1)
                act.wait_ge(s_y1st, 16 * g + 16)
            for i in range(2):
                last = A_.activation(YT[:, i, c * P:(c + 1) * P], psV[:, i * P:(i + 1) * P], ACT.Copy,
                                     scale=gnorm[:, i:i + 1])
            last.then_inc(s_yte, 1)

        def decays(g, c):
            act.wait_ge(s_r, LT * g + c + 1)
            if c:
                act.wait_ge(s_wm, LT * g + c)
            for d in range(DIRS):
                for h in range(GH):
                    x = slice((d * GH + h) * P, (d * GH + h + 1) * P)
                    last = A_.activation(E[:, x], psT[:, x], ACT.Exp, bias=GP[:, R_LOG + c, d, h:h + 1])
            last.then_inc(s_e, 1)

        def weighted_hi(g, i):
            act.wait_ge(s_xw, STEPS * g + i + 1)
            A_.activation(xwhi[:, i % 2], xw[:, i % 2], ACT.Copy).then_inc(s_xwh, 1)

        def cb_hi(g, c):
            act.wait_ge(s_m, LT * g + c + 1)
            if c:
                act.wait_ge(s_yd, LT * g + c)
            A_.activation(Mhi[:], Mf[:], ACT.Copy).then_inc(s_mh, 1)

        def ssd(g, last):
            G = g + 1
            ps = psT[:, 0:TOK].rearrange("p (t d) -> p t d", t=TT)
            for i in range(3):
                act.wait_ge(s_tx, 3 * g + i + 1)
                A_.activation(xt[:, :, i * P:(i + 1) * P] if i < 2 else bthi[:], ps, ACT.Copy).then_inc(s_txe, 1)
            act.wait_ge(s_txe, 3 * g + 2)
            A_.activation(xthi[:], xt[:, CT:TT, :], ACT.Copy).then_inc(s_txh, 1)
            weighted_hi(g, 0)
            weighted_hi(g, 1)
            act.wait_ge(s_zc, 2 * g + 1)
            if not last:
                ssm_hi(2 * g + 2, 0, 1)
            act.wait_ge(s_u, 4 * g + 4)
            A_.activation(bfhi[:, 0, :], U[2][:, CTX:TOK], ACT.Copy)
            A_.activation(bfhi[:, 1, :], U[3], ACT.Copy).then_inc(s_bfh, 1)
            act.wait_ge(s_zc, 2 * g + 2)
            A_.activation(thz[:], psS[:, :], ACT.Tanh, scale=0.5).then_inc(s_tz, 1)
            act.wait_ge(s_gp, g + 1)
            decays(g, 0)
            for i in range(STEPS):
                if i + 2 < STEPS:
                    act.wait_ge(s_st, STEPS * g + i + 1)
                    weighted_hi(g, i + 2)
                if i:
                    act.wait_ge(s_hc, STEPS * g + i + 1)
                    A_.activation(Hhi[:, i - 1, 0, :], hcur[:, 0:GW], ACT.Copy)
                    A_.activation(Hhi[:, LT - i, 1, :], hcur[:, GW:2 * GW], ACT.Copy).then_inc(s_Hh, 1)
                if i == 0 and not last:
                    ssm_hi(2 * g + 2, 1, 0)
                elif i == 0:
                    for c in range(2):
                        act.wait_ge(s_w[c], 16 * (USES_OUT1[c] + 1))
                        A_.activation(whi[:, (W_OUT1 + c) % 2], wraw[:, c], ACT.Copy).then_inc(s_whi, 1)
                if i == 2 and not last:
                    act.wait_ge(s_nh, G + 3)
                    conv_ctx(G, 0)
                if i == 2:
                    cb_hi(g, 0)
                if i == 3:
                    decays(g, 1)
                if i == 4 and not last:
                    conv_lat(G, 0)
            if not last:
                conv_ctx(G, 1)
                conv_tanh(G, 0)
                ssm_hi(2 * g + 2, 2, 1)
            for c in range(LT):
                if c < LT - 1:
                    cb_hi(g, c + 1)
                if c < LT - 2:
                    decays(g, c + 2)
                if c == 1 and not last:
                    conv_lat(G, 1)
                    ssm_hi(2 * g + 3, 0, 0)
                if c == 2 and not last:
                    conv_ctx(G, 2)
                    conv_tanh(G, 1)
                if c == 3 and not last:
                    conv_lat(G, 2)
                    ssm_hi(2 * g + 3, 1, 1)
                if c:
                    y_out(g, c - 1)
                squares(g, c)
                y_norm(g, c)
            if not last:
                conv_tanh(G, 2)
                conv_lat(G, 3)
            y_out(g, LT - 1)
            if not last:
                ssm_hi(2 * g + 3, 2, 0)
                conv_tanh(G, 3)

        with act.Fori(0, SSM_GROUPS - 1) as g:
            ssd(g, False)
        ssd(SSM_GROUPS - 1, True)

        def y1_load(k):
            if k >= 2:
                act.wait_ge(s_yl, HEADS + k - 1)
            act.wait_ge(s_y1st, 16 * (k // 2 + 1) + 16)
            act.dma_start(Y1raw[:, k % 2, :], io["y1_spill"][k // 2, :, k % 2, :]).then_inc(s_y1ld[k % 2], 16)

        def out1_hi(i):
            act.wait_ge(s_w[i % NR], 16 * (USES_OUT1[i % NR] + i // NR + 1))
            chunk_done(act, 1, i - 2)
            A_.activation(whi[:, (W_OUT1 + i) % 2], wraw[:, i % NR], ACT.Copy).then_inc(s_whi, 1)

        act.wait_ge(s_y1st, 16 * SSM_GROUPS + 16)
        y1_load(0)
        y1_load(1)
        for nh in range(2):
            for c in range(KT):
                i = nh * KT + c
                if i >= 2 and not (nh == 1 and c < 2):
                    out1_hi(i)
                if nh == 0:
                    for k in (2 * c, 2 * c + 1):
                        act.wait_ge(s_y1ld[k % 2], 16 * (k // 2 + 1))
                        A_.activation(Y1hi[:, k, :], Y1raw[:, k % 2, :], ACT.Copy).then_inc(s_yh, 1)
                        if 1 <= k < HEADS - 1:
                            y1_load(k + 1)
                if nh == 0 and c == 5:
                    act.wait_ge(s_gr1, KT)
                    A_.activation(grow1[:], psT[:, :], ACT.Copy).then_inc(s_gre1, 1)
            if nh == 0:
                out1_hi(KT)
                out1_hi(KT + 1)
            for t in range(LT):
                out_squares(1, nh, t, Yo1, junk3)

    @block.vector
    def _(dve):
        dve.wait_ge(s_c, 1)
        V_.scalar_tensor_tensor(csilu[:], cth[:], 1.0, csilu[:], ALU.add, ALU.mult).then_inc(s_c, 1)

        def modulation(tile):
            for v in range(2):
                n = 2 * tile + v
                if n % 3 == 2:
                    continue
                place, loaded, count = ada_slot(tile)
                dve.wait_ge(loaded, count)
                if n:
                    dve.wait_ge(s_ada, dve_sums(n))
                V_.tensor_tensor_reduce(out=product, in0=place, in1=csilu[:, v, :], scale=0.5, scalar=0.0,
                                        op0=ALU.mult, op1=ALU.add, accum_out=mod[:, tile, v:v + 1]).then_inc(s_ada, 1)

        dve.wait_ge(s_c, 2)
        for t in range(ADA_EARLY):
            if t == ADA_EARLY // 2:
                dve.wait_ge(s_ssq, TT)
                V_.tensor_scalar(vvar[:, 0, 0:TT], ssq[:, 0, 0:TT], 1.0 / D_MODEL, EPS, ALU.mult,
                                 ALU.add).then_inc(s_var, 1)
            modulation(t)
        dve.wait_ge(s_ada, dve_sums(2 * ADA_EARLY))
        dve.wait_ge(s_ads, pool_sums(2 * ADA_EARLY))
        V_.tensor_tensor(mod[:, 0:ADA_EARLY, :], mod[:, 0:ADA_EARLY, :],
                         bcast2(col("b_ada", 0, ADA_EARLY), ADA_EARLY), ALU.add).then_inc(s_mod, 1)
        dve.wait_ge(s_mod, 1)
        V_.scalar_tensor_tensor(gain[:, 0], mod[:, KT:2 * KT, :], 1.0, bcast2(col("pre", 0, KT), KT),
                                ALU.add, ALU.mult).then_inc(s_gain, 1)
        for k in range(KT):
            dve.wait_ge(s_hs, k + 1)
            V_.tensor_copy(hhi[:, k, :], HS0[:, k % 2, :]).then_inc(s_hh, 1)
            dve.wait_ge(s_hh, k + 1)
            V_.tensor_tensor(hlo[:, k, :], HS0[:, k % 2, :], f(hhi[:, k, :]), ALU.subtract).then_inc(s_hl, 1)

        H2 = P // 2

        def rope(e):
            dve.wait_ge(s_qlev, e + 1)
            x = QR[:, CTX:TOK]
            V_.tensor_tensor(T1[:], x, costab[:], ALU.mult).then_inc(s_t1, 1)
            V_.tensor_tensor(T2[0:H2, :], x[H2:P, :], sintab[H2:P, :], ALU.mult)
            V_.tensor_tensor(T2[H2:P, :], x[0:H2, :], sintab[0:H2, :], ALU.mult).then_inc(s_t2, 1)
            dve.wait_ge(s_t1, e + 1)
            dve.wait_ge(s_t2, e + 1)
            V_.tensor_tensor(x, T1[:], T2[:], ALU.add).then_inc(s_rope, 1)

        def variance(u, factor=1.0):
            dve.wait_ge(s_nq, u + 1)
            V_.tensor_scalar(vq[:], psV[:, 0:TT], factor / P, factor * EPS, ALU.mult,
                             ALU.add).then_inc(s_vq, 1)

        def gate(e, par, part):
            if part == 0:
                dve.wait_ge(s_thc, e + 1)
                V_.scalar_tensor_tensor(SG[:, par, 0:CTX], TH[:, 0:CTX], 1.0, psC[:, 0:CTX], ALU.add,
                                        ALU.mult).then_inc(s_sgc, 1)
            else:
                dve.wait_ge(s_thl, e + 1)
                V_.scalar_tensor_tensor(SG[:, par, CTX:TOK], TH[:, CTX:TOK], 1.0, psL[1][:, :], ALU.add,
                                        ALU.mult).then_inc(s_sgl, 1)

        dve.wait_ge(s_tab, 48)
        V_.tensor_scalar(nsink[:], rowt[:], -1.0, None, ALU.mult).then_inc(s_nsink, 1)
        def late_modulation(n0, n1):
            for n in range(n0, n1):
                modulation(ADA_EARLY + n)

        late_modulation(0, LATE_AHEAD)
        for g in range(GROUPS):
            vals = slice(g * P, (g + 1) * P)
            rope(g)
            cut = LATE_START[g] + LATE_SHARE[g][0]
            late_modulation(LATE_START[g], cut)
            if g >= 2:
                variance(g - 2)
                dve.wait_ge(s_rq, g - 1)
                for t in range(TT):
                    last = V_.tensor_scalar(dgk[:, t, :], ident[:], rq[:, g % 2, t:t + 1], None, ALU.mult)
                last.then_inc(s_dgk, 1)
            dve.wait_ge(s_vhi, g + 1)
            V_.tensor_tensor(Vlo[:, :, vals], psT[:, 0:TOK].rearrange("p (t d) -> p t d", t=TT),
                             f(Vhi[:, :, vals]), ALU.subtract).then_inc(s_vlo, 1)
            if g >= 2:
                dve.wait_ge(s_rkb, g - 1)
                dve.wait_ge(s_rope, g + 1)
                V_.tensor_tensor(QR[:], QR[:], psT[:, 0:TOK], ALU.mult).then_inc(s_kn, 1)
            dve.wait_ge(s_qhi, g + 1)
            V_.tensor_tensor(Klo[:, g, :], QR[:], f(Khi[:, g, :]), ALU.subtract).then_inc(s_qlo, 1)
            late_modulation(cut, LATE_START[g + 1])
        dve.wait_ge(s_ada, dve_sums(2 * (ADA_EARLY + ADA_LATE)))
        dve.wait_ge(s_ads, POOL_LATE)
        V_.tensor_tensor(mod[:, ADA_EARLY:ADA_EARLY + ADA_LATE, :], mod[:, ADA_EARLY:ADA_EARLY + ADA_LATE, :],
                         bcast2(col("b_ada", ADA_EARLY, ADA_LATE), ADA_LATE), ALU.add).then_inc(s_adal, 1)
        rope(GROUPS)
        gate(GROUPS, 0, 0)
        gate(GROUPS, 0, 1)

        def attention(r, last):
            for s in range(SLOTS + 3):
                n = SLOTS * r + s
                skip = lambda hs: hs is None or (last and hs == GROUPS - 1)
                tile = lambda hs: GROUPS + GROUPS * r + hs + 1
                if not skip(hs := due(s, 5, 6)):
                    gate(tile(hs), (hs + 1) % 2, 0)
                if not skip(hs := due(s, 6, 8)):
                    gate(tile(hs), (hs + 1) % 2, 1)
                if s < SLOTS:
                    hs, b = s // BLOCKS, s % BLOCKS
                    banded, (lo, hi, a) = hs < 2, window(b, hs < 2)
                    p = slice(s % 2, s % 2 + 1)
                    dve.wait_ge(s_sc, n + 1)
                    V_.reduce_max(smax[:, p], psS[:, a:TOK], AX.X).then_inc(s_mx, 1)
                    dve.wait_ge(s_mx, n + 1)
                    if banded:
                        V_.tensor_scalar(nmax[:, p], smax[:, p], -SCALE, nsink[:, ds(2 * r + hs, 1)], ALU.mult,
                                         ALU.min).then_inc(s_nm, 1)
                    else:
                        if b == 0:
                            dve.wait_ge(s_rq, 2 * r + hs + 1)
                        V_.tensor_scalar(nmax[:, p], smax[:, p], rq[:, hs % 2, b:b + 1], -1.0, ALU.mult,
                                         ALU.mult).then_inc(s_nm, 1)
                if s < SLOTS:
                    hs, b = s // BLOCKS, s % BLOCKS
                    if hs < 2:
                        dve.wait_ge(s_es, 2 * BLOCKS * r + s + 1)
                        dve.wait_ge(s_ex, n + 1)
                        V_.tensor_tensor(eall[:, p], esum[:, p], esink[:, p], ALU.add).then_inc(s_ea, 1)
                        dve.wait_ge(s_ea, 2 * BLOCKS * r + s + 1)
                        V_.reciprocal(rinv[:, p], eall[:, p]).then_inc(s_ri, 1)
                    else:
                        dve.wait_ge(s_ex, n + 1)
                        V_.reciprocal(rinv[:, p], esum[:, p]).then_inc(s_ri, 1)
                    dve.wait_ge(s_ri, n + 1)
                    V_.tensor_scalar(PR[:, s % 2, a:TOK], PR[:, s % 2, a:TOK], rinv[:, p], 0.5, ALU.mult,
                                     ALU.mult).then_inc(s_pn, 1)
                if not skip(hs := due(s, 4, 5)):
                    rope(tile(hs))
                if 1 <= s <= SLOTS:
                    pb = (s - 1) % BLOCKS
                    lo, hi, a = window(pb, (s - 1) // BLOCKS < 2)
                    q = slice((pb % 2) * P, (pb % 2 + 1) * P)
                    dve.wait_ge(s_pth, n)
                    V_.tensor_tensor(PTlo[:, a // P:TT, q], psT[:, a:TOK].rearrange("p (t q) -> p t q", q=P),
                                     f(PThi[:, a // P:TT, q]), ALU.subtract).then_inc(s_ptl, 1)
                if s >= 3 and s % 2:
                    pair = (s - 3) // 2
                    hs, q = pair // PAIRS, pair % PAIRS
                    dve.wait_ge(s_pv, PAIRS * GROUPS * r + pair + 1)
                    if q == 0:
                        dve.wait_ge(s_yst, 16 * (GROUPS * r + hs + 1))
                    V_.tensor_tensor(Yst[:, hs % 2, q * 2 * P:(q + 1) * 2 * P], psV[:, 0:2 * P],
                                     SG[:, hs % 2, q * 2 * P:(q + 1) * 2 * P], ALU.mult).then_inc(s_y, 1)
                if not skip(hs := due(s, 4, 5)) and (hs + 1) % GROUPS >= 2:
                    variance(2 * r + hs + 1, P)
                if s == SLOTS + 1:
                    dve.wait_ge(s_ads, POOL_LATE + 2 * GROUPS * (r + 1))
                    at = ADA_EARLY + ADA_LATE + GROUPS * r
                    V_.tensor_tensor(mod[:, ds(at, GROUPS), :], modp[:],
                                     bcast2(cols[:, ds(at + COLS["b_ada"][0], GROUPS)], GROUPS), ALU.add).then_inc(s_adal, 1)

        with dve.Fori(0, HEADS // GROUPS - 1) as r:
            attention(r, False)
        attention(HEADS // GROUPS - 1, True)

        def gate_columns(layer):
            V_.tensor_tensor(gcolx[:, layer], mod[:, layer * ADA + 2 * KT:layer * ADA + 3 * KT, :],
                             bcast2(col("post", layer * KT, KT), KT), ALU.mult).then_inc(s_gate, 1)

        def gate_diag(layer, v, first):
            for k in range(KT):
                u = first + v * KT + k
                if u >= KT:
                    dve.wait_ge(s_gr4, u - KT + 1)
                V_.tensor_scalar(dg[:, k, :], ident[:], gcolx[:, layer, k, v:v + 1], None,
                                 ALU.mult).then_inc(s_dg, 1)

        dve.wait_ge(s_adal, 1 + HEADS // GROUPS)
        gate_columns(0)
        dve.wait_ge(s_gate, 1)
        for k in range(HEADS):
            dve.wait_ge(s_yh, k + 1)
            V_.tensor_tensor(Ylo[:, k, :], Yraw[:, k % 2, :], f(Yhi[:, k, :]), ALU.subtract).then_inc(s_yl, 1)
            if k in (7, 11):
                gate_diag(0, (k - 7) // 4, 0)
        def out_first_half(layer, yo):
            n = OUT_TILES[layer]
            for t in range(n):
                dve.wait_ge(s_half, OUT_HALF[layer] + t + 1)
                V_.tensor_copy(yo[:, t, 0:512], tok_bank[t]).then_inc(s_yo, 1)
            dve.wait_ge(s_sq2, OUT_HALF[layer] + n)
            V_.tensor_scalar(ssq[:, 3, 0:n], ssq[:, 1, 0:n], 1.0 / D_MODEL, EPS, ALU.mult, ALU.add).then_inc(s_var, 1)
            dve.wait_ge(s_var, OUT_VAR[layer] + 1)

        def out_variance(layer, t):
            dve.wait_ge(s_sq2, OUT_HALF[layer] + OUT_TILES[layer] + t + 1)
            V_.scalar_tensor_tensor(vvar[:, 1 + 2 * layer, t:t + 1], ssq[:, 2, t:t + 1], 1.0 / D_MODEL, ssq[:, 3, t:t + 1],
                                    ALU.mult, ALU.add).then_inc(s_var, 1)

        def out_scaled(layer, t, yo, gate_row):
            dve.wait_ge(s_rstd, OUT_RSTD[layer] + t + 1)
            r = rstd[:, 1 + 2 * layer, t:t + 1]
            V_.scalar_tensor_tensor(yo[:, t, 0:512], yo[:, t, 0:512], r, gate_row[:, 0:512], ALU.mult, ALU.mult)
            V_.scalar_tensor_tensor(yo[:, t, 512:1024], tok_bank[t], r, gate_row[:, 512:1024], ALU.mult,
                                    ALU.mult).then_inc(s_res, 1)

        def out_added(layer, t, x, yo):
            dve.wait_ge(s_res, OUT_RES[layer] + 2 * t + 1)
            V_.tensor_tensor(x[:, t, :], x[:, t, :], yo[:, t, :], ALU.add).then_inc(s_res, 1)

        def norm_variance(t0, t1):
            dve.wait_ge(s_ssq, TT + t1)
            V_.tensor_scalar(vvar[:, 2, t0:t1], ssq[:, 0, t0:t1], 1.0 / D_MODEL, EPS, ALU.mult, ALU.add).then_inc(s_var, 1)

        out_first_half(0, Yo)
        dve.wait_ge(s_gre, 2)
        dve.wait_ge(s_xr, 16 * TT)
        out_variance(0, 0)
        for t in range(TT):
            out_scaled(0, t, Yo, grow[:, int(t < CT), :])
            if t < TT - 1:
                out_variance(0, t + 1)
            else:
                norm_variance(*NORM_BATCHES[0])
            out_added(0, t, X1, Yo)

        norm_variance(*NORM_BATCHES[1])
        V_.scalar_tensor_tensor(gain[:, 1], mod[:, ADA + KT:ADA + 2 * KT, :], 1.0, bcast2(col("pre", KT, KT), KT),
                                ALU.add, ALU.mult).then_inc(s_gain, 1)
        gate_columns(1)
        for k in range(KT):
            dve.wait_ge(s_hs, KT + k + 1)
            V_.tensor_copy(h1hi[:, k, :], HS1[:, k % 2, :]).then_inc(s_hh, 1)
            dve.wait_ge(s_hh, KT + k + 1)
            V_.tensor_tensor(h1lo[:, k, :], HS1[:, k % 2, :], f(h1hi[:, k, :]), ALU.subtract).then_inc(s_hl, 1)
        dve.wait_ge(s_hl, KT + KT)
        V_.tensor_scalar(convh[:], cols[:, COLS["conv_w"][0]:COLS["conv_b"][1]], 0.5, None, ALU.mult).then_inc(s_nh, 1)
        V_.tensor_scalar(normh[:], col("ssm_norm", 0, 16), 0.5, None, ALU.mult).then_inc(s_nh, 1)
        def group_taps(g):
            at = convh[:].rearrange("p (j b g) -> p j b g", j=4, b=4)
            V_.tensor_copy(gtap[:, :, 0:2], convh[:].rearrange("p (j b) -> p j b", j=4)[:, :, ds(2 * g, 2)])
            V_.tensor_copy(gtap[:, :, 2:4], at[:, :, 2:4, ds(g, 1)].rearrange("p j b g -> p j (b g)")).then_inc(s_nh, 1)

        dve.wait_ge(s_nh, 2)
        group_taps(0)
        H2_ = 2 * SSM_HEADS

        def outer_taps(g, i, u, ps, n, mid, step, done, k):
            dve.wait_ge(mid, k + 1)
            V_.scalar_tensor_tensor(u[:, 1:n], ps[:, 0:n - 1], tap(0, i), u[:, 1:n], ALU.mult, ALU.add).then_inc(step, 1)
            dve.wait_ge(step, k + 1)
            V_.scalar_tensor_tensor(u[:, 0:n - 1], ps[:, 1:n], tap(2, i), u[:, 0:n - 1], ALU.mult,
                                    ALU.add).then_inc(done, 1)

        def taps_ctx(g, i):
            outer_taps(g, i, U[i], psC, CTX, s_cmc, s_cv1, s_cvc, 3 * g + i)

        def taps_lat(g, i):
            outer_taps(g, i, lat(U[i], i), psL[i % 2], SEQ, s_cml, s_cv2, s_cvl, 4 * g + i)

        def silu(g, i):
            dve.wait_ge(s_cth, 4 * g + i + 1)
            V_.scalar_tensor_tensor(U[i], CTH[:, 0:SEQ if i == 3 else TOK], 1.0, U[i], ALU.add, ALU.mult).then_inc(s_u, 1)

        def rows_b(ap):
            return ap.unsqueeze(1).broadcast_to([P, TT, H2_])

        dve.wait_ge(s_rows1, 16)
        dve.wait_ge(s_x1s, 16 * LT)
        dve.wait_ge(s_dtp, 2)
        V_.tensor_tensor(dt_x, psT[:, 0:TT * H2_].rearrange("p (t h) -> p t h", t=TT), rows_b(rows1[:, H2_:2 * H2_]),
                         ALU.add).then_inc(s_dt, 1)
        dve.wait_ge(s_dt, 1)
        V_.scalar_tensor_tensor(dt_nx, dt_x, -1.0, dt_x, ALU.mult, ALU.min).then_inc(s_dt, 1)
        dve.wait_ge(s_dt, 3)
        V_.tensor_scalar(dt_u, dt_e, 1.0, None, ALU.add).then_inc(s_dt, 1)
        dve.wait_ge(s_dt, 5)
        V_.scalar_tensor_tensor(dt_e, dt_u, -1.0, dt_e, ALU.add, ALU.subtract).then_inc(s_ny, 1)
        V_.reciprocal(dt_nx, dt_u).then_inc(s_ny, 1)
        dve.wait_ge(s_ny, 2)
        V_.tensor_tensor(dt_e, dt_e, dt_nx, ALU.mult).then_inc(s_ny, 1)
        dve.wait_ge(s_ny, 3)
        V_.tensor_tensor(dt_l, dt_l, dt_e, ALU.subtract).then_inc(s_ny, 1)
        dve.wait_ge(s_ny, 4)
        V_.scalar_tensor_tensor(dt_x, dt_x, 0.0, dt_l, ALU.max, ALU.add).then_inc(s_ny, 1)
        dve.wait_ge(s_ny, 5)
        dve.wait_ge(s_dt, 6)
        V_.tensor_scalar(dt_u, dt_x, 1e-37, None, ALU.max)
        V_.tensor_copy(TAB[:, R_D, 0:SSM_HEADS], rows1[:, 2 * H2_:2 * H2_ + SSM_HEADS])
        V_.memset(TAB[:, R_D, SSM_HEADS:H2_], 0.0)
        V_.scalar_tensor_tensor(dt_a, dt_x, -1.0, rows_b(rows1[:, 0:H2_]), ALU.mult, ALU.mult).then_inc(s_aa, 1)
        dve.wait_ge(s_aa, 2)
        V_.tensor_tensor(alo[:], dt_a, f(ahi[:]), ALU.subtract).then_inc(s_aa, 1)
        taps_ctx(0, 0)
        dve.wait_ge(s_cum, 2)
        V_.tensor_tensor(dt_nx, psS[:, 0:TT * H2_].rearrange("p (t h) -> p t h", t=TT), acu[:],
                         ALU.subtract).then_inc(s_cum, 1)
        dve.wait_ge(s_dt, 7)
        V_.tensor_tensor(TAB[:, R_LOG:R_LOG + LT, :], dt_u[:, CT:TT, :], acu[:, CT:TT, :], ALU.subtract)
        dve.wait_ge(s_cum, 4)
        for i in range(STEPS):
            V_.tensor_tensor(TAB[:, R_WE + i, 0:SSM_HEADS], dt_l[:, FWD[i], 0:SSM_HEADS], dt_x[:, FWD[i], 0:SSM_HEADS],
                             ALU.mult)
            last = V_.tensor_tensor(TAB[:, R_WE + i, SSM_HEADS:H2_], dt_l[:, BWD[i], SSM_HEADS:H2_],
                                    dt_x[:, BWD[i], SSM_HEADS:H2_], ALU.mult)
        last.then_inc(s_cum, 1)

        for i in range(4):
            if 0 < i < 3:
                taps_ctx(0, i)
            taps_lat(0, i)
            silu(0, i)

        def variance1(g, c):
            dve.wait_ge(s_yq, LT * g + c + 1)
            V_.tensor_scalar(yvv[:, 0:1], yss[:, 0:1], 0.25 / GW, EPS, ALU.mult, ALU.add).then_inc(s_yv, 1)

        def by_head(ap, n):
            return ap.rearrange("p (h x) -> p h x", x=n)

        def per_head(ap, d0, d1, n):
            return ap.rearrange("p d h -> p (d h)")[:, d0 * GH:d1 * GH].unsqueeze(2).broadcast_to([P, (d1 - d0) * GH, n])

        dve.wait_ge(s_cum, 5)

        def weighted_lo(g, i):
            dve.wait_ge(s_xwh, STEPS * g + i + 1)
            V_.tensor_tensor(xwlo[:, i % 2], xw[:, i % 2], f(xwhi[:, i % 2]), ALU.subtract).then_inc(s_xwl, 1)

        def decay_sum(g, c):
            dve.wait_ge(s_e, LT * g + c + 1)
            V_.tensor_tensor(Wm[:], E[:, 0:GH * P], E[:, GH * P:2 * GH * P], ALU.add).then_inc(s_wm, 1)

        def cb_times(g, c):
            dve.wait_ge(s_wm, LT * g + c + 1)
            dve.wait_ge(s_cb, LT * g + c + 1)
            V_.tensor_tensor(by_head(Mf[:], P), by_head(Wm[:], P),
                             ybank[1][:, 0:P].unsqueeze(1).broadcast_to([P, GH, P]), ALU.mult).then_inc(s_m, 1)

        def cb_lo(g, c):
            dve.wait_ge(s_mh, LT * g + c + 1)
            V_.tensor_tensor(Mlo[:], Mf[:], f(Mhi[:]), ALU.subtract).then_inc(s_ml, 1)

        def ssd(g, last):
            G = g + 1
            if not last:
                group_taps(G)
            V_.tensor_copy(GP[:], TAB[:].rearrange("p r (d h) -> p r d h", d=DIRS)[:, :, :, ds(GH * g, GH)]).then_inc(s_gp, 1)
            V_.tensor_copy(aghi[:], f(ahi[:]).rearrange("p t (d h) -> p t d h", d=DIRS)[:, CT:TT, :, ds(GH * g, GH)])
            V_.tensor_copy(aglo[:], f(alo[:]).rearrange("p t (d h) -> p t d h", d=DIRS)[:, CT:TT, :, ds(GH * g, GH)]).then_inc(s_gpa, 1)
            dve.wait_ge(s_txh, g + 1)
            V_.tensor_tensor(xtlo[:], xt[:, CT:TT, :], f(xthi[:]), ALU.subtract).then_inc(s_txl, 1)
            dve.wait_ge(s_txe, 3 * g + 3)
            V_.tensor_tensor(btlo[:], psT[:, 0:TOK].rearrange("p (t d) -> p t d", t=TT), f(bthi[:]), ALU.subtract).then_inc(s_btl, 1)
            weighted_lo(g, 0)
            weighted_lo(g, 1)
            dve.wait_ge(s_bfh, g + 1)
            V_.tensor_tensor(bflo[:, 0, :], U[2][:, CTX:TOK], f(bfhi[:, 0, :]), ALU.subtract)
            V_.tensor_tensor(bflo[:, 1, :], U[3], f(bfhi[:, 1, :]), ALU.subtract).then_inc(s_bfl, 1)
            dve.wait_ge(s_tz, g + 1)
            V_.scalar_tensor_tensor(sz, thz[:], 1.0, psS[:, :], ALU.add, ALU.mult).then_inc(s_sz, 1)
            dve.wait_ge(s_gp, g + 1)
            for i in range(STEPS):
                if i:
                    dve.wait_ge(s_hc, STEPS * g + i)
                    V_.tensor_tensor(by_head(hdec[:], HD), by_head(hcur[:], HD), per_head(GP[:, R_DEC + i], 0, DIRS, HD),
                                     ALU.mult).then_inc(s_hd, 1)
                    dve.wait_ge(s_hd, (STEPS - 1) * g + i)
                dve.wait_ge(s_st, STEPS * g + i + 1)
                if i == 0:
                    V_.tensor_copy(hcur[:], ybank[0]).then_inc(s_hc, 1)
                else:
                    if i > 1:
                        dve.wait_ge(s_Hl, LT * g + i - 1)
                    V_.tensor_tensor(hcur[:], hdec[:], ybank[0], ALU.add).then_inc(s_hc, 1)
                if i + 2 < STEPS:
                    weighted_lo(g, i + 2)
                if i == 0:
                    decay_sum(g, 0)
                    cb_times(g, 0)
                if i == 2:
                    cb_lo(g, 0)
                if i == 3 and not last:
                    taps_ctx(G, 0)
            if not last:
                taps_lat(G, 0)
                taps_ctx(G, 1)
            dve.wait_ge(s_y1st, 16 * g + 16)
            decay_sum(g, 1)
            V_.tensor_copy(gnorm[:], normh[:, ds(2 * g, 2)]).then_inc(s_gn, 1)
            for c in range(LT):
                n = LT * g + c
                dve.wait_ge(s_xD, n + 1)
                dve.wait_ge(s_yd, n + 1)
                V_.tensor_tensor(y2, ybank[1][:, P:P + GW], xD[:, c % 2], ALU.add).then_inc(s_y2, 1)
                dve.wait_ge(s_yof, n + 1)
                V_.tensor_tensor(by_head(y1, HD), by_head(ybank[0], HD), per_head(GP[:, R_EA + c], 0, DIRS, HD),
                                 ALU.mult).then_inc(s_y1, 1)
                if c < LT - 1:
                    cb_times(g, c + 1)
                dve.wait_ge(s_y1, n + 1)
                V_.tensor_tensor(y3, y1[:, 0:GW], y1[:, GW:2 * GW], ALU.add).then_inc(s_y3, 1)
                if c < LT - 1:
                    cb_lo(g, c + 1)
                dve.wait_ge(s_y3, n + 1)
                V_.tensor_tensor(y2, y2, y3, ALU.add).then_inc(s_yy, 1)
                dve.wait_ge(s_yy, n + 1)
                if c:
                    dve.wait_ge(s_yn, n)
                V_.tensor_tensor(yg, y2, sz[:, c * GW:(c + 1) * GW], ALU.mult).then_inc(s_yg, 1)
                if c < LT - 2:
                    decay_sum(g, c + 2)
                variance1(g, c)
                if c == 0 and not last:
                    silu(G, 0)
                if c == 1 and not last:
                    taps_lat(G, 1)
                if c == 2 and not last:
                    silu(G, 1)
                    taps_ctx(G, 2)
            if not last:
                taps_lat(G, 2)
                silu(G, 2)
                taps_lat(G, 3)
                silu(G, 3)

        with dve.Fori(0, SSM_GROUPS - 1) as g:
            ssd(g, False)
        ssd(SSM_GROUPS - 1, True)

        for k in range(HEADS):
            dve.wait_ge(s_yh, HEADS + k + 1)
            V_.tensor_tensor(Y1lo[:, k, :], Y1raw[:, k % 2, :], f(Y1hi[:, k, :]), ALU.subtract).then_inc(s_yl, 1)
            if k == 7:
                for j in range(KT):
                    V_.tensor_scalar(dg1[:, j, :], ident[:], gcolx[:, 1, j, 0:1], None, ALU.mult).then_inc(s_dg1, 1)
        out_first_half(1, Yo1)
        dve.wait_ge(s_gre1, 1)
        dve.wait_ge(s_x2, 16 * LT)
        out_variance(1, 0)
        for t in range(LT):
            out_scaled(1, t, Yo1, grow1[:])
            if t < LT - 1:
                out_variance(1, t + 1)
            out_added(1, t, X2, Yo1)

    @block.gpsimd
    def _(pool):
        G_.memset(half[:], -0.5).then_inc(s_yst, STORED)
        G_.memset(ones[:], 1.0).then_inc(s_const, 1)
        G_.memset(ident[:], 0.0).then_inc(s_const, 1)
        G_.memset(nothing[:], 0.0).then_inc(s_y1st, 16)
        pool.wait_ge(s_const, 2)
        G_.affine_select(out=ident[:], in_=ident[:], compare_op=ALU.not_equal, fill=1.0, base=0,
                         pattern=[[-1, P]], channel_multiplier=1).then_inc(s_const, 1)
        pool.wait_ge(s_const, 3)
        G_.tensor_copy(identr[:], ident[:]).then_inc(s_const, 1)

        def inv_sqrt(dst, src, n, done):
            G_.tensor_tensor(dst, src, half[:, 0:n], ALU.pow).then_inc(done, 1)

        def weight_lo(w, par, slot):
            pool.wait_ge(s_whi, w + 1)
            G_.tensor_tensor(wlo[:, par], wraw[:, slot], f(whi[:, par]), ALU.subtract).then_inc(s_wlo, 1)

        def modulation(tile0, tile1):
            for n in range(2 * tile0, 2 * tile1):
                if n % 3 != 2:
                    continue
                j, (place, loaded, count) = n // 3, ada_slot(n // 2)
                pool.wait_ge(loaded, count)
                if j >= 2:
                    pool.wait_ge(s_ads, j - 1)
                G_.tensor_tensor(products[j % 2], place, csilu[:, n % 2, :], ALU.mult).then_inc(s_adp, 1)

        pool.wait_ge(s_yst, STORED)
        pool.wait_ge(s_c, 2)
        modulation(0, ADA_EARLY // 2 + 2)
        pool.wait_ge(s_var, 1)
        inv_sqrt(rstd[:, 0, 0:TT], vvar[:, 0, 0:TT], TT, s_rstd)
        modulation(ADA_EARLY // 2 + 2, ADA_EARLY)
        weight_lo(0, 0, 0)
        weight_lo(1, 1, 1)
        pool.wait_ge(s_hl, KT)
        for m in range(2):
            sign = 1 - 2 * m
            G_.memset(T2[:, m * P:(m + 1) * P], 0.0).then_inc(s_mask, 1)
            pool.wait_ge(s_mask, 3 * m + 1)
            G_.affine_select(out=T2[:, m * P:(m + 1) * P], in_=T2[:, m * P:(m + 1) * P], compare_op=ALU.is_ge,
                             fill=MASKED, base=0, pattern=[[sign, P]], channel_multiplier=-sign).then_inc(s_mask, 1)
            pool.wait_ge(s_mask, 3 * m + 2)
            G_.tensor_copy(maskr[:, m, :], T2[:, m * P:(m + 1) * P]).then_inc(s_mask, 1)

        def qk_rstd(u, par):
            pool.wait_ge(s_vq, u + 1)
            inv_sqrt(rq[:, par, :], vq[:], TT, s_rq)

        def q_lo(e, par):
            pool.wait_ge(s_qhi, e + 1)
            G_.tensor_tensor(Qlo[:, par, :], QR[:], f(Qhi[:, par, :]), ALU.subtract).then_inc(s_qlo, 1)

        modulation(ADA_EARLY, ADA_EARLY + LATE_AHEAD)
        for g in range(GROUPS):
            cut = ADA_EARLY + LATE_START[g] + LATE_SHARE[g][0]
            weight_lo(2 * g + 2, 0, 0)
            weight_lo(2 * g + 3, 1, 1)
            modulation(ADA_EARLY + LATE_START[g], cut)
            if g >= 2:
                qk_rstd(g - 2, g % 2)
            modulation(cut, ADA_EARLY + LATE_START[g + 1])
        q_lo(GROUPS, 0)
        for c in range(2):
            weight_lo(W_HEAD0 + 2 + c, c, c)

        def attention(r, last):
            for s in range(SLOTS + 3):
                n = SLOTS * r + s
                skip = lambda hs: hs is None or (last and hs == GROUPS - 1)
                if s < SLOTS and s % BLOCKS in (0, 2):
                    hs, v = s // BLOCKS, s % BLOCKS // 2
                    j = 2 * GROUPS * r + 2 * hs + v
                    if v == 0:
                        pool.wait_ge(s_w[2 + hs % 2], 16 * (USES_LAST[hs % 2] + hs // 2 + 1) + 16 * 2 * r)
                    pool.wait_ge(s_ads, POOL_LATE + j)
                    G_.tensor_tensor(product0[:], wraw[:, 2 + hs % 2].rearrange("p a b -> p (a b)"), csilu[:, v, :],
                                     ALU.mult).then_inc(s_adp, 1)
                if not skip(hs := due(s, 4, 5)):
                    q_lo(GROUPS + GROUPS * r + hs + 1, (hs + 1) % 2)
                if not skip(hs := due(s, 5, 6)) and (hs + 1) % GROUPS >= 2:
                    qk_rstd(2 * r + hs + 1, (hs + 1) % 2)
                if not skip(hs := due(s, 4, 5)):
                    weight_lo(W_HEAD0 + 2 * (GROUPS * r + hs + 2), 0, 0)
                if not skip(hs := due(s, 7, 8)):
                    weight_lo(W_HEAD0 + 2 * (GROUPS * r + hs + 2) + 1, 1, 1)

        with pool.Fori(0, HEADS // GROUPS - 1) as r:
            attention(r, False)
        attention(HEADS // GROUPS - 1, True)
        for w in range(W_OUT0 + 2, W_OUT0 + 2 * KT):
            weight_lo(w, w % 2, (w - W_OUT0) % NR)

        def out_rstd(layer):
            for t in range(OUT_TILES[layer]):
                pool.wait_ge(s_var, OUT_VAR[layer] + t + 2)
                inv_sqrt(rstd[:, 1 + 2 * layer, t:t + 1], vvar[:, 1 + 2 * layer, t:t + 1], 1, s_rstd)

        out_rstd(0)
        for b, (t0, t1) in enumerate(NORM_BATCHES):
            pool.wait_ge(s_var, TT + 3 + b)
            inv_sqrt(rstd[:, 2, t0:t1], vvar[:, 2, t0:t1], t1 - t0, s_rstd)
        H2_ = 2 * SSM_HEADS
        pool.wait_ge(s_whi, W_DT + 1)
        G_.tensor_tensor(wlo[:, 0, :, 0:H2_], wraw[:, NR - 1, :, 0:H2_], f(whi[:, 0, :, 0:H2_]),
                         ALU.subtract).then_inc(s_wlo, 1)
        weight_lo(W_SSM, 1, 0)
        pool.wait_ge(s_hl, KT + KT)
        G_.tensor_copy(onesr[:], ones[:]).then_inc(s_tri, 1)
        tri = xt[:, 0, 0:P]
        n = 1
        for d in range(DIRS):
            sign = 1 - 2 * d
            for base, fill, dst in ((ones[:], 0.0, trir[:, d, :]), (None, MASKED, negr[:, d, :])):
                if base is None:
                    pool.wait_ge(s_tri, n)
                    G_.memset(tri, 0.0).then_inc(s_tri, 1)
                    n += 1
                    base = tri
                pool.wait_ge(s_tri, n)
                G_.affine_select(out=tri, in_=base, compare_op=ALU.is_ge, fill=fill, base=0, pattern=[[sign, P]],
                                 channel_multiplier=-sign).then_inc(s_tri, 1)
                pool.wait_ge(s_tri, n + 1)
                G_.tensor_copy(dst, tri).then_inc(s_tri, 1)
                n += 2
        for q in range(1, 6):
            weight_lo(W_SSM + q, (W_SSM + q) % 2, q % 3)

        def by_head(ap, n):
            return ap.rearrange("p (h x) -> p h x", x=n)

        def per_head(ap, n):
            return ap.unsqueeze(2).broadcast_to([P, ap.shape[1], n])

        def ssd(g, last):
            w = W_SSM + 6 + 6 * g
            G = g + 1
            pool.wait_ge(s_gp, g + 1)
            pool.wait_ge(s_txe, 3 * g + 2)
            weighted(g, 0)
            weighted(g, 1)
            if not last:
                weight_lo(w, 1, 0)
            weighted(g, 2)
            weighted(g, 3)
            weighted(g, 4)
            if not last:
                weight_lo(w + 1, 0, 1)
            else:
                for c in range(2):
                    weight_lo(W_OUT1 + c, (W_OUT1 + c) % 2, c)
            for i in range(1, STEPS):
                state_lo(g, i)
            if not last:
                weight_lo(w + 2, 1, 2)
            for c in range(LT):
                n = LT * g + c
                if c == 0:
                    times_d(g, 0)
                if c < LT - 1:
                    times_d(g, c + 1)
                if c == 1 and not last:
                    weight_lo(w + 3, 0, 0)
                if c == 3 and not last:
                    weight_lo(w + 4, 1, 1)
                pool.wait_ge(s_yv, n + 1)
                inv_sqrt(yrs[:, 0:1], yvv[:, 0:1], 1, s_yr)
            if not last:
                weight_lo(w + 5, 0, 2)

        def times_d(g, c):
            if c >= 2:
                pool.wait_ge(s_y2, LT * g + c - 1)
            G_.tensor_tensor(by_head(xD[:, c % 2], HD), by_head(xt[:, CT + c, :], HD), per_head(GP[:, R_D, 0, :], HD),
                             ALU.mult).then_inc(s_xD, 1)

        def weighted(g, i):
            if i >= 2:
                pool.wait_ge(s_xwl, STEPS * g + i - 1)
            for d, u in ((0, FWD[i]), (1, BWD[i])):
                done = G_.tensor_tensor(by_head(xw[:, i % 2, d * GW:(d + 1) * GW], HD), by_head(xt[:, u, :], HD),
                                        per_head(GP[:, R_WE + i, d, :], HD), ALU.mult)
            done.then_inc(s_xw, 1)

        def state_lo(g, i):
            pool.wait_ge(s_Hh, LT * g + i)
            G_.tensor_tensor(Hlo[:, i - 1, 0, :], hcur[:, 0:GW], f(Hhi[:, i - 1, 0, :]), ALU.subtract)
            G_.tensor_tensor(Hlo[:, LT - i, 1, :], hcur[:, GW:2 * GW], f(Hhi[:, LT - i, 1, :]),
                             ALU.subtract).then_inc(s_Hl, 1)

        with pool.Fori(0, SSM_GROUPS - 1) as g:
            ssd(g, False)
        ssd(SSM_GROUPS - 1, True)
        for c in range(2, 2 * KT):
            weight_lo(W_OUT1 + c, (W_OUT1 + c) % 2, c % NR)
        out_rstd(1)

    @block.tensor
    def _(pe):
        def mm3(out, a_hi, a_lo, b_hi, b_lo, start, stop):
            PE_.matmul(out, a_hi, b_hi, start=start, stop=False, skip_group_check=True)
            PE_.matmul(out, a_hi, b_lo, start=False, stop=False, skip_group_check=True)
            return PE_.matmul(out, a_lo, b_hi, start=False, stop=stop, skip_group_check=True)

        pe.wait_ge(s_const, 4)
        pe.wait_ge(s_xn, TT)
        for k in range(KT):
            ps = (psS, psT)[k % 2]
            if k >= 2:
                pe.wait_ge(s_hs, k - 1)
            for t in range(TT):
                last = PE_.transpose(ps[:, t * P:(t + 1) * P], X0[:, t, k * P:(k + 1) * P], ident[:])
            last.then_inc(s_xt, 1)

        def project(e, kind, part, k0, k1, w, done):
            par = kind
            toks = slice(0, CTX) if part == 0 else slice(CTX, TOK)
            out = psC[:, 0:CTX] if part == 0 else psL[kind][:, :]
            for i in range(k0, k1):
                k, m = divmod(i, 3)
                if m == 0 and kind == 0 and part == 0 and isinstance(e, int) and e == 0:
                    pe.wait_ge(s_hl, k + 1)
                a = (whi, whi, wlo)[m][:, par, k, :]
                b = (hhi, hlo, hhi)[m][:, k, toks]
                last = PE_.matmul(out, a, b, start=i == 0, stop=i == 3 * KT - 1, skip_group_check=True)
                if i == 3 * KT - 1:
                    last.then_inc(done, 1)

        def ctx_bank_free(e, kind):
            if kind == 0:
                if isinstance(e, int) and e <= GROUPS:
                    if e:
                        pe.wait_ge(s_thc, e)
                else:
                    pe.wait_ge(s_sgc, e - GROUPS)
            else:
                pe.wait_ge(s_qcev, e + 1)

        def lat_bank_free(e, kind):
            if kind == 0:
                if not (isinstance(e, int) and e == 0):
                    pe.wait_ge(s_qlev, e)
            elif isinstance(e, int) and e <= GROUPS:
                if e:
                    pe.wait_ge(s_thl, e)
            else:
                pe.wait_ge(s_sgl, e - GROUPS)

        def tile_ready(w):
            pe.wait_ge(s_whi, w + 1)
            pe.wait_ge(s_wlo, w + 1)

        def project_tile(e, kind, w):
            tile_ready(w)
            ctx_bank_free(e, kind)
            project(e, kind, 0, 0, 3 * KT, w, (s_qc, s_gc)[kind])
            lat_bank_free(e, kind)
            project(e, kind, 1, 0, 3 * KT, w, (s_ql, s_gl)[kind])

        def square_sums(u, e, pairs=None):
            pe.wait_ge(s_qlev, e + 1)
            if not (isinstance(u, int) and u == 0):
                pe.wait_ge(s_vq, u)
            if pairs is not None:
                pe.wait_ge(s_y, pairs)
            for t in range(TT):
                last = PE_.matmul(psV[:, t:t + 1], SQ[:, t * P:(t + 1) * P], ones[:, 0:1],
                                  start=True, stop=True, skip_group_check=True)
            last.then_inc(s_nq, 1)

        def finish_kv(g):
            if g >= 2:
                square_sums(g - 2, g)
            pe.wait_ge(s_thl, g + 1)
            if g >= 1:
                pe.wait_ge(s_vlo, g)
            if g >= 3:
                pe.wait_ge(s_kn, g - 2)
            for t in range(TT):
                last = PE_.transpose(psT[:, t * P:(t + 1) * P], TH[:, t * P:(t + 1) * P], ident[:])
            last.then_inc(s_vt, 1)
            if g >= 2:
                pe.wait_ge(s_dgk, g - 1)
                pe.wait_ge(s_vlo, g + 1)
                for t in range(TT):
                    last = PE_.matmul(psT[:, t * P:(t + 1) * P], ones[:], dgk[:, t, :], start=True, stop=True,
                                      skip_group_check=True)
                last.then_inc(s_rkb, 1)

        for e in range(GROUPS + 1):
            project_tile(e, 0, 2 * e)
            if e:
                finish_kv(e - 1)
            project_tile(e, 1, 2 * e + 1)

        def scores(r, s):
            n = SLOTS * r + s
            hs, b = s // BLOCKS, s % BLOCKS
            banded, (lo, hi, a) = hs < 2, window(b, hs < 2)
            if b == 0:
                pe.wait_ge(s_qlo, GROUPS + GROUPS * r + hs + 1)
            if s:
                pe.wait_ge(s_ex, n)
            q = slice(b * P, (b + 1) * P)
            qh, ql = Qhi[:, hs % 2, q], Qlo[:, hs % 2, q]
            if hi > lo:
                keys = slice(CTX + lo * P, CTX + hi * P)
                i = b - CT
                mm3(psS[:, a:SEQ], qh, ql, Khi[:, hs, keys], Klo[:, hs, keys], True, not banded)
                if banded and i >= 1:
                    PE_.matmul(psS[:, a:a + P], identr[:], maskr[:, 0, :], start=False, stop=i == LT - 1,
                               skip_group_check=True)
                if banded and i < LT - 1:
                    PE_.matmul(psS[:, SEQ - P:SEQ], identr[:], maskr[:, 1, :], start=False, stop=True,
                               skip_group_check=True)
            mm3(psS[:, SEQ:TOK], qh, ql, Khi[:, hs, 0:CTX], Klo[:, hs, 0:CTX], True, True).then_inc(s_sc, 1)

        def transposes(r, s):
            n = SLOTS * r + s
            lo, hi, a = window(s % BLOCKS, s // BLOCKS < 2)
            pe.wait_ge(s_pn, n + 1)
            if s:
                pe.wait_ge(s_ptl, n)
            for t in range(a // P, TT):
                last = PE_.transpose(psT[:, t * P:(t + 1) * P], PR[:, s % 2, t * P:(t + 1) * P], ident[:])
            last.then_inc(s_pt, 1)

        def values(r, pair):
            hs, q = pair // PAIRS, pair % PAIRS
            p = PAIRS * GROUPS * r + pair
            pe.wait_ge(s_ptl, 2 * p + 2)
            if pair:
                pe.wait_ge(s_y, p)
            if q == 1 and hs in (1, 2):
                pe.wait_ge(s_vq, 2 * r + hs + 2)
            todo = [(c, SEQ // P + c, 0, 2) for c in range(CT)]
            if q:
                b = 2 * q
                (lo0, hi0, a0), (lo1, hi1, a1) = window(b, hs < 2), window(b + 1, hs < 2)
                slot = lambda kt, lo, a: a // P + kt - lo
                for kt in range(min(lo0, lo1), max(hi0, hi1)):
                    in0, in1 = lo0 <= kt < hi0, lo1 <= kt < hi1
                    if in0 and in1 and slot(kt, lo0, a0) == slot(kt, lo1, a1):
                        todo.append((CT + kt, slot(kt, lo0, a0), 0, 2))
                    else:
                        if in0:
                            todo.append((CT + kt, slot(kt, lo0, a0), 0, 1))
                        if in1:
                            todo.append((CT + kt, slot(kt, lo1, a1), 1, 2))
            for i, (kt, sl, x0, x1) in enumerate(todo):
                x = slice(x0 * P, x1 * P)
                last = mm3(psV[:, x0 * P:x1 * P], Vhi[:, kt, hs * P:(hs + 1) * P],
                           Vlo[:, kt, hs * P:(hs + 1) * P], PThi[:, sl, x], PTlo[:, sl, x], i == 0,
                           i == len(todo) - 1)
            last.then_inc(s_pv, 1)

        def next_part(r, s, h, last):
            hs = min(s // BLOCKS, GROUPS - 1)
            if last and hs == GROUPS - 1:
                return
            e, w = GROUPS + GROUPS * r + hs + 1, W_HEAD0 + 2 * (GROUPS * r + hs + 1)
            at = 2 * (s - hs * BLOCKS) + h
            if hs < GROUPS - 1:
                i0, i1 = 8 * at, 8 * at + 8
            else:
                i0, i1 = (6 * at, 6 * at + 6) if at < 12 else (72 + 12 * ((at - 12) // 2), 72 + 12 * ((at - 12) // 2) + 12)
                if at >= 12 and h == 1:
                    return
            kind, part, i0 = i0 // 48, i0 // 24 % 2, i0 % 24
            i1 = i0 + (8 if hs < GROUPS - 1 else 6 if at < 12 else 12)
            if i0 == 0 and part == 0:
                tile_ready(w + kind)
                ctx_bank_free(e, kind)
            if i0 == 0 and part == 1:
                lat_bank_free(e, kind)
            project(e, kind, part, i0, i1, w + kind, ((s_qc, s_gc), (s_ql, s_gl))[part][kind])

        def attention(r, last):
            for s in range(SLOTS + 2):
                hs, b = s // BLOCKS, s % BLOCKS
                if s < SLOTS:
                    scores(r, s)
                if s >= 3 and s % 2 and s < SLOTS:
                    values(r, (s - 3) // 2)
                next_part(r, s, 0, last)
                if 1 <= s <= SLOTS:
                    transposes(r, s - 1)
                next_part(r, s, 1, last)
                if (h := due(s, 4, 5)) is not None and not (last and h == GROUPS - 1) and (h + 1) % GROUPS >= 2:
                    square_sums(2 * r + h + 1, GROUPS + GROUPS * r + h + 1, PAIRS * (GROUPS * r + h) + 1)
                if s == SLOTS + 1:
                    values(r, PAIRS * GROUPS - 1)

        with pe.Fori(0, HEADS // GROUPS - 1) as r:
            attention(r, False)
        attention(HEADS // GROUPS - 1, True)

        def tail(layer, w, y_hi, y_lo):
            tile_ready(w)
            tile_ready(w + 1)
            for t in range(OUT_TILES[layer]):
                q = slice(t * P, (t + 1) * P)
                for i in range(4):
                    k = HEADS - 4 + i
                    x = slice(4 * (i % 2), 4 * (i % 2) + 4)
                    wh = whi[:, (w + i // 2) % 2, x, :].rearrange("p a b -> p (a b)")
                    wl = wlo[:, (w + i // 2) % 2, x, :].rearrange("p a b -> p (a b)")
                    last = mm3(tok_bank[t], y_hi[:, k, q], y_lo[:, k, q], wh, wl, False, i == 3)
                last.then_inc(s_half, 1)

        for nh in range(2):
            for c in range(KT - 2 * nh):
                w = W_OUT0 + nh * KT + c
                tile_ready(w)
                for kk in range(2):
                    k = 2 * c + kk
                    wh = whi[:, w % 2, 4 * kk:4 * kk + 4, :].rearrange("p a b -> p (a b)")
                    wl = wlo[:, w % 2, 4 * kk:4 * kk + 4, :].rearrange("p a b -> p (a b)")
                    if nh == 0:
                        pe.wait_ge(s_yl, k + 1)
                    for t in range(TT):
                        if k == 0:
                            if nh == 0 and t == 0:
                                pe.wait_ge(s_y, PAIRS * HEADS)
                                pe.wait_ge(s_ptl, BLOCKS * HEADS)
                            if nh == 1:
                                pe.wait_ge(s_yo, t + 1)
                        q = slice(t * P, (t + 1) * P)
                        last = mm3(tok_bank[t], Yhi[:, k, q], Ylo[:, k, q], wh, wl, k == 0, k == HEADS - 1)
                        if k == HEADS - 1:
                            last.then_inc(s_half, 1)
                if c < KT - 1:
                    last.then_inc(s_wused, 1)
                if nh == 0 and c in (4, 6):
                    v = (c - 4) // 2
                    if v:
                        pe.wait_ge(s_gre, 1)
                    for k in range(KT):
                        pe.wait_ge(s_dg, v * KT + k + 1)
                        last = PE_.matmul(psT[:, k * P:(k + 1) * P], ones[:], dg[:, k, :], start=True,
                                          stop=True, skip_group_check=True)
                        last.then_inc(s_gr4, 1)

        tail(0, W_OUT0 + 2 * KT - 2, Yhi, Ylo)

        pe.wait_ge(s_xn, TT + TT)
        for k in range(KT):
            ps = (psS, psT)[k % 2]
            if k >= 2:
                pe.wait_ge(s_hs, KT + k - 1)
            for t in range(TT):
                last = PE_.transpose(ps[:, t * P:(t + 1) * P], XN[:, t, k * P:(k + 1) * P], ident[:])
            last.then_inc(s_xt, 1)
        H2_ = 2 * SSM_HEADS
        tile_ready(W_DT)
        for out, toks in ((psC[0:H2_, 0:CTX], slice(0, CTX)), (psL[0][0:H2_, :], slice(CTX, TOK))):
            for k in range(KT):
                pe.wait_ge(s_hl, KT + k + 1)
                last = mm3(out, whi[:, 0, k, 0:H2_], wlo[:, 0, k, 0:H2_], h1hi[:, k, toks], h1lo[:, k, toks], k == 0,
                           k == KT - 1)
        last.then_inc(s_dtp, 1)
        pe.wait_ge(s_dtt, 1)
        for t in range(TT):
            last = PE_.transpose(psT[:, t * H2_:(t + 1) * H2_], CTH[0:H2_, t * P:(t + 1) * P], ident[0:H2_, 0:H2_])
        last.then_inc(s_dtp, 1)

        def project1(g, i, part, k0, k1, q2):
            toks = slice(0, CTX) if part == 0 else slice(CTX, TOK)
            out = psC[:, 0:CTX] if part == 0 else psL[i % 2][:, :]
            for j in range(k0, k1):
                k, m = divmod(j, 3)
                last = PE_.matmul(out, (whi, whi, wlo)[m][:, q2, k, :], (h1hi, h1lo, h1hi)[m][:, k, toks],
                                  start=j == 0, stop=j == 3 * KT - 1, skip_group_check=True)
            if k1 == 3 * KT:
                last.then_inc((s_pc, s_pl)[part], 1)

        def tile_start(g, i, part, w, first):
            if part == 0 or i == 3:
                tile_ready(w)
            if part == 0:
                if not (first and i == 0):
                    pe.wait_ge(s_cvc, 3 * g + i)
            elif not (first and i < 2):
                pe.wait_ge(s_cvl, 4 * g + i - 1)

        def running_sums():
            pe.wait_ge(s_aa, 3)
            pe.wait_ge(s_tri, TRI_STEPS)
            cF = psL[1][:, 0:TT * H2_].rearrange("p (t h) -> p t h", t=TT)
            for d in range(DIRS):
                h = slice(d * SSM_HEADS, (d + 1) * SSM_HEADS)
                PE_.matmul(cF[:, :, h], trir[:, d, :], ahi[:, :, h], start=True, stop=False, skip_group_check=True)
                PE_.matmul(cF[:, :, h], trir[:, d, :], alo[:, :, h], start=False, stop=True, skip_group_check=True)
            PE_.matmul(psS[:, 0:TT * H2_], onesr[:], ahi[:].rearrange("p t h -> p (t h)"), start=True, stop=False,
                       skip_group_check=True)
            PE_.matmul(psS[:, 0:TT * H2_], onesr[:], alo[:].rearrange("p t h -> p (t h)"), start=False, stop=True,
                       skip_group_check=True).then_inc(s_cum, 1)

        for i in range(4):
            for part in range(2):
                if i == 3 and part == 0:
                    continue
                tile_start(0, i, part, W_SSM + i, True)
                if i == 1 and part == 1:
                    pe.wait_ge(s_cum, 2)
                project1(0, i, part, 0, 3 * KT, (W_SSM + i) % 2)
                if i == 0 and part == 1:
                    running_sums()

        def ssd(g, last_group):
            G = g + 1
            def tokens(i):
                pe.wait_ge(s_u, 4 * g + i + 1)
                if i:
                    pe.wait_ge(s_txe, 3 * g + i)
                for t in range(TT):
                    last = PE_.transpose(psT[:, t * P:(t + 1) * P], U[i][:, t * P:(t + 1) * P], ident[:])
                last.then_inc(s_tx, 1)

            def z(half, cs):
                for c in cs:
                    q = slice((CT + c) * P, (CT + c + 1) * P)
                    for kk in range(KT // 2):
                        k = half * KT // 2 + kk
                        slot = (1, 0)[half]
                        wh = whi[:, slot, 2 * kk:2 * kk + 2, :].rearrange("p a b -> p (a b)")
                        wl = wlo[:, slot, 2 * kk:2 * kk + 2, :].rearrange("p a b -> p (a b)")
                        last = mm3(psS[:, c * GW:(c + 1) * GW], h1hi[:, k, q], h1lo[:, k, q], wh, wl,
                                   k == 0 and c % 2 == 0, k == KT - 1)
                return last

            def next_part(p):
                if last_group:
                    return
                i, part = ((0, 0), (0, 1), (1, 0), (1, 1), (2, 0), (2, 1), (3, 1))[p // 2]
                if p % 2 == 0:
                    tile_start(G, i, part, W_SSM + 6 + 6 * g + i, False)
                project1(G, i, part, 12 * (p % 2), 12 * (p % 2) + 12, (1, 0, 1, 0)[i])

            def log_decays(c):
                if c == 0:
                    pe.wait_ge(s_btl, g + 1)
                    pe.wait_ge(s_gpa, g + 1)
                else:
                    pe.wait_ge(s_e, LT * g + c)
                for d in range(DIRS):
                    bank = psT[:, d * 512:(d + 1) * 512]
                    PE_.matmul(bank, identr[:], negr[:, d, :].unsqueeze(1).broadcast_to([P, GH, P]), start=True,
                               stop=False, skip_group_check=True)
                    for h in range(GH):
                        for m, a in enumerate((aghi, aglo)):
                            last = PE_.matmul(bank[:, h * P:(h + 1) * P], a[:, c, d, h:h + 1].broadcast_to([P, P]),
                                              trir[:, d, :], start=False, stop=m == 1, skip_group_check=True)
                last.then_inc(s_r, 1)

            def cb(c):
                q = slice(c * P, (c + 1) * P)
                mm3(ybank[1][:, 0:P], bfhi[:, 0, q], bflo[:, 0, q], bfhi[:, 1, q], bflo[:, 1, q], True,
                    True).then_inc(s_cb, 1)

            tile_ready(W_SSM + 4 + 6 * g)
            tokens(0)
            z(0, (0, 1))
            tokens(1)
            z(0, (2, 3)).then_inc(s_zc, 1)
            tokens(2)
            tile_ready(W_SSM + 5 + 6 * g)
            z(1, (0, 1))
            z(1, (2, 3)).then_inc(s_zc, 1)
            log_decays(0)
            pe.wait_ge(s_sz, g + 1)
            pe.wait_ge(s_bfl, g + 1)
            cb(0)
            for i in range(STEPS):
                pe.wait_ge(s_xwl, STEPS * g + i + 1)
                if i:
                    pe.wait_ge(s_hc, STEPS * g + i)
                for d, u in ((0, FWD[i]), (1, BWD[i])):
                    x = slice(d * GW, (d + 1) * GW)
                    last = mm3(ybank[0][:, x], bthi[:, u, :], btlo[:, u, :], xwhi[:, i % 2, x], xwlo[:, i % 2, x],
                               True, True)
                last.then_inc(s_st, 1)
                if i == 2:
                    log_decays(1)
                next_part(i)
            next_part(STEPS)
            pe.wait_ge(s_txl, g + 1)
            for c in range(LT):
                n = LT * g + c
                pe.wait_ge(s_ml, n + 1)
                for h in range(GH):
                    x, m = slice(h * HD, (h + 1) * HD), slice(h * P, (h + 1) * P)
                    last = mm3(ybank[1][:, P + h * HD:P + (h + 1) * HD], Mhi[:, m], Mlo[:, m], xthi[:, c, x],
                               xtlo[:, c, x], True, True)
                last.then_inc(s_yd, 1)
                if c == 0:
                    pe.wait_ge(s_hc, STEPS * (g + 1))
                    pe.wait_ge(s_Hl, LT * (g + 1))
                else:
                    pe.wait_ge(s_y1, n)
                q = slice(c * P, (c + 1) * P)
                mm3(ybank[0], bfhi[:, 1, q], bflo[:, 1, q], Hhi[:, c].rearrange("p d x -> p (d x)"),
                    Hlo[:, c].rearrange("p d x -> p (d x)"), True, True).then_inc(s_yof, 1)
                next_part(6 + 2 * c)
                if c < LT - 1:
                    pe.wait_ge(s_y2, n + 1)
                    cb(c + 1)
                if c < LT - 2:
                    log_decays(c + 2)
                if c:
                    y_transposed(g, c - 1)
                next_part(7 + 2 * c)
            y_transposed(g, LT - 1)

        def y_transposed(g, c):
            pe.wait_ge(s_yn, LT * g + c + 1)
            if c:
                pe.wait_ge(s_yte, LT * g + c)
            for i in range(2):
                last = PE_.transpose(psV[:, i * P:(i + 1) * P], ynm[:, i * P:(i + 1) * P], ident[:])
            last.then_inc(s_yt, 1)

        with pe.Fori(0, SSM_GROUPS - 1) as g:
            ssd(g, False)
        ssd(SSM_GROUPS - 1, True)

        for nh in range(2):
            for c in range(KT - 2 * nh):
                i = nh * KT + c
                tile_ready(W_OUT1 + i)
                for kk in range(2):
                    k = 2 * c + kk
                    sl = (W_OUT1 + i) % 2
                    wh = whi[:, sl, 4 * kk:4 * kk + 4, :].rearrange("p a b -> p (a b)")
                    wl = wlo[:, sl, 4 * kk:4 * kk + 4, :].rearrange("p a b -> p (a b)")
                    if nh == 0:
                        pe.wait_ge(s_yl, HEADS + k + 1)
                    for t in range(LT):
                        if k == 0 and nh == 1:
                            pe.wait_ge(s_yo, OUT_YO[1] + t + 1)
                        q = slice(t * P, (t + 1) * P)
                        last = mm3(tok_bank[t], Y1hi[:, k, q], Y1lo[:, k, q], wh, wl, k == 0, k == HEADS - 1)
                        if k == HEADS - 1:
                            last.then_inc(s_half, 1)
                if c < KT - 1:
                    last.then_inc(s_wused, 1)
                if nh == 0 and c == 4:
                    for k in range(KT):
                        pe.wait_ge(s_dg1, k + 1)
                        PE_.matmul(psT[:, k * P:(k + 1) * P], ones[:], dg1[:, k, :], start=True, stop=True,
                                   skip_group_check=True).then_inc(s_gr1, 1)
        tail(1, W_OUT1 + 2 * KT - 2, Y1hi, Y1lo)


def kernel(**inputs):
    import numpy as np
    import concourse.bacc as bacc
    from concourse.bass_utils import run_bass_kernel_spmd as run
    a = {k: np.asarray(v) for k, v in inputs.items()}
    f32 = mybir.dt.float32

    def tiles(w, columns):
        w = w[:, columns].reshape(KT, P, -1, P)
        return np.ascontiguousarray(w.transpose(2, 1, 0, 3))

    def colvec(v):
        return v.reshape(-1, P).T

    def out_chunks(w):
        w = w.reshape(-1, 2, P, 2, 512)
        return np.ascontiguousarray(w.transpose(3, 0, 2, 1, 4).reshape(-1, P, KT, P))

    split = np.concatenate([np.arange(0, P, 2), np.arange(1, P, 2)])
    off = dict(zip(("qa", "ka", "va", "ga", "qb", "kb", "vb", "gb"), (0, 1024, 1280, 1536, 2560, 3584, 3840, 4096)))
    order, rows_out, sinks = [], [], []
    for g in range(GROUPS):
        t = "ab"[g // 2]
        order += [off["k" + t] + (g % 2) * P + split, off["v" + t] + (g % 2) * P + np.arange(P)]
    for r in range(HEADS // GROUPS):
        for g in range(GROUPS):
            t, h = "ab"[g // 2], (g % 2) * GROUPS + r
            order += [off["q" + t] + h * P + split, off["g" + t] + h * P + np.arange(P)]
            rows_out.append((g // 2) * 1024 + h * P + np.arange(P))
            if g < 2:
                sinks.append(h)
    order, rows_out = np.concatenate(order), np.concatenate(rows_out)

    inv = 1.0 / (np.float32(10000.0) ** (np.arange(32, dtype=np.float32) / np.float32(32)))
    row = np.repeat(np.arange(SEQ // 64), 64).astype(np.float32)
    colp = np.tile(np.arange(64), SEQ // 64).astype(np.float32)
    ang = np.concatenate([row[:, None] * inv, colp[:, None] * inv], -1).astype(np.float32).T
    cos, sin = np.cos(ang).astype(np.float32), np.sin(ang).astype(np.float32)

    cw = a["ssm_conv_w"][0]
    columns = [colvec(a["b_ada"].reshape(-1)), colvec(a["norm_pre"].reshape(-1)), colvec(a["norm_post"].reshape(-1)),
               colvec(cw.reshape(-1)), colvec(a["ssm_conv_b"][0]), colvec(a["ssm_norm"][0]),
               a["attn_q_norm"][0][split][:, None], a["attn_k_norm"][0][split][:, None]]
    wi = a["ssm_w_in"][0]
    ssm = []
    for g in range(SSM_GROUPS):
        x = [tiles(wi, 2048 + 256 * g + np.arange(256)), tiles(wi, 4096 + P * g + np.arange(P)),
             tiles(wi, 5120 + P * g + np.arange(P))]
        z = wi[:, 256 * g:256 * g + 256].reshape(2, 4, P, 256).transpose(0, 2, 1, 3).reshape(2, P, KT, P)
        ssm += x + [z]
    ada = [a["w_ada"][l].T.reshape(-1, P, KT, P) for l in range(2)]
    arrays = {
        "xc": np.concatenate([a["ctx"][0], a["x"][0]]).reshape(TT, P, D_MODEL),
        "cvec": np.stack([a["c"][0], a["c_ctx"]]),
        "cols": np.concatenate(columns, 1),
        "rows": np.concatenate([a["attn_sink"][0][sinks], a["ssm_a_log"][0].reshape(-1),
                                a["ssm_dt_bias"][0].reshape(-1), a["ssm_d"][0]]),
        "w_ada": ada[0][None, :ADA_EARLY],
        "w_ada_late": np.concatenate([ada[0][ADA_EARLY:], ada[1]]),
        "w_in": tiles(a["attn_w_in"][0], order),
        "w_out0": out_chunks(a["attn_w_out"][0][rows_out]),
        "w_ssm": np.concatenate(ssm),
        "w_dt": wi[:, 6144:6208].reshape(KT, P, 64).transpose(1, 0, 2),
        "w_out1": out_chunks(a["ssm_w_out"][0]),
        "cos": np.concatenate([cos, cos]), "sin": np.concatenate([sin, -sin]),
    }
    arrays = {"in_" + k: np.ascontiguousarray(v) for k, v in arrays.items()}
    nc = bacc.Bacc("TRN2", target_bir_lowering=False, num_devices=1)
    io = {k[3:]: nc.dram_tensor(k, v.shape, f32, kind="ExternalInput").ap() for k, v in arrays.items()}
    io["out"] = nc.dram_tensor("out", (LT, P, D_MODEL), f32, kind="ExternalOutput").ap()
    io["y_spill"] = nc.dram_tensor("y_spill", (HEADS, P, TOK), f32, kind="Internal").ap()
    io["x1_spill"] = nc.dram_tensor("x1_spill", (LT, P, D_MODEL), f32, kind="Internal").ap()
    io["y1_spill"] = nc.dram_tensor("y1_spill", (SSM_GROUPS, P, 2, SEQ), f32, kind="Internal").ap()
    build(nc, io)
    r = run(nc, [arrays], core_ids=[0])
    return r.results[0]["out"].reshape(1, SEQ, D_MODEL)
```

```python
import concourse.bass as bass
from concourse import mybir
from contextlib import ExitStack

P = 128
D_MODEL, SEQ, CTX = 1024, 512, 256
TOK = CTX + SEQ
TT = TOK // P
CT = CTX // P
KT = D_MODEL // P
EPS = 1e-6
HEADS = 16
GROUPS = 4
SCALE = P ** -0.5
NR = 4
ADA = 3 * KT
ADA_EARLY = 2 * KT
MASKED = -float(2 ** 100)
SSM_GROUPS = 8
SSM_HEADS = 32
GH = SSM_HEADS // SSM_GROUPS
HD = 64
GW = GH * HD
LT = SEQ // P
DIRS = 2


def column_places():
    at, where = 0, {}
    for name, n in (("b_ada", 2 * ADA), ("pre", 2 * KT), ("post", 2 * KT), ("conv_w", 3 * 32), ("conv_b", 32),
                    ("ssm_norm", 16), ("q_norm", 1), ("k_norm", 1)):
        where[name] = (at, at + n)
        at += n
    return where, at


COLS, NCOLS = column_places()
R_LOG, R_EA, R_WE, R_DEC, R_D = 0, 4, 8, 13, 18
TAB_ROWS = 19
STEPS = 5
FWD, BWD = (0, 1, 2, 3, 4), (1, 0, 5, 4, 3)
ROWS = {"sink": (0, 8), "a_log": (8, 72), "dt_bias": (72, 136), "d": (136, 168)}
NROWS = 168


def build(nc, io):
    f32, f32r = mybir.dt.float32, mybir.dt.float32r
    ALU, ACT, AX = mybir.AluOpType, mybir.ActivationFunctionType, mybir.AxisListType
    PE_, V_, A_, G_ = nc.tensor, nc.vector, nc.scalar, nc.gpsimd
    ds = bass.ds

    keep = ExitStack()

    def sbuf(stack, name, shape, dt=f32):
        return stack.enter_context(nc.sbuf_tensor(name, shape, dt))

    def psum(name, shape):
        return keep.enter_context(nc.psum_tensor(name, shape, f32))

    def sem(name):
        return keep.enter_context(nc.semaphore(name))

    def f(ap):
        return ap.bitcast(f32)

    wraw = sbuf(keep, "wraw", [P, NR, KT, P])
    whi = sbuf(keep, "whi", [P, 2, KT, P], f32r)
    wlo = sbuf(keep, "wlo", [P, 2, KT, P], f32r)
    cols = sbuf(keep, "cols", [P, NCOLS])
    ident = sbuf(keep, "ident", [P, P])
    identr = sbuf(keep, "identr", [P, P], f32r)
    ones = sbuf(keep, "ones", [P, P])
    mod = sbuf(keep, "mod", [P, 2 * ADA, 2])
    modp = sbuf(keep, "modp", [P, GROUPS, 2])
    gain = sbuf(keep, "gain", [P, 2, KT, 2])
    ssq = sbuf(keep, "ssq", [P, 4, 8])
    vvar = sbuf(keep, "vvar", [P, 4, 8])
    rstd = sbuf(keep, "rstd", [P, 4, 8])
    half = sbuf(keep, "half", [P, 8])
    nothing = sbuf(keep, "nothing", [P, 1])
    gcolx = sbuf(keep, "gcolx", [P, 2, KT, 2])

    psL = [psum("psL0", [P, 512]), psum("psL1", [P, 512])]
    psC = psum("psC", [P, 512])
    psS = psum("psS", [P, 1024])
    psT = psum("psT", [P, 1024])
    psV = psum("psV", [P, 512])
    tok_bank = [psL[0][:, :], psL[1][:, :], psC[:, :], psS[:, 0:512], psS[:, 512:1024], psV[:, :]]

    ph = ExitStack()
    csilu = sbuf(ph, "csilu", [P, 2, D_MODEL])
    hhi = sbuf(ph, "hhi", [P, KT, TOK], f32r)
    hlo = sbuf(ph, "hlo", [P, KT, TOK], f32r)
    with ExitStack() as s:
        X0 = sbuf(s, "X0", [P, TT, D_MODEL])
        HS0 = sbuf(s, "HS0", [P, 2, TOK])
        junk0 = sbuf(s, "junk0", [P, D_MODEL])
        cth = sbuf(s, "cth", [P, 2, D_MODEL])
    with ExitStack() as s:
        rowt = sbuf(s, "rowt", [P, 8])
        nsink = sbuf(s, "nsink", [P, 8])
        costab = sbuf(s, "costab", [P, SEQ])
        sintab = sbuf(s, "sintab", [P, SEQ])
        maskr = sbuf(s, "maskr", [P, 2, P], f32r)
        Khi = sbuf(s, "Khi", [P, GROUPS, TOK], f32r)
        Klo = sbuf(s, "Klo", [P, GROUPS, TOK], f32r)
        Vhi = sbuf(s, "Vhi", [P, TT, GROUPS * P], f32r)
        Vlo = sbuf(s, "Vlo", [P, TT, GROUPS * P], f32r)
        PThi = sbuf(s, "PThi", [P, TT, 2 * P], f32r)
        PTlo = sbuf(s, "PTlo", [P, TT, 2 * P], f32r)
        QR = sbuf(s, "QR", [P, TOK])
        SQ = sbuf(s, "SQ", [P, TOK])
        T1 = sbuf(s, "T1", [P, SEQ])
        T2 = sbuf(s, "T2", [P, SEQ])
        Qhi = sbuf(s, "Qhi", [P, 2, TOK], f32r)
        Qlo = sbuf(s, "Qlo", [P, 2, TOK], f32r)
        TH = sbuf(s, "TH", [P, TOK])
        SG = sbuf(s, "SG", [P, 2, TOK])
        PR = sbuf(s, "PR", [P, 2, TOK])
        Yst = sbuf(s, "Yst", [P, 2, TOK])
        smax = sbuf(s, "smax", [P, 2])
        nmax = sbuf(s, "nmax", [P, 2])
        esum = sbuf(s, "esum", [P, 2])
        esink = sbuf(s, "esink", [P, 2])
        eall = sbuf(s, "eall", [P, 2])
        rinv = sbuf(s, "rinv", [P, 2])
        vq = sbuf(s, "vq", [P, TT])
        rq = sbuf(s, "rq", [P, 2, TT])
        dgk = sbuf(s, "dgk", [P, TT, P])
        product0 = sbuf(s, "product0", [P, D_MODEL])

    def flat(ap):
        return ap.rearrange("p a b -> p (a b)")[:, 0:D_MODEL]

    product = flat(Yst[:])
    products = (product0[:], flat(SG[:]))
    ph.close()
    ph = ExitStack()
    X1 = sbuf(ph, "X1", [P, TT, D_MODEL])
    with ExitStack() as s:
        Yparts = sbuf(s, "Yparts", [P, HEADS, 2, TOK], f32r)
        Yhi, Ylo = Yparts[:, :, 0, :], Yparts[:, :, 1, :]
        Yraw = X1[:, :, :].rearrange("p t d -> p (t d)")[:, 2 * D_MODEL:2 * D_MODEL + 2 * TOK].rearrange(
            "p (a b) -> p a b", a=2)
        Yo = sbuf(s, "Yo", [P, TT, D_MODEL])
        grow = sbuf(s, "grow", [P, 2, D_MODEL])
        dg = sbuf(s, "dg", [P, KT, P])
        junk1 = sbuf(s, "junk1", [P, 512])
    h1hi = sbuf(ph, "h1hi", [P, KT, TOK], f32r)
    h1lo = sbuf(ph, "h1lo", [P, KT, TOK], f32r)
    with ExitStack() as s:
        XN = sbuf(s, "XN", [P, TT, D_MODEL])
        HS1 = sbuf(s, "HS1", [P, 2, TOK])
    x1flat = X1[:, :, :].rearrange("p t d -> p (t d)")
    places = {}
    UEND = 3 * TOK + SEQ
    at = 0
    for name, n in (("U", 3 * TOK + SEQ), ("sz", LT * GW), ("E", DIRS * GH * P), ("y1", 2 * GW), ("y2", GW),
                    ("y3", GW), ("yg", GW)):
        places[name] = x1flat[:, at:at + n]
        at += n
    U, sz, E, y1, y2, y3, yg = places.values()
    U = [U[:, i * TOK:min((i + 1) * TOK, 3 * TOK + SEQ)] for i in range(4)]
    with ExitStack() as s:
        rows1 = sbuf(s, "rows1", [P, NROWS - 8])
        TAB = sbuf(s, "TAB", [P, TAB_ROWS, 2 * SSM_HEADS])
        GP = sbuf(s, "GP", [P, TAB_ROWS, DIRS, GH])
        acu = sbuf(s, "acu", [P, TT, 2 * SSM_HEADS])
        ahi = sbuf(s, "ahi", [P, TT, 2 * SSM_HEADS], f32r)
        alo = sbuf(s, "alo", [P, TT, 2 * SSM_HEADS], f32r)
        aghi = sbuf(s, "aghi", [P, LT, DIRS, GH], f32r)
        aglo = sbuf(s, "aglo", [P, LT, DIRS, GH], f32r)
        trir = sbuf(s, "trir", [P, DIRS, P], f32r)
        onesr = sbuf(s, "onesr", [P, P], f32r)
        negr = sbuf(s, "negr", [P, DIRS, P], f32r)
        convh = sbuf(s, "convh", [P, 4 * 32])
        normh = sbuf(s, "normh", [P, 16])
        gtap = sbuf(s, "gtap", [P, 4, 4])
        gnorm = sbuf(s, "gnorm", [P, 2])
        xt = sbuf(s, "xt", [P, TT, GW])
        xthi = sbuf(s, "xthi", [P, LT, GW], f32r)
        xtlo = sbuf(s, "xtlo", [P, LT, GW], f32r)
        bthi = sbuf(s, "bthi", [P, TT, P], f32r)
        btlo = sbuf(s, "btlo", [P, TT, P], f32r)
        bfhi = sbuf(s, "bfhi", [P, 2, SEQ], f32r)
        bflo = sbuf(s, "bflo", [P, 2, SEQ], f32r)
        xw = sbuf(s, "xw", [P, 2, DIRS * GW])
        xwhi = sbuf(s, "xwhi", [P, 2, DIRS * GW], f32r)
        xwlo = sbuf(s, "xwlo", [P, 2, DIRS * GW], f32r)
        hcur = sbuf(s, "hcur", [P, DIRS * GW])
        hdec = sbuf(s, "hdec", [P, DIRS * GW])
        Hhi = sbuf(s, "Hhi", [P, LT, DIRS, GW], f32r)
        Hlo = sbuf(s, "Hlo", [P, LT, DIRS, GW], f32r)
        Wm = sbuf(s, "Wm", [P, GH * P])
        Mf = sbuf(s, "Mf", [P, GH * P])
        Mhi = sbuf(s, "Mhi", [P, GH * P], f32r)
        Mlo = sbuf(s, "Mlo", [P, GH * P], f32r)
        xD = sbuf(s, "xD", [P, 2, GW])
        thz = sbuf(s, "thz", [P, LT * GW])
        CTH = sbuf(s, "CTH", [P, TOK])
        yss = sbuf(s, "yss", [P, 2])
        ynm = sbuf(s, "ynm", [P, GW])
        yvv = sbuf(s, "yvv", [P, 2])
        yrs = sbuf(s, "yrs", [P, 2])
        YT = sbuf(s, "YT", [P, 2, SEQ])
    ph.close()
    ph = ExitStack()
    X2 = sbuf(ph, "X2", [P, TT, D_MODEL])
    with ExitStack() as s:
        Y1raw = sbuf(s, "Y1raw", [P, 2, SEQ])
        Y1parts = sbuf(s, "Y1parts", [P, HEADS, 2, SEQ], f32r)
        Y1hi, Y1lo = Y1parts[:, :, 0, :], Y1parts[:, :, 1, :]
        Yo1 = sbuf(s, "Yo1", [P, LT, D_MODEL])
        grow1 = sbuf(s, "grow1", [P, D_MODEL])
        junk3 = sbuf(s, "junk3", [P, 512])
        dg1 = sbuf(s, "dg1", [P, KT, P])

    s_small_loaded = sem("small_loaded")
    s_x_loaded = [sem(f"x_loaded{t}") for t in range(TT)]
    s_raw_weights_loaded = [sem(f"raw_weights_loaded{i}") for i in range(NR)]
    s_constants_made = sem("constants_made")
    s_weight_hi, s_weight_lo, s_weight_used = sem("weight_hi"), sem("weight_lo"), sem("weight_used")
    s_modulation_tile_done = sem("modulation_tile_done")
    s_modulation_product, s_modulation_product_summed = sem("modulation_product"), sem("modulation_product_summed")
    s_modulation_tile_loaded = sem("modulation_tile_loaded")
    s_silu_c_step = sem("silu_c_step")
    s_modulation_columns = sem("modulation_columns")
    s_gain_columns = sem("gain_columns")
    s_sum_of_squares, s_variance, s_rstd = sem("sum_of_squares"), sem("variance"), sem("rstd")
    s_x_normed = sem("x_normed")
    s_x_transposed, s_h_scaled, s_h_hi, s_h_lo = sem("x_transposed"), sem("h_scaled"), sem("h_hi"), sem("h_lo")
    s_q_ctx_proj, s_q_lat_proj, s_g_ctx_proj, s_g_lat_proj = sem("q_ctx_proj"), sem("q_lat_proj"), sem("g_ctx_proj"), sem("g_lat_proj")
    s_rope_step = sem("rope_step")
    s_q_hi, s_q_lo = sem("q_hi"), sem("q_lo")
    s_qk_square_sums, s_qk_variance, s_qk_rstd = sem("qk_square_sums"), sem("qk_variance"), sem("qk_rstd")
    s_k_rstd_diag, s_k_rstd_rows, s_k_normed = sem("k_rstd_diag"), sem("k_rstd_rows"), sem("k_normed")
    s_v_transposed, s_v_hi, s_v_lo = sem("v_transposed"), sem("v_hi"), sem("v_lo")
    s_scores, s_score_max, s_neg_max, s_probs, s_sink_exp = sem("scores"), sem("score_max"), sem("neg_max"), sem("probs"), sem("sink_exp")
    s_denominator, s_inv_denominator, s_probs_normed = sem("denominator"), sem("inv_denominator"), sem("probs_normed")
    s_probs_transposed, s_probs_t_hi, s_probs_t_lo = sem("probs_transposed"), sem("probs_t_hi"), sem("probs_t_lo")
    s_pv_done, s_y_gated, s_y_stored = sem("pv_done"), sem("y_gated"), sem("y_stored")
    s_late_modulation_columns = sem("late_modulation_columns")
    s_y_loaded = [sem(f"y_loaded{i}") for i in range(2)]
    s_y_hi, s_y_lo = sem("y_hi"), sem("y_lo")
    s_out_half, s_out_evacuated, s_out_squares = sem("out_half"), sem("out_evacuated"), sem("out_squares")
    s_gate_columns, s_gate_diag, s_gate_rows_out = sem("gate_columns"), sem("gate_diag"), sem("gate_rows_out")
    s_residual, s_out_stored = sem("residual"), sem("out_stored")
    s_x_reloaded = sem("x_reloaded")
    s_gate_diag_used = sem("gate_diag_used")
    s_tables_loaded, s_neg_sink, s_band_masks = sem("tables_loaded"), sem("neg_sink"), sem("band_masks")
    s_rope_cos_part, s_rope_sin_part = sem("rope_cos_part"), sem("rope_sin_part")
    s_q_ctx_evacuated, s_q_lat_evacuated = sem("q_ctx_evacuated"), sem("q_lat_evacuated")
    s_tanh_ctx, s_tanh_lat, s_gate_ctx, s_gate_lat = sem("tanh_ctx"), sem("tanh_lat"), sem("gate_ctx"), sem("gate_lat")

    NW_KV = 2 * GROUPS
    W_HEAD0 = NW_KV
    W_OUT0 = NW_KV + 2 * HEADS
    USES_ADA = ADA_EARLY // NR
    ADA_LATE = HEADS
    ADA_LAST = 2 * ADA - ADA_EARLY - ADA_LATE
    assert ADA_LAST == HEADS
    LATE_AHEAD = 4
    LATE_SHARE = ((2, 1), (2, 1), (2, 1), (2, 1))
    LATE_START = [LATE_AHEAD + sum(sum(p) for p in LATE_SHARE[:g]) for g in range(GROUPS + 1)]
    assert LATE_START[GROUPS] == ADA_LATE
    USES_HEAD0 = USES_ADA + NW_KV // 2
    USES_LAST = (USES_ADA + 6, USES_ADA + 5)
    USES_OUT0 = [USES_HEAD0 + HEADS] * 2 + [n + HEADS // 2 for n in USES_LAST]
    STORED = 32

    W_DT = W_OUT0 + 2 * KT
    W_SSM = W_DT + 1
    W_OUT1 = W_SSM + 6 * SSM_GROUPS
    USES_SSM = [n + 2 * KT // NR for n in USES_OUT0]
    TRI_STEPS = 11
    Q_OUT1 = W_OUT1 - W_SSM
    USES_OUT1 = [n + Q_OUT1 // 3 for n in USES_SSM[:3]] + [USES_SSM[3] + 1]

    BLOCKS = TT
    PAIRS = TT // 2
    SLOTS = GROUPS * BLOCKS

    def pool_sums(n):
        return n // 3

    def dve_sums(n):
        return n - n // 3

    POOL_LATE = (2 * ADA_EARLY + 2 * ADA_LATE) // 3

    def tile_summed(eng, tile):
        eng.wait_ge(s_modulation_tile_done, dve_sums(2 * tile + 2))
        if pool_sums(2 * tile + 2):
            eng.wait_ge(s_modulation_product, pool_sums(2 * tile + 2))

    def ada_slot(tile):
        if tile < ADA_EARLY:
            return wraw[:, tile % NR].rearrange("p a b -> p (a b)"), s_raw_weights_loaded[tile % NR], 16 * (tile // NR + 1)
        n = tile - ADA_EARLY
        if n % 3 < 2:
            return wraw[:, 2 + n % 3].rearrange("p a b -> p (a b)"), s_raw_weights_loaded[2 + n % 3], 16 * (USES_ADA + n // 3 + 1)
        return flat(PR[:]), s_modulation_tile_loaded, 16 * (n // 3 + 1)

    def col(name, i=0, n=1):
        a = COLS[name][0] + i
        return cols[:, a:a + n]

    s_x1_stored = sem("x1_stored")
    s_dt_step, s_dt_projected, s_rows_loaded, s_triangles = sem("dt_step"), sem("dt_projected"), sem("rows_loaded"), sem("triangles")
    s_a_split, s_running_sums = sem("a_split"), sem("running_sums")
    s_dt_evacuated = sem("dt_evacuated")
    s_tile_ctx_projected, s_tile_lat_projected = sem("tile_ctx_projected"), sem("tile_lat_projected")
    s_conv_mid_ctx, s_conv_mid_lat = sem("conv_mid_ctx"), sem("conv_mid_lat")
    s_conv_ctx, s_conv_lat, s_conv_tanh, s_conv_done = sem("conv_ctx"), sem("conv_lat"), sem("conv_tanh"), sem("conv_done")
    s_group_columns, s_group_a = sem("group_columns"), sem("group_a")
    s_tokens_transposed, s_tokens_out, s_tokens_hi, s_tokens_lo = sem("tokens_transposed"), sem("tokens_out"), sem("tokens_hi"), sem("tokens_lo")
    s_bc_hi, s_bc_lo = sem("bc_hi"), sem("bc_lo")
    s_z_tanh, s_z_silu = sem("z_tanh"), sem("z_silu")
    s_x_weighted, s_x_weighted_hi, s_x_weighted_lo = sem("x_weighted"), sem("x_weighted_hi"), sem("x_weighted_lo")
    s_state_added, s_state_decayed, s_state_new, s_state_hi, s_state_lo = (sem("state_added"), sem("state_decayed"), sem("state_new"), sem("state_hi"),
                                    sem("state_lo"))
    s_log_decays, s_decays, s_decays_summed, s_cb_decayed, s_cb_decayed_hi, s_cb_decayed_lo = (sem("log_decays"), sem("decays"), sem("decays_summed"),
                                             sem("cb_decayed"), sem("cb_decayed_hi"), sem("cb_decayed_lo"))
    s_y_chunk, s_y_off_scaled, s_y_diag_d, s_y_off_sum, s_y_sum = sem("y_chunk"), sem("y_off_scaled"), sem("y_diag_d"), sem("y_off_sum"), sem("y_sum")
    s_x_d, s_y_gated1, s_y_squares, s_y_variance, s_y_rstd, s_y_normed = (sem("x_d"), sem("y_gated1"), sem("y_squares"), sem("y_variance"),
                                          sem("y_rstd"), sem("y_normed"))
    s_y_transposed, s_y_out, s_y1_stored = sem("y_transposed"), sem("y_out"), sem("y1_stored")
    s_y1_loaded = [sem(f"y1_loaded{i}") for i in range(2)]
    s_gate1_diag, s_gate1_rows, s_gate1_rows_out, s_x1_reloaded = sem("gate1_diag"), sem("gate1_rows"), sem("gate1_rows_out"), sem("x1_reloaded")
    s_z_weight_used, s_conv_ctx_step, s_conv_lat_step, s_b_tokens_lo, s_halved_columns = (sem("z_weight_used"), sem("conv_ctx_step"), sem("conv_lat_step"),
                                       sem("b_tokens_lo"), sem("halved_columns"))
    s_cb_done, s_y_off_done = sem("cb_done"), sem("y_off_done")
    s_dt_correction, s_group_norm_columns = sem("dt_correction"), sem("group_norm_columns")
    dt_x, dt_nx, dt_e, dt_u, dt_l, dt_a = (
        x1flat[:, UEND + i * TT * 2 * SSM_HEADS:UEND + (i + 1) * TT * 2 * SSM_HEADS].rearrange(
            "p (t h) -> p t h", t=TT) for i in range(6))
    ybank = (psS[:, 0:512], psS[:, 512:1024])

    def tap(j, i):
        return gtap[:, j, i:i + 1]

    def bcast2(ap, n):
        return ap.unsqueeze(2).broadcast_to([P, n, 2])

    block = keep.enter_context(nc.Block())

    @block.sync
    def _(sp):
        for v in range(2):
            sp.dma_start(csilu[:, v], io["cvec"][v].partition_broadcast(P)).then_inc(s_small_loaded, 16)
        sp.dma_start(cols[:], io["cols"]).then_inc(s_small_loaded, 16)
        for t in range(NR):
            sp.dma_start(wraw[:, t], io["w_ada"][0, t]).then_inc(s_raw_weights_loaded[t], 16)
        for t in range(TT):
            sp.dma_start(X0[:, t, :], io["xc"][t]).then_inc(s_x_loaded[t], 16)
        for t in range(NR, ADA_EARLY):
            tile_summed(sp, t - NR)
            sp.dma_start(wraw[:, t % NR], io["w_ada"][0, t]).then_inc(s_raw_weights_loaded[t % NR], 16)
        def w_in_load(u):
            sp.dma_start(wraw[:, u % 2], io["w_in"][u]).then_inc(s_raw_weights_loaded[u % 2], 16)

        for u in range(2):
            tile_summed(sp, ADA_EARLY - NR + u)
            w_in_load(u)
        sp.wait_ge(s_h_lo, KT)
        sp.dma_start(costab[:], io["cos"]).then_inc(s_tables_loaded, 16)
        sp.dma_start(sintab[:], io["sin"]).then_inc(s_tables_loaded, 16)
        sp.dma_start(rowt[:], io["rows"][ROWS["sink"][0]:ROWS["sink"][1]].partition_broadcast(P)).then_inc(s_tables_loaded, 16)

        def late_load(n):
            if n < 2:
                tile_summed(sp, ADA_EARLY - 2 + n)
            elif n >= 3:
                tile_summed(sp, ADA_EARLY + n - 3)
            place, loaded, _ = ada_slot(ADA_EARLY + n)
            sp.dma_start(place, io["w_ada_late"][n].rearrange("p a b -> p (a b)")).then_inc(loaded, 16)

        for n in range(3):
            late_load(n)
        for g in range(GROUPS + 1):
            first, last = (LATE_START[g - 1] + 3, min(LATE_START[g] + 3, ADA_LATE)) if g else (3, LATE_AHEAD + 3)
            cut = first + (LATE_SHARE[g - 1][0] if g else 0)
            first = min(first, last)
            cut = (min(cut, last), min(cut + 2, last), last)
            for n in range(first, cut[0]):
                late_load(n)
            for c in range(2):
                u = 2 * g + 2 + c
                if u < 2 * GROUPS + 2:
                    sp.wait_ge(s_weight_lo, u - 1)
                    w_in_load(u)
                for n in range(cut[c], cut[c + 1]):
                    late_load(n)

        def head_loads(j):
            for c in range(2):
                sp.wait_ge(s_weight_lo, W_HEAD0 + 2 * (j - 1) + c + 1)
                sp.dma_start(wraw[:, c], io["w_in"][NW_KV + 2 * j + c]).then_inc(s_raw_weights_loaded[c], 16)

        def y_store(j, par):
            sp.wait_ge(s_y_gated, 3 * j + 3)
            sp.wait_ge(s_y_stored, 16 * j + STORED)
            sp.dma_start(io["y_spill"][j], Yst[:, par, :]).then_inc(s_y_stored, 16)

        def modulation_load(j, par):
            if isinstance(j, int) and j < 2:
                tile_summed(sp, ADA_EARLY + ADA_LATE - 1)
            else:
                sp.wait_ge(s_modulation_product, POOL_LATE + 2 * (j - 1))
            sp.dma_start(wraw[:, 2 + par], io["w_ada_late"][ADA_LATE + j]).then_inc(s_raw_weights_loaded[2 + par], 16)

        head_loads(1)
        modulation_load(0, 0)
        modulation_load(1, 1)
        with sp.Fori(0, (HEADS - 2) // 2) as i:
            for e in range(2):
                head_loads(2 * i + 2 + e)
                modulation_load(2 * i + 2 + e, e)
                y_store(2 * i + e, e)
        for c in range(2):
            sp.wait_ge(s_weight_lo, W_OUT0 - 2 + c + 1)
            sp.dma_start(wraw[:, c], io["w_out0"][c]).then_inc(s_raw_weights_loaded[c], 16)
        for c in range(2, NR):
            sp.wait_ge(s_modulation_product, POOL_LATE + 2 * (HEADS - NR + c) + 2)
            sp.dma_start(wraw[:, c], io["w_out0"][c]).then_inc(s_raw_weights_loaded[c], 16)
        y_store(HEADS - 2, 0)
        y_store(HEADS - 1, 1)
        sp.wait_ge(s_pv_done, 3 * HEADS)
        sp.wait_ge(s_y_gated, 3 * HEADS)
        for c in range(NR, 2 * KT):
            if c == KT + NR:
                sp.wait_ge(s_y_lo, HEADS)
                for t in range(TT):
                    sp.dma_start(X1[:, t, :], io["xc"][t]).then_inc(s_x_reloaded, 16)
            sp.wait_ge(s_weight_lo, W_OUT0 + c - NR + 1)
            sp.dma_start(wraw[:, c % NR], io["w_out0"][c]).then_inc(s_raw_weights_loaded[c % NR], 16)
        sp.wait_ge(s_weight_lo, W_OUT0 + 2 * KT)
        sp.dma_start(wraw[:, NR - 1, :, 0:2 * SSM_HEADS], io["w_dt"]).then_inc(s_raw_weights_loaded[NR - 1], 16)

        def tile_load(q, q3):
            sp.wait_ge(s_weight_lo, W_SSM + q - 2 if not (isinstance(q, int) and q < 3) else W_OUT0 + 2 * KT - 3 + q)
            sp.dma_start(wraw[:, q3], io["w_ssm"][q]).then_inc(s_raw_weights_loaded[q3], 16)

        tile_load(0, 0)
        tile_load(1, 1)
        sp.wait_ge(s_residual, 2 * TT)
        for t in range(LT):
            sp.dma_start(io["x1_spill"][t], X1[:, CT + t, :]).then_inc(s_x1_stored, 16)
        tile_load(2, 2)
        sp.wait_ge(s_h_lo, KT + KT)
        sp.dma_start(rows1[:], io["rows"][8:NROWS].partition_broadcast(P)).then_inc(s_rows_loaded, 16)
        tile_load(3, 0)

        def group_loads(g, last):
            for c in range(2 if last else 6):
                tile_load(6 * g + 4 + c, (4 + c) % 3)

        def y1_store(g):
            sp.wait_ge(s_y_out, LT * (g + 1))
            sp.wait_ge(s_y1_stored, 16 * g + 16)
            sp.dma_start(io["y1_spill"][g], YT[:]).then_inc(s_y1_stored, 16)

        group_loads(0, False)
        with sp.Fori(0, SSM_GROUPS - 2) as g:
            group_loads(g + 1, False)
            y1_store(g)
        group_loads(SSM_GROUPS - 1, True)
        y1_store(SSM_GROUPS - 2)

        def out1_load(c):
            if c < NR - 1:
                sp.wait_ge(s_weight_lo, W_OUT1 - 2 + c)
            elif c == NR - 1:
                sp.wait_ge(s_weight_lo, W_DT + 1)
            else:
                sp.wait_ge(s_weight_lo, W_OUT1 + c - NR + 1)
            sp.dma_start(wraw[:, c % NR], io["w_out1"][c]).then_inc(s_raw_weights_loaded[c % NR], 16)

        for c in range(NR):
            out1_load(c)
        y1_store(SSM_GROUPS - 1)
        sp.wait_ge(s_y1_stored, 16 * SSM_GROUPS + 16)
        for t in range(LT):
            sp.dma_start(X2[:, t, :], io["x1_spill"][t]).then_inc(s_x1_reloaded, 16)
        for c in range(NR, 2 * KT):
            out1_load(c)
        for t in range(LT):
            sp.wait_ge(s_residual, 2 * TT + 2 * t + 2)
            sp.dma_start(io["out"][t], X2[:, t, :]).then_inc(s_out_stored, 16)
        sp.wait_ge(s_out_stored, 16 * LT)

    def window(b, banded):
        if b < CT:
            lo = hi = 0
        elif banded:
            lo, hi = max(0, b - CT - 1), min(LT, b - CT + 2)
        else:
            lo, hi = 0, LT
        return lo, hi, SEQ - (hi - lo) * P

    def due(s, light, heavy):
        for hs in range(GROUPS):
            if s == hs * BLOCKS + (heavy if hs == GROUPS - 1 else light):
                return hs
        return None

    OUT_TILES = (TT, LT)
    OUT_HALF, OUT_YO, OUT_WUSED = (0, 2 * TT), (0, TT), (0, 2 * KT - 3)
    OUT_VAR, OUT_RSTD, OUT_RES = (1, TT + 4), (1, TT + 3), (0, 2 * TT)
    NORM_BATCHES = ((0, 4), (4, TT))

    def chunk_done(eng, layer, c):
        if c in (KT - 1, 2 * KT - 2, 2 * KT - 1):
            eng.wait_ge(s_out_half, OUT_HALF[layer] + OUT_TILES[layer] * (c // KT + 1))
        else:
            eng.wait_ge(s_weight_used, OUT_WUSED[layer] + c - c // KT + 1)

    def lat(u, i):
        return u if i == 3 else u[:, CTX:TOK]

    def free_hi_lo(eng, w, par, tile):
        if isinstance(w, int) and w < 2:
            return
        if isinstance(w, int) and W_DT + 2 > w >= W_OUT0 + 2:
            chunk_done(eng, 0, w - 2 - W_OUT0)
        else:
            eng.wait_ge((s_q_lat_proj, s_g_lat_proj)[par], tile)
    @block.scalar
    def _(act):
        def weight_hi(tile, par, slot, use):
            w = 2 * tile + par
            act.wait_ge(s_raw_weights_loaded[slot], 16 * use)
            free_hi_lo(act, w, par, tile)
            A_.activation(whi[:, par], wraw[:, slot], ACT.Copy).then_inc(s_weight_hi, 1)

        def product_sums(j0, j1):
            for j in range(j0, j1):
                n = 3 * j + 2
                act.wait_ge(s_modulation_product, j + 1)
                A_.activation(products[j % 2], products[j % 2], ACT.Copy, scale=0.5,
                              accum_out=mod[:, n // 2, n % 2:n % 2 + 1]).then_inc(s_modulation_product_summed, 1)

        def late_sums(tile0, tile1):
            product_sums(pool_sums(2 * (ADA_EARLY + tile0)), pool_sums(2 * (ADA_EARLY + tile1)))

        act.wait_ge(s_small_loaded, 48)
        A_.activation(cth[:], csilu[:], ACT.Tanh, scale=0.5).then_inc(s_silu_c_step, 1)
        for t in range(TT):
            act.wait_ge(s_x_loaded[t], 16)
            if t:
                act.wait_ge(s_sum_of_squares, t)
            A_.activation(junk0[:], X0[:, t, :], ACT.Square, accum_out=ssq[:, 0, t:t + 1]).then_inc(s_sum_of_squares, 1)
            if t >= TT - 3:
                product_sums(t - TT + 3, t - TT + 4)
        product_sums(3, pool_sums(ADA_EARLY + 4))
        act.wait_ge(s_rstd, 1)
        for t in range(TT):
            A_.activation(X0[:, t, :], X0[:, t, :], ACT.Copy, scale=rstd[:, 0, t:t + 1]).then_inc(s_x_normed, 1)
        product_sums(pool_sums(ADA_EARLY + 4), pool_sums(2 * ADA_EARLY))
        act.wait_ge(s_gain_columns, 1)
        for k in range(KT):
            act.wait_ge(s_x_transposed, k + 1)
            if k >= 2:
                act.wait_ge(s_h_lo, k - 1)
            ps = (psS, psT)[k % 2]
            A_.activation(HS0[:, k % 2, 0:CTX], ps[:, 0:CTX], ACT.Identity, bias=mod[:, k, 1:2],
                          scale=gain[:, 0, k, 1:2])
            A_.activation(HS0[:, k % 2, CTX:TOK], ps[:, CTX:TOK], ACT.Identity, bias=mod[:, k, 0:1],
                          scale=gain[:, 0, k, 0:1]).then_inc(s_h_scaled, 1)

        def q_ctx(e, norm, scale):
            act.wait_ge(s_q_ctx_proj, e + 1)
            if not (isinstance(e, int) and e == 0):
                act.wait_ge(s_q_lo, e)
            if norm:
                A_.activation(SQ[:, 0:CTX], psC[:, 0:CTX], ACT.Square)
            A_.activation(QR[:, 0:CTX], psC[:, 0:CTX], ACT.Identity, scale=scale).then_inc(s_q_ctx_evacuated, 1)

        def q_lat(e, norm, scale):
            act.wait_ge(s_q_lat_proj, e + 1)
            if norm:
                A_.activation(SQ[:, CTX:TOK], psL[0][:, :], ACT.Square)
            A_.activation(QR[:, CTX:TOK], psL[0][:, :], ACT.Identity, scale=scale).then_inc(s_q_lat_evacuated, 1)

        def q_hi(e, par):
            act.wait_ge(s_rope_step, e + 1)
            A_.activation(Qhi[:, par, :], QR[:], ACT.Copy).then_inc(s_q_hi, 1)

        def gate_ctx(e):
            act.wait_ge(s_g_ctx_proj, e + 1)
            A_.activation(TH[:, 0:CTX], psC[:, 0:CTX], ACT.Tanh, scale=0.5).then_inc(s_tanh_ctx, 1)

        def gate_lat(e):
            act.wait_ge(s_g_lat_proj, e + 1)
            A_.activation(TH[:, CTX:TOK], psL[1][:, :], ACT.Tanh, scale=0.5).then_inc(s_tanh_lat, 1)

        for w in range(2):
            weight_hi(0, w, w, USES_ADA + 1)
        act.wait_ge(s_h_lo, KT)
        late_sums(0, LATE_AHEAD)
        for g in range(GROUPS):
            norm = g >= 2
            scale = col("k_norm") if norm else 1.0
            q_ctx(g, norm, scale)
            q_lat(g, norm, scale)
            weight_hi(g + 1, 0, 0, USES_ADA + g + 2)
            cut = LATE_START[g] + LATE_SHARE[g][0]
            act.wait_ge(s_g_ctx_proj, g + 1)
            if g:
                act.wait_ge(s_v_transposed, g)
            A_.activation(TH[:, 0:CTX], psC[:, 0:CTX], ACT.Copy).then_inc(s_tanh_ctx, 1)
            act.wait_ge(s_g_lat_proj, g + 1)
            A_.activation(TH[:, CTX:TOK], psL[1][:, :], ACT.Copy).then_inc(s_tanh_lat, 1)
            weight_hi(g + 1, 1, 1, USES_ADA + g + 2)
            late_sums(LATE_START[g], cut)
            act.wait_ge(s_v_transposed, g + 1)
            A_.activation(Vhi[:, :, g * P:(g + 1) * P], psT[:, 0:TOK].rearrange("p (t d) -> p t d", t=TT),
                          ACT.Copy).then_inc(s_v_hi, 1)
            if norm:
                act.wait_ge(s_k_normed, g - 1)
            else:
                act.wait_ge(s_rope_step, g + 1)
            A_.activation(Khi[:, g, :], QR[:], ACT.Copy).then_inc(s_q_hi, 1)
            late_sums(cut, LATE_START[g + 1])
        q_ctx(GROUPS, False, 1.0)
        q_lat(GROUPS, False, 1.0)
        gate_ctx(GROUPS)
        gate_lat(GROUPS)
        q_hi(GROUPS, 0)
        for c in range(2):
            weight_hi(W_HEAD0 // 2 + 1, c, c, USES_HEAD0 + 2)

        def attention(r, last):
            for s in range(SLOTS + 3):
                n = SLOTS * r + s
                if (hs := due(s, 6, 8)) is not None and not (last and hs == GROUPS - 1):
                    gate_lat(GROUPS + GROUPS * r + hs + 1)
                if s < SLOTS:
                    hs, b = s // BLOCKS, s % BLOCKS
                    banded, (lo, hi, a) = hs < 2, window(b, hs < 2)
                    act.wait_ge(s_neg_max, n + 1)
                    if s >= 2:
                        act.wait_ge(s_probs_transposed, n - 1)
                        act.wait_ge(s_inv_denominator, n - 1)
                    A_.activation(PR[:, s % 2, a:TOK], psS[:, a:TOK], ACT.Exp, bias=nmax[:, s % 2:s % 2 + 1],
                                  scale=SCALE if banded else rq[:, hs % 2, b:b + 1],
                                  accum_out=esum[:, s % 2:s % 2 + 1]).then_inc(s_probs, 1)
                    if banded:
                        A_.activation(esink[:, s % 2:s % 2 + 1], rowt[:, ds(2 * r + hs, 1)], ACT.Exp,
                                      bias=nmax[:, s % 2:s % 2 + 1]).then_inc(s_sink_exp, 1)
                if 1 <= s <= SLOTS:
                    pb = (s - 1) % BLOCKS
                    lo, hi, a = window(pb, (s - 1) // BLOCKS < 2)
                    act.wait_ge(s_probs_transposed, n)
                    if pb % 2 == 0 and s > 1:
                        act.wait_ge(s_pv_done, PAIRS * GROUPS * r + (s - 1) // 2)
                    A_.activation(PThi[:, a // P:TT, (pb % 2) * P:(pb % 2 + 1) * P],
                                  psT[:, a:TOK].rearrange("p (t q) -> p t q", q=P), ACT.Copy).then_inc(s_probs_t_hi, 1)
                if s < SLOTS and s % BLOCKS in (2, 4):
                    hs, v = s // BLOCKS, s % BLOCKS // 2 - 1
                    act.wait_ge(s_modulation_product, POOL_LATE + 2 * GROUPS * r + 2 * hs + v + 1)
                    if hs == 0 and v == 0 and not (isinstance(r, int) and r == 0):
                        act.wait_ge(s_late_modulation_columns, r + 1)
                    A_.activation(product0[:], product0[:], ACT.Copy, scale=0.5,
                                  accum_out=modp[:, hs, v:v + 1]).then_inc(s_modulation_product_summed, 1)
                if (hs := due(s, 2, 2)) is not None and not (last and hs == GROUPS - 1):
                    norm = (hs + 1) % GROUPS >= 2
                    q_ctx(GROUPS + GROUPS * r + hs + 1, norm, col("q_norm") if norm else 1.0)
                if (hs := due(s, 3, 4)) is not None and not (last and hs == GROUPS - 1):
                    norm = (hs + 1) % GROUPS >= 2
                    q_lat(GROUPS + GROUPS * r + hs + 1, norm, col("q_norm") if norm else 1.0)
                if (hs := due(s, 4, 5)) is not None and not (last and hs == GROUPS - 1):
                    gate_ctx(GROUPS + GROUPS * r + hs + 1)
                    q_hi(GROUPS + GROUPS * r + hs + 1, (hs + 1) % 2)
                    weight_hi(W_HEAD0 // 2 + GROUPS * r + hs + 2, 0, 0, USES_HEAD0 + GROUPS * r + hs + 3)
                if (hs := due(s, 7, 8)) is not None and not (last and hs == GROUPS - 1):
                    weight_hi(W_HEAD0 // 2 + GROUPS * r + hs + 2, 1, 1, USES_HEAD0 + GROUPS * r + hs + 3)

        with act.Fori(0, HEADS // GROUPS - 1) as r:
            attention(r, False)
        attention(HEADS // GROUPS - 1, True)

        def y_load(k):
            if k >= 2:
                act.wait_ge(s_y_lo, k - 1)
            act.wait_ge(s_y_stored, 16 * (k + 1) + STORED)
            act.dma_start(Yraw[:, k % 2, :], io["y_spill"][k]).then_inc(s_y_loaded[k % 2], 16)

        act.wait_ge(s_g_lat_proj, GROUPS + HEADS)
        y_load(0)
        y_load(1)
        def out_squares(layer, nh, t, yo, junk):
            n = OUT_HALF[layer] + nh * OUT_TILES[layer] + t
            if nh == 0:
                act.wait_ge(s_out_evacuated, OUT_YO[layer] + t + 1)
            else:
                act.wait_ge(s_out_half, n + 1)
            if nh or t:
                act.wait_ge(s_out_squares, n)
            A_.activation(junk[:], yo[:, t, 0:512] if nh == 0 else tok_bank[t], ACT.Square,
                          accum_out=ssq[:, 1 + nh, t:t + 1]).then_inc(s_out_squares, 1)

        def x_squares(t):
            act.wait_ge(s_residual, 2 * t + 2)
            if t:
                act.wait_ge(s_sum_of_squares, TT + t)
            A_.activation(psT[:, :], X1[:, t, :], ACT.Square, accum_out=ssq[:, 0, t:t + 1]).then_inc(s_sum_of_squares, 1)

        def out_hi(c):
            weight_hi((W_OUT0 + c) // 2, c % 2, c % NR, USES_OUT0[c % NR] + c // NR + 1)

        for nh in range(2):
            for c in range(KT):
                if 2 <= nh * KT + c and not (nh == 1 and c < 2):
                    out_hi(nh * KT + c)
                if nh == 0:
                    for k in (2 * c, 2 * c + 1):
                        if k == 4:
                            act.wait_ge(s_pv_done, PAIRS * HEADS)
                            act.wait_ge(s_y_gated, PAIRS * HEADS)
                            act.wait_ge(s_y_stored, 16 * HEADS + STORED)
                        act.wait_ge(s_y_loaded[k % 2], 16 * (k // 2 + 1))
                        A_.activation(Yhi[:, k, :], Yraw[:, k % 2, :], ACT.Copy).then_inc(s_y_hi, 1)
                        if 1 <= k < HEADS - 1:
                            y_load(k + 1)
                if nh == 0 and c in (5, 7):
                    v = (c - 5) // 2
                    act.wait_ge(s_gate_diag_used, KT * (v + 1))
                    A_.activation(grow[:, v, :], psT[:, :], ACT.Copy).then_inc(s_gate_rows_out, 1)
            if nh == 0:
                out_hi(KT)
                out_hi(KT + 1)
            for t in range(TT):
                out_squares(0, nh, t, Yo, junk1)
                if nh == 1 and t >= 2:
                    x_squares(t - 2)

        x_squares(TT - 2)
        act.wait_ge(s_out_half, 2 * TT)
        for b, (t0, t1) in enumerate(NORM_BATCHES):
            act.wait_ge(s_rstd, TT + 2 + b)
            for t in range(t0, t1):
                A_.activation(XN[:, t, :], X1[:, t, :], ACT.Copy, scale=rstd[:, 2, t:t + 1]).then_inc(s_x_normed, 1)
            if b == 0:
                x_squares(TT - 1)
        H2_ = 2 * SSM_HEADS

        def ssm_hi(q, q3, q2):
            act.wait_ge(s_raw_weights_loaded[q3], 16 * (USES_SSM[q3] + 1) + 16 * q)
            A_.activation(whi[:, q2], wraw[:, q3], ACT.Copy).then_inc(s_weight_hi, 1)

        act.wait_ge(s_raw_weights_loaded[NR - 1], 16 * (USES_SSM[NR - 1] + 1))
        chunk_done(act, 0, 2 * KT - 2)
        A_.activation(whi[:, 0, :, 0:H2_], wraw[:, NR - 1, :, 0:H2_], ACT.Copy).then_inc(s_weight_hi, 1)
        chunk_done(act, 0, 2 * KT - 1)
        ssm_hi(0, 0, 1)
        act.wait_ge(s_gain_columns, 2)
        for k in range(KT):
            act.wait_ge(s_x_transposed, KT + k + 1)
            if k >= 2:
                act.wait_ge(s_h_lo, KT + k - 1)
            ps = (psS, psT)[k % 2]
            A_.activation(HS1[:, k % 2, 0:CTX], ps[:, 0:CTX], ACT.Identity, bias=mod[:, ADA + k, 1:2],
                          scale=gain[:, 1, k, 1:2])
            A_.activation(HS1[:, k % 2, CTX:TOK], ps[:, CTX:TOK], ACT.Identity, bias=mod[:, ADA + k, 0:1],
                          scale=gain[:, 1, k, 0:1]).then_inc(s_h_scaled, 1)

        act.wait_ge(s_dt_projected, 1)
        A_.activation(CTH[0:H2_, 0:CTX], psC[0:H2_, 0:CTX], ACT.Copy)
        A_.activation(CTH[0:H2_, CTX:TOK], psL[0][0:H2_, :], ACT.Copy).then_inc(s_dt_evacuated, 1)
        ssm_hi(0, 1, 0)
        act.wait_ge(s_dt_step, 2)
        A_.activation(dt_e, dt_nx, ACT.Exp).then_inc(s_dt_step, 1)
        act.wait_ge(s_dt_step, 4)
        A_.activation(dt_l, dt_u, ACT.Ln).then_inc(s_dt_step, 1)
        act.wait_ge(s_rows_loaded, 16)
        A_.activation(rows1[:, 0:H2_], rows1[:, 0:H2_], ACT.Exp).then_inc(s_dt_step, 1)
        def conv_ctx(g, i):
            act.wait_ge(s_tile_ctx_projected, 3 * g + i + 1)
            A_.activation(U[i][:, 0:CTX], psC[:, 0:CTX], ACT.Identity, bias=tap(3, i),
                          scale=tap(1, i)).then_inc(s_conv_mid_ctx, 1)

        act.wait_ge(s_a_split, 1)
        A_.activation(ahi[:], dt_a, ACT.Copy).then_inc(s_a_split, 1)
        act.wait_ge(s_halved_columns, 3)
        conv_ctx(0, 0)
        A_.activation(dt_u, dt_u, ACT.Ln).then_inc(s_dt_step, 1)
        act.wait_ge(s_running_sums, 1)
        cF = psL[1][:, 0:TT * H2_].rearrange("p (t h) -> p t h", t=TT)
        cT = psS[:, 0:TT * H2_].rearrange("p (t h) -> p t h", t=TT)
        A_.activation(acu[:], cF, ACT.Copy)
        A_.activation(TAB[:, R_EA:R_EA + LT, :], cF[:, CT:TT, :], ACT.Exp)
        for i in range(STEPS):
            A_.activation(TAB[:, R_DEC + i, 0:SSM_HEADS], cT[:, FWD[i], 0:SSM_HEADS], ACT.Exp)
            last = A_.activation(TAB[:, R_DEC + i, SSM_HEADS:H2_], cT[:, BWD[i], SSM_HEADS:H2_], ACT.Exp)
        last.then_inc(s_running_sums, 1)
        act.wait_ge(s_running_sums, 3)
        A_.activation(dt_l, dt_nx, ACT.Exp).then_inc(s_running_sums, 1)

        def conv_lat(g, i):
            act.wait_ge(s_tile_lat_projected, 4 * g + i + 1)
            A_.activation(lat(U[i], i), psL[i % 2][:, :], ACT.Identity, bias=tap(3, i),
                          scale=tap(1, i)).then_inc(s_conv_mid_lat, 1)

        def conv_tanh(g, i, first=False):
            act.wait_ge(s_conv_lat, 4 * g + i + 1)
            act.wait_ge(s_conv_ctx, 3 * g + min(i, 2) + 1)
            if not first:
                act.wait_ge(s_conv_done, 4 * g + i)
            A_.activation(CTH[:, 0:SEQ if i == 3 else TOK], U[i], ACT.Tanh).then_inc(s_conv_tanh, 1)

        for i in range(4):
            if 0 < i < 3:
                conv_ctx(0, i)
            conv_lat(0, i)
            if i < 2:
                ssm_hi(0 if i == 0 else 1, (2 + i) % 3, (1 + i) % 2)
            elif i == 2:
                ssm_hi(1, 1, 1)
            else:
                ssm_hi(1, 2, 0)
            conv_tanh(0, i, first=i == 0)

        def squares(g, c):
            act.wait_ge(s_y_gated1, LT * g + c + 1)
            A_.activation(y1[:, 0:GW], yg, ACT.Square, accum_out=yss[:, 0:1]).then_inc(s_y_squares, 1)

        def y_norm(g, c):
            act.wait_ge(s_y_rstd, LT * g + c + 1)
            A_.activation(ynm[:], yg, ACT.Copy, scale=yrs[:, 0:1]).then_inc(s_y_normed, 1)

        def y_out(g, c):
            act.wait_ge(s_y_transposed, LT * g + c + 1)
            if c == 0:
                act.wait_ge(s_group_norm_columns, g + 1)
                act.wait_ge(s_y1_stored, 16 * g + 16)
            for i in range(2):
                last = A_.activation(YT[:, i, c * P:(c + 1) * P], psV[:, i * P:(i + 1) * P], ACT.Copy,
                                     scale=gnorm[:, i:i + 1])
            last.then_inc(s_y_out, 1)

        def decays(g, c):
            act.wait_ge(s_log_decays, LT * g + c + 1)
            if c:
                act.wait_ge(s_decays_summed, LT * g + c)
            for d in range(DIRS):
                for h in range(GH):
                    x = slice((d * GH + h) * P, (d * GH + h + 1) * P)
                    last = A_.activation(E[:, x], psT[:, x], ACT.Exp, bias=GP[:, R_LOG + c, d, h:h + 1])
            last.then_inc(s_decays, 1)

        def weighted_hi(g, i):
            act.wait_ge(s_x_weighted, STEPS * g + i + 1)
            A_.activation(xwhi[:, i % 2], xw[:, i % 2], ACT.Copy).then_inc(s_x_weighted_hi, 1)

        def cb_hi(g, c):
            act.wait_ge(s_cb_decayed, LT * g + c + 1)
            if c:
                act.wait_ge(s_y_chunk, LT * g + c)
            A_.activation(Mhi[:], Mf[:], ACT.Copy).then_inc(s_cb_decayed_hi, 1)

        def ssd(g, last):
            G = g + 1
            ps = psT[:, 0:TOK].rearrange("p (t d) -> p t d", t=TT)
            for i in range(3):
                act.wait_ge(s_tokens_transposed, 3 * g + i + 1)
                A_.activation(xt[:, :, i * P:(i + 1) * P] if i < 2 else bthi[:], ps, ACT.Copy).then_inc(s_tokens_out, 1)
            act.wait_ge(s_tokens_out, 3 * g + 2)
            A_.activation(xthi[:], xt[:, CT:TT, :], ACT.Copy).then_inc(s_tokens_hi, 1)
            weighted_hi(g, 0)
            weighted_hi(g, 1)
            act.wait_ge(s_z_weight_used, 2 * g + 1)
            if not last:
                ssm_hi(2 * g + 2, 0, 1)
            act.wait_ge(s_conv_done, 4 * g + 4)
            A_.activation(bfhi[:, 0, :], U[2][:, CTX:TOK], ACT.Copy)
            A_.activation(bfhi[:, 1, :], U[3], ACT.Copy).then_inc(s_bc_hi, 1)
            act.wait_ge(s_z_weight_used, 2 * g + 2)
            A_.activation(thz[:], psS[:, :], ACT.Tanh, scale=0.5).then_inc(s_z_tanh, 1)
            act.wait_ge(s_group_columns, g + 1)
            decays(g, 0)
            for i in range(STEPS):
                if i + 2 < STEPS:
                    act.wait_ge(s_state_added, STEPS * g + i + 1)
                    weighted_hi(g, i + 2)
                if i:
                    act.wait_ge(s_state_new, STEPS * g + i + 1)
                    A_.activation(Hhi[:, i - 1, 0, :], hcur[:, 0:GW], ACT.Copy)
                    A_.activation(Hhi[:, LT - i, 1, :], hcur[:, GW:2 * GW], ACT.Copy).then_inc(s_state_hi, 1)
                if i == 0 and not last:
                    ssm_hi(2 * g + 2, 1, 0)
                elif i == 0:
                    for c in range(2):
                        act.wait_ge(s_raw_weights_loaded[c], 16 * (USES_OUT1[c] + 1))
                        A_.activation(whi[:, (W_OUT1 + c) % 2], wraw[:, c], ACT.Copy).then_inc(s_weight_hi, 1)
                if i == 2 and not last:
                    act.wait_ge(s_halved_columns, G + 3)
                    conv_ctx(G, 0)
                if i == 2:
                    cb_hi(g, 0)
                if i == 3:
                    decays(g, 1)
                if i == 4 and not last:
                    conv_lat(G, 0)
            if not last:
                conv_ctx(G, 1)
                conv_tanh(G, 0)
                ssm_hi(2 * g + 2, 2, 1)
            for c in range(LT):
                if c < LT - 1:
                    cb_hi(g, c + 1)
                if c < LT - 2:
                    decays(g, c + 2)
                if c == 1 and not last:
                    conv_lat(G, 1)
                    ssm_hi(2 * g + 3, 0, 0)
                if c == 2 and not last:
                    conv_ctx(G, 2)
                    conv_tanh(G, 1)
                if c == 3 and not last:
                    conv_lat(G, 2)
                    ssm_hi(2 * g + 3, 1, 1)
                if c:
                    y_out(g, c - 1)
                squares(g, c)
                y_norm(g, c)
            if not last:
                conv_tanh(G, 2)
                conv_lat(G, 3)
            y_out(g, LT - 1)
            if not last:
                ssm_hi(2 * g + 3, 2, 0)
                conv_tanh(G, 3)

        with act.Fori(0, SSM_GROUPS - 1) as g:
            ssd(g, False)
        ssd(SSM_GROUPS - 1, True)

        def y1_load(k):
            if k >= 2:
                act.wait_ge(s_y_lo, HEADS + k - 1)
            act.wait_ge(s_y1_stored, 16 * (k // 2 + 1) + 16)
            act.dma_start(Y1raw[:, k % 2, :], io["y1_spill"][k // 2, :, k % 2, :]).then_inc(s_y1_loaded[k % 2], 16)

        def out1_hi(i):
            act.wait_ge(s_raw_weights_loaded[i % NR], 16 * (USES_OUT1[i % NR] + i // NR + 1))
            chunk_done(act, 1, i - 2)
            A_.activation(whi[:, (W_OUT1 + i) % 2], wraw[:, i % NR], ACT.Copy).then_inc(s_weight_hi, 1)

        act.wait_ge(s_z_weight_used, 2 * SSM_GROUPS)
        y1_load(0)
        y1_load(1)
        for nh in range(2):
            for c in range(KT):
                i = nh * KT + c
                if i >= 2 and not (nh == 1 and c < 2):
                    out1_hi(i)
                if nh == 0:
                    for k in (2 * c, 2 * c + 1):
                        if k == 10:
                            act.wait_ge(s_y1_stored, 16 * SSM_GROUPS + 16)
                        act.wait_ge(s_y1_loaded[k % 2], 16 * (k // 2 + 1))
                        A_.activation(Y1hi[:, k, :], Y1raw[:, k % 2, :], ACT.Copy).then_inc(s_y_hi, 1)
                        if 1 <= k < HEADS - 1:
                            y1_load(k + 1)
                if nh == 0 and c == 5:
                    act.wait_ge(s_gate1_rows, KT)
                    A_.activation(grow1[:], psT[:, :], ACT.Copy).then_inc(s_gate1_rows_out, 1)
            if nh == 0:
                out1_hi(KT)
                out1_hi(KT + 1)
            for t in range(LT):
                out_squares(1, nh, t, Yo1, junk3)

    @block.vector
    def _(dve):
        dve.wait_ge(s_silu_c_step, 1)
        V_.scalar_tensor_tensor(csilu[:], cth[:], 1.0, csilu[:], ALU.add, ALU.mult).then_inc(s_silu_c_step, 1)

        def modulation(tile):
            for v in range(2):
                n = 2 * tile + v
                if n % 3 == 2:
                    continue
                place, loaded, count = ada_slot(tile)
                dve.wait_ge(loaded, count)
                if n:
                    dve.wait_ge(s_modulation_tile_done, dve_sums(n))
                V_.tensor_tensor_reduce(out=product, in0=place, in1=csilu[:, v, :], scale=0.5, scalar=0.0,
                                        op0=ALU.mult, op1=ALU.add, accum_out=mod[:, tile, v:v + 1]).then_inc(s_modulation_tile_done, 1)

        dve.wait_ge(s_silu_c_step, 2)
        for t in range(ADA_EARLY):
            if t == ADA_EARLY // 2:
                dve.wait_ge(s_sum_of_squares, TT)
                V_.tensor_scalar(vvar[:, 0, 0:TT], ssq[:, 0, 0:TT], 1.0 / D_MODEL, EPS, ALU.mult,
                                 ALU.add).then_inc(s_variance, 1)
            modulation(t)
        dve.wait_ge(s_modulation_tile_done, dve_sums(2 * ADA_EARLY))
        dve.wait_ge(s_modulation_product_summed, pool_sums(2 * ADA_EARLY))
        V_.tensor_tensor(mod[:, 0:ADA_EARLY, :], mod[:, 0:ADA_EARLY, :],
                         bcast2(col("b_ada", 0, ADA_EARLY), ADA_EARLY), ALU.add).then_inc(s_modulation_columns, 1)
        dve.wait_ge(s_modulation_columns, 1)
        V_.scalar_tensor_tensor(gain[:, 0], mod[:, KT:2 * KT, :], 1.0, bcast2(col("pre", 0, KT), KT),
                                ALU.add, ALU.mult).then_inc(s_gain_columns, 1)
        for k in range(KT):
            dve.wait_ge(s_h_scaled, k + 1)
            V_.tensor_copy(hhi[:, k, :], HS0[:, k % 2, :]).then_inc(s_h_hi, 1)
            dve.wait_ge(s_h_hi, k + 1)
            V_.tensor_tensor(hlo[:, k, :], HS0[:, k % 2, :], f(hhi[:, k, :]), ALU.subtract).then_inc(s_h_lo, 1)

        H2 = P // 2

        def rope(e):
            dve.wait_ge(s_q_lat_evacuated, e + 1)
            x = QR[:, CTX:TOK]
            V_.tensor_tensor(T1[:], x, costab[:], ALU.mult).then_inc(s_rope_cos_part, 1)
            V_.tensor_tensor(T2[0:H2, :], x[H2:P, :], sintab[H2:P, :], ALU.mult)
            V_.tensor_tensor(T2[H2:P, :], x[0:H2, :], sintab[0:H2, :], ALU.mult).then_inc(s_rope_sin_part, 1)
            dve.wait_ge(s_rope_cos_part, e + 1)
            dve.wait_ge(s_rope_sin_part, e + 1)
            V_.tensor_tensor(x, T1[:], T2[:], ALU.add).then_inc(s_rope_step, 1)

        def variance(u, factor=1.0):
            dve.wait_ge(s_qk_square_sums, u + 1)
            V_.tensor_scalar(vq[:], psV[:, 0:TT], factor / P, factor * EPS, ALU.mult,
                             ALU.add).then_inc(s_qk_variance, 1)

        def gate(e, par, part):
            if part == 0:
                dve.wait_ge(s_tanh_ctx, e + 1)
                V_.scalar_tensor_tensor(SG[:, par, 0:CTX], TH[:, 0:CTX], 1.0, psC[:, 0:CTX], ALU.add,
                                        ALU.mult).then_inc(s_gate_ctx, 1)
            else:
                dve.wait_ge(s_tanh_lat, e + 1)
                V_.scalar_tensor_tensor(SG[:, par, CTX:TOK], TH[:, CTX:TOK], 1.0, psL[1][:, :], ALU.add,
                                        ALU.mult).then_inc(s_gate_lat, 1)

        dve.wait_ge(s_tables_loaded, 48)
        V_.tensor_scalar(nsink[:], rowt[:], -1.0, None, ALU.mult).then_inc(s_neg_sink, 1)
        def late_modulation(n0, n1):
            for n in range(n0, n1):
                modulation(ADA_EARLY + n)

        late_modulation(0, LATE_AHEAD)
        for g in range(GROUPS):
            vals = slice(g * P, (g + 1) * P)
            rope(g)
            cut = LATE_START[g] + LATE_SHARE[g][0]
            late_modulation(LATE_START[g], cut)
            if g >= 2:
                variance(g - 2)
                dve.wait_ge(s_qk_rstd, g - 1)
                for t in range(TT):
                    last = V_.tensor_scalar(dgk[:, t, :], ident[:], rq[:, g % 2, t:t + 1], None, ALU.mult)
                last.then_inc(s_k_rstd_diag, 1)
            dve.wait_ge(s_v_hi, g + 1)
            V_.tensor_tensor(Vlo[:, :, vals], psT[:, 0:TOK].rearrange("p (t d) -> p t d", t=TT),
                             f(Vhi[:, :, vals]), ALU.subtract).then_inc(s_v_lo, 1)
            if g >= 2:
                dve.wait_ge(s_k_rstd_rows, g - 1)
                dve.wait_ge(s_rope_step, g + 1)
                V_.tensor_tensor(QR[:], QR[:], psT[:, 0:TOK], ALU.mult).then_inc(s_k_normed, 1)
            dve.wait_ge(s_q_hi, g + 1)
            V_.tensor_tensor(Klo[:, g, :], QR[:], f(Khi[:, g, :]), ALU.subtract).then_inc(s_q_lo, 1)
            late_modulation(cut, LATE_START[g + 1])
        dve.wait_ge(s_modulation_tile_done, dve_sums(2 * (ADA_EARLY + ADA_LATE)))
        dve.wait_ge(s_modulation_product_summed, POOL_LATE)
        V_.tensor_tensor(mod[:, ADA_EARLY:ADA_EARLY + ADA_LATE, :], mod[:, ADA_EARLY:ADA_EARLY + ADA_LATE, :],
                         bcast2(col("b_ada", ADA_EARLY, ADA_LATE), ADA_LATE), ALU.add).then_inc(s_late_modulation_columns, 1)
        rope(GROUPS)
        gate(GROUPS, 0, 0)
        gate(GROUPS, 0, 1)

        def attention(r, last):
            for s in range(SLOTS + 3):
                n = SLOTS * r + s
                skip = lambda hs: hs is None or (last and hs == GROUPS - 1)
                tile = lambda hs: GROUPS + GROUPS * r + hs + 1
                if not skip(hs := due(s, 5, 6)):
                    gate(tile(hs), (hs + 1) % 2, 0)
                if not skip(hs := due(s, 6, 8)):
                    gate(tile(hs), (hs + 1) % 2, 1)
                if s < SLOTS:
                    hs, b = s // BLOCKS, s % BLOCKS
                    banded, (lo, hi, a) = hs < 2, window(b, hs < 2)
                    p = slice(s % 2, s % 2 + 1)
                    dve.wait_ge(s_scores, n + 1)
                    V_.reduce_max(smax[:, p], psS[:, a:TOK], AX.X).then_inc(s_score_max, 1)
                    dve.wait_ge(s_score_max, n + 1)
                    if banded:
                        V_.tensor_scalar(nmax[:, p], smax[:, p], -SCALE, nsink[:, ds(2 * r + hs, 1)], ALU.mult,
                                         ALU.min).then_inc(s_neg_max, 1)
                    else:
                        if b == 0:
                            dve.wait_ge(s_qk_rstd, 2 * r + hs + 1)
                        V_.tensor_scalar(nmax[:, p], smax[:, p], rq[:, hs % 2, b:b + 1], -1.0, ALU.mult,
                                         ALU.mult).then_inc(s_neg_max, 1)
                if s < SLOTS:
                    hs, b = s // BLOCKS, s % BLOCKS
                    if hs < 2:
                        dve.wait_ge(s_sink_exp, 2 * BLOCKS * r + s + 1)
                        dve.wait_ge(s_probs, n + 1)
                        V_.tensor_tensor(eall[:, p], esum[:, p], esink[:, p], ALU.add).then_inc(s_denominator, 1)
                        dve.wait_ge(s_denominator, 2 * BLOCKS * r + s + 1)
                        V_.reciprocal(rinv[:, p], eall[:, p]).then_inc(s_inv_denominator, 1)
                    else:
                        dve.wait_ge(s_probs, n + 1)
                        V_.reciprocal(rinv[:, p], esum[:, p]).then_inc(s_inv_denominator, 1)
                    dve.wait_ge(s_inv_denominator, n + 1)
                    V_.tensor_scalar(PR[:, s % 2, a:TOK], PR[:, s % 2, a:TOK], rinv[:, p], 0.5, ALU.mult,
                                     ALU.mult).then_inc(s_probs_normed, 1)
                if not skip(hs := due(s, 4, 5)):
                    rope(tile(hs))
                if 1 <= s <= SLOTS:
                    pb = (s - 1) % BLOCKS
                    lo, hi, a = window(pb, (s - 1) // BLOCKS < 2)
                    q = slice((pb % 2) * P, (pb % 2 + 1) * P)
                    dve.wait_ge(s_probs_t_hi, n)
                    V_.tensor_tensor(PTlo[:, a // P:TT, q], psT[:, a:TOK].rearrange("p (t q) -> p t q", q=P),
                                     f(PThi[:, a // P:TT, q]), ALU.subtract).then_inc(s_probs_t_lo, 1)
                if s >= 3 and s % 2:
                    pair = (s - 3) // 2
                    hs, q = pair // PAIRS, pair % PAIRS
                    dve.wait_ge(s_pv_done, PAIRS * GROUPS * r + pair + 1)
                    if q == 0:
                        dve.wait_ge(s_y_stored, 16 * (GROUPS * r + hs + 1))
                    V_.tensor_tensor(Yst[:, hs % 2, q * 2 * P:(q + 1) * 2 * P], psV[:, 0:2 * P],
                                     SG[:, hs % 2, q * 2 * P:(q + 1) * 2 * P], ALU.mult).then_inc(s_y_gated, 1)
                if not skip(hs := due(s, 4, 5)) and (hs + 1) % GROUPS >= 2:
                    variance(2 * r + hs + 1, P)
                if s == SLOTS + 1:
                    dve.wait_ge(s_modulation_product_summed, POOL_LATE + 2 * GROUPS * (r + 1))
                    at = ADA_EARLY + ADA_LATE + GROUPS * r
                    V_.tensor_tensor(mod[:, ds(at, GROUPS), :], modp[:],
                                     bcast2(cols[:, ds(at + COLS["b_ada"][0], GROUPS)], GROUPS), ALU.add).then_inc(s_late_modulation_columns, 1)

        with dve.Fori(0, HEADS // GROUPS - 1) as r:
            attention(r, False)
        attention(HEADS // GROUPS - 1, True)

        def gate_columns(layer):
            V_.tensor_tensor(gcolx[:, layer], mod[:, layer * ADA + 2 * KT:layer * ADA + 3 * KT, :],
                             bcast2(col("post", layer * KT, KT), KT), ALU.mult).then_inc(s_gate_columns, 1)

        def gate_diag(layer, v, first):
            for k in range(KT):
                u = first + v * KT + k
                if u >= KT:
                    dve.wait_ge(s_gate_diag_used, u - KT + 1)
                V_.tensor_scalar(dg[:, k, :], ident[:], gcolx[:, layer, k, v:v + 1], None,
                                 ALU.mult).then_inc(s_gate_diag, 1)

        dve.wait_ge(s_late_modulation_columns, 1 + HEADS // GROUPS)
        gate_columns(0)
        dve.wait_ge(s_gate_columns, 1)
        for k in range(HEADS):
            dve.wait_ge(s_y_hi, k + 1)
            V_.tensor_tensor(Ylo[:, k, :], Yraw[:, k % 2, :], f(Yhi[:, k, :]), ALU.subtract).then_inc(s_y_lo, 1)
            if k in (7, 11):
                gate_diag(0, (k - 7) // 4, 0)
        def out_first_half(layer, yo):
            n = OUT_TILES[layer]
            for t in range(n):
                dve.wait_ge(s_out_half, OUT_HALF[layer] + t + 1)
                V_.tensor_copy(yo[:, t, 0:512], tok_bank[t]).then_inc(s_out_evacuated, 1)
            dve.wait_ge(s_out_squares, OUT_HALF[layer] + n)
            V_.tensor_scalar(ssq[:, 3, 0:n], ssq[:, 1, 0:n], 1.0 / D_MODEL, EPS, ALU.mult, ALU.add).then_inc(s_variance, 1)
            dve.wait_ge(s_variance, OUT_VAR[layer] + 1)

        def out_variance(layer, t):
            dve.wait_ge(s_out_squares, OUT_HALF[layer] + OUT_TILES[layer] + t + 1)
            V_.scalar_tensor_tensor(vvar[:, 1 + 2 * layer, t:t + 1], ssq[:, 2, t:t + 1], 1.0 / D_MODEL, ssq[:, 3, t:t + 1],
                                    ALU.mult, ALU.add).then_inc(s_variance, 1)

        def out_scaled(layer, t, yo, gate_row):
            dve.wait_ge(s_rstd, OUT_RSTD[layer] + t + 1)
            r = rstd[:, 1 + 2 * layer, t:t + 1]
            V_.scalar_tensor_tensor(yo[:, t, 0:512], yo[:, t, 0:512], r, gate_row[:, 0:512], ALU.mult, ALU.mult)
            V_.scalar_tensor_tensor(yo[:, t, 512:1024], tok_bank[t], r, gate_row[:, 512:1024], ALU.mult,
                                    ALU.mult).then_inc(s_residual, 1)

        def out_added(layer, t, x, yo):
            dve.wait_ge(s_residual, OUT_RES[layer] + 2 * t + 1)
            V_.tensor_tensor(x[:, t, :], x[:, t, :], yo[:, t, :], ALU.add).then_inc(s_residual, 1)

        def norm_variance(t0, t1):
            dve.wait_ge(s_sum_of_squares, TT + t1)
            V_.tensor_scalar(vvar[:, 2, t0:t1], ssq[:, 0, t0:t1], 1.0 / D_MODEL, EPS, ALU.mult, ALU.add).then_inc(s_variance, 1)

        out_first_half(0, Yo)
        dve.wait_ge(s_gate_rows_out, 2)
        dve.wait_ge(s_x_reloaded, 16 * TT)
        out_variance(0, 0)
        for t in range(TT):
            out_scaled(0, t, Yo, grow[:, int(t < CT), :])
            if t < TT - 1:
                out_variance(0, t + 1)
            else:
                norm_variance(*NORM_BATCHES[0])
            out_added(0, t, X1, Yo)

        norm_variance(*NORM_BATCHES[1])
        V_.scalar_tensor_tensor(gain[:, 1], mod[:, ADA + KT:ADA + 2 * KT, :], 1.0, bcast2(col("pre", KT, KT), KT),
                                ALU.add, ALU.mult).then_inc(s_gain_columns, 1)
        gate_columns(1)
        for k in range(KT):
            dve.wait_ge(s_h_scaled, KT + k + 1)
            V_.tensor_copy(h1hi[:, k, :], HS1[:, k % 2, :]).then_inc(s_h_hi, 1)
            dve.wait_ge(s_h_hi, KT + k + 1)
            V_.tensor_tensor(h1lo[:, k, :], HS1[:, k % 2, :], f(h1hi[:, k, :]), ALU.subtract).then_inc(s_h_lo, 1)
        dve.wait_ge(s_h_lo, KT + KT)
        V_.tensor_scalar(convh[:], cols[:, COLS["conv_w"][0]:COLS["conv_b"][1]], 0.5, None, ALU.mult).then_inc(s_halved_columns, 1)
        V_.tensor_scalar(normh[:], col("ssm_norm", 0, 16), 0.5, None, ALU.mult).then_inc(s_halved_columns, 1)
        def group_taps(g):
            at = convh[:].rearrange("p (j b g) -> p j b g", j=4, b=4)
            V_.tensor_copy(gtap[:, :, 0:2], convh[:].rearrange("p (j b) -> p j b", j=4)[:, :, ds(2 * g, 2)])
            V_.tensor_copy(gtap[:, :, 2:4], at[:, :, 2:4, ds(g, 1)].rearrange("p j b g -> p j (b g)")).then_inc(s_halved_columns, 1)

        dve.wait_ge(s_halved_columns, 2)
        group_taps(0)
        H2_ = 2 * SSM_HEADS

        def outer_taps(g, i, u, ps, n, mid, step, done, k):
            dve.wait_ge(mid, k + 1)
            V_.scalar_tensor_tensor(u[:, 1:n], ps[:, 0:n - 1], tap(0, i), u[:, 1:n], ALU.mult, ALU.add).then_inc(step, 1)
            dve.wait_ge(step, k + 1)
            V_.scalar_tensor_tensor(u[:, 0:n - 1], ps[:, 1:n], tap(2, i), u[:, 0:n - 1], ALU.mult,
                                    ALU.add).then_inc(done, 1)

        def taps_ctx(g, i):
            outer_taps(g, i, U[i], psC, CTX, s_conv_mid_ctx, s_conv_ctx_step, s_conv_ctx, 3 * g + i)

        def taps_lat(g, i):
            outer_taps(g, i, lat(U[i], i), psL[i % 2], SEQ, s_conv_mid_lat, s_conv_lat_step, s_conv_lat, 4 * g + i)

        def silu(g, i):
            dve.wait_ge(s_conv_tanh, 4 * g + i + 1)
            V_.scalar_tensor_tensor(U[i], CTH[:, 0:SEQ if i == 3 else TOK], 1.0, U[i], ALU.add, ALU.mult).then_inc(s_conv_done, 1)

        def rows_b(ap):
            return ap.unsqueeze(1).broadcast_to([P, TT, H2_])

        dve.wait_ge(s_rows_loaded, 16)
        dve.wait_ge(s_x1_stored, 16 * LT)
        dve.wait_ge(s_dt_projected, 2)
        V_.tensor_tensor(dt_x, psT[:, 0:TT * H2_].rearrange("p (t h) -> p t h", t=TT), rows_b(rows1[:, H2_:2 * H2_]),
                         ALU.add).then_inc(s_dt_step, 1)
        dve.wait_ge(s_dt_step, 1)
        V_.scalar_tensor_tensor(dt_nx, dt_x, -1.0, dt_x, ALU.mult, ALU.min).then_inc(s_dt_step, 1)
        dve.wait_ge(s_dt_step, 3)
        V_.tensor_scalar(dt_u, dt_e, 1.0, None, ALU.add).then_inc(s_dt_step, 1)
        dve.wait_ge(s_dt_step, 5)
        V_.scalar_tensor_tensor(dt_e, dt_u, -1.0, dt_e, ALU.add, ALU.subtract).then_inc(s_dt_correction, 1)
        V_.reciprocal(dt_nx, dt_u).then_inc(s_dt_correction, 1)
        dve.wait_ge(s_dt_correction, 2)
        V_.tensor_tensor(dt_e, dt_e, dt_nx, ALU.mult).then_inc(s_dt_correction, 1)
        dve.wait_ge(s_dt_correction, 3)
        V_.tensor_tensor(dt_l, dt_l, dt_e, ALU.subtract).then_inc(s_dt_correction, 1)
        dve.wait_ge(s_dt_correction, 4)
        V_.scalar_tensor_tensor(dt_x, dt_x, 0.0, dt_l, ALU.max, ALU.add).then_inc(s_dt_correction, 1)
        dve.wait_ge(s_dt_correction, 5)
        dve.wait_ge(s_dt_step, 6)
        V_.tensor_scalar(dt_u, dt_x, 1e-37, None, ALU.max)
        V_.tensor_copy(TAB[:, R_D, 0:SSM_HEADS], rows1[:, 2 * H2_:2 * H2_ + SSM_HEADS])
        V_.memset(TAB[:, R_D, SSM_HEADS:H2_], 0.0)
        V_.scalar_tensor_tensor(dt_a, dt_x, -1.0, rows_b(rows1[:, 0:H2_]), ALU.mult, ALU.mult).then_inc(s_a_split, 1)
        dve.wait_ge(s_a_split, 2)
        V_.tensor_tensor(alo[:], dt_a, f(ahi[:]), ALU.subtract).then_inc(s_a_split, 1)
        taps_ctx(0, 0)
        dve.wait_ge(s_running_sums, 2)
        V_.tensor_tensor(dt_nx, psS[:, 0:TT * H2_].rearrange("p (t h) -> p t h", t=TT), acu[:],
                         ALU.subtract).then_inc(s_running_sums, 1)
        dve.wait_ge(s_dt_step, 7)
        V_.tensor_tensor(TAB[:, R_LOG:R_LOG + LT, :], dt_u[:, CT:TT, :], acu[:, CT:TT, :], ALU.subtract)
        dve.wait_ge(s_running_sums, 4)
        for i in range(STEPS):
            V_.tensor_tensor(TAB[:, R_WE + i, 0:SSM_HEADS], dt_l[:, FWD[i], 0:SSM_HEADS], dt_x[:, FWD[i], 0:SSM_HEADS],
                             ALU.mult)
            last = V_.tensor_tensor(TAB[:, R_WE + i, SSM_HEADS:H2_], dt_l[:, BWD[i], SSM_HEADS:H2_],
                                    dt_x[:, BWD[i], SSM_HEADS:H2_], ALU.mult)
        last.then_inc(s_running_sums, 1)

        for i in range(4):
            if 0 < i < 3:
                taps_ctx(0, i)
            taps_lat(0, i)
            silu(0, i)

        def variance1(g, c):
            dve.wait_ge(s_y_squares, LT * g + c + 1)
            V_.tensor_scalar(yvv[:, 0:1], yss[:, 0:1], 0.25 / GW, EPS, ALU.mult, ALU.add).then_inc(s_y_variance, 1)

        def by_head(ap, n):
            return ap.rearrange("p (h x) -> p h x", x=n)

        def per_head(ap, d0, d1, n):
            return ap.rearrange("p d h -> p (d h)")[:, d0 * GH:d1 * GH].unsqueeze(2).broadcast_to([P, (d1 - d0) * GH, n])

        dve.wait_ge(s_running_sums, 5)

        def weighted_lo(g, i):
            dve.wait_ge(s_x_weighted_hi, STEPS * g + i + 1)
            V_.tensor_tensor(xwlo[:, i % 2], xw[:, i % 2], f(xwhi[:, i % 2]), ALU.subtract).then_inc(s_x_weighted_lo, 1)

        def decay_sum(g, c):
            dve.wait_ge(s_decays, LT * g + c + 1)
            V_.tensor_tensor(Wm[:], E[:, 0:GH * P], E[:, GH * P:2 * GH * P], ALU.add).then_inc(s_decays_summed, 1)

        def cb_times(g, c):
            dve.wait_ge(s_decays_summed, LT * g + c + 1)
            dve.wait_ge(s_cb_done, LT * g + c + 1)
            V_.tensor_tensor(by_head(Mf[:], P), by_head(Wm[:], P),
                             ybank[1][:, 0:P].unsqueeze(1).broadcast_to([P, GH, P]), ALU.mult).then_inc(s_cb_decayed, 1)

        def cb_lo(g, c):
            dve.wait_ge(s_cb_decayed_hi, LT * g + c + 1)
            V_.tensor_tensor(Mlo[:], Mf[:], f(Mhi[:]), ALU.subtract).then_inc(s_cb_decayed_lo, 1)

        def ssd(g, last):
            G = g + 1
            if not last:
                group_taps(G)
            V_.tensor_copy(GP[:], TAB[:].rearrange("p r (d h) -> p r d h", d=DIRS)[:, :, :, ds(GH * g, GH)]).then_inc(s_group_columns, 1)
            V_.tensor_copy(aghi[:], f(ahi[:]).rearrange("p t (d h) -> p t d h", d=DIRS)[:, CT:TT, :, ds(GH * g, GH)])
            V_.tensor_copy(aglo[:], f(alo[:]).rearrange("p t (d h) -> p t d h", d=DIRS)[:, CT:TT, :, ds(GH * g, GH)]).then_inc(s_group_a, 1)
            dve.wait_ge(s_tokens_hi, g + 1)
            V_.tensor_tensor(xtlo[:], xt[:, CT:TT, :], f(xthi[:]), ALU.subtract).then_inc(s_tokens_lo, 1)
            dve.wait_ge(s_tokens_out, 3 * g + 3)
            V_.tensor_tensor(btlo[:], psT[:, 0:TOK].rearrange("p (t d) -> p t d", t=TT), f(bthi[:]), ALU.subtract).then_inc(s_b_tokens_lo, 1)
            weighted_lo(g, 0)
            weighted_lo(g, 1)
            dve.wait_ge(s_bc_hi, g + 1)
            V_.tensor_tensor(bflo[:, 0, :], U[2][:, CTX:TOK], f(bfhi[:, 0, :]), ALU.subtract)
            V_.tensor_tensor(bflo[:, 1, :], U[3], f(bfhi[:, 1, :]), ALU.subtract).then_inc(s_bc_lo, 1)
            dve.wait_ge(s_z_tanh, g + 1)
            V_.scalar_tensor_tensor(sz, thz[:], 1.0, psS[:, :], ALU.add, ALU.mult).then_inc(s_z_silu, 1)
            dve.wait_ge(s_group_columns, g + 1)
            for i in range(STEPS):
                if i:
                    dve.wait_ge(s_state_new, STEPS * g + i)
                    V_.tensor_tensor(by_head(hdec[:], HD), by_head(hcur[:], HD), per_head(GP[:, R_DEC + i], 0, DIRS, HD),
                                     ALU.mult).then_inc(s_state_decayed, 1)
                    dve.wait_ge(s_state_decayed, (STEPS - 1) * g + i)
                dve.wait_ge(s_state_added, STEPS * g + i + 1)
                if i == 0:
                    V_.tensor_copy(hcur[:], ybank[0]).then_inc(s_state_new, 1)
                else:
                    if i > 1:
                        dve.wait_ge(s_state_lo, LT * g + i - 1)
                    V_.tensor_tensor(hcur[:], hdec[:], ybank[0], ALU.add).then_inc(s_state_new, 1)
                if i + 2 < STEPS:
                    weighted_lo(g, i + 2)
                if i == 0:
                    decay_sum(g, 0)
                    cb_times(g, 0)
                if i == 2:
                    cb_lo(g, 0)
                if i == 3 and not last:
                    taps_ctx(G, 0)
            if not last:
                taps_lat(G, 0)
                taps_ctx(G, 1)
            dve.wait_ge(s_y1_stored, 16 * g + 16)
            decay_sum(g, 1)
            V_.tensor_copy(gnorm[:], normh[:, ds(2 * g, 2)]).then_inc(s_group_norm_columns, 1)
            for c in range(LT):
                n = LT * g + c
                dve.wait_ge(s_x_d, n + 1)
                dve.wait_ge(s_y_chunk, n + 1)
                V_.tensor_tensor(y2, ybank[1][:, P:P + GW], xD[:, c % 2], ALU.add).then_inc(s_y_diag_d, 1)
                dve.wait_ge(s_y_off_done, n + 1)
                V_.tensor_tensor(by_head(y1, HD), by_head(ybank[0], HD), per_head(GP[:, R_EA + c], 0, DIRS, HD),
                                 ALU.mult).then_inc(s_y_off_scaled, 1)
                if c < LT - 1:
                    cb_times(g, c + 1)
                dve.wait_ge(s_y_off_scaled, n + 1)
                V_.tensor_tensor(y3, y1[:, 0:GW], y1[:, GW:2 * GW], ALU.add).then_inc(s_y_off_sum, 1)
                if c < LT - 1:
                    cb_lo(g, c + 1)
                dve.wait_ge(s_y_off_sum, n + 1)
                V_.tensor_tensor(y2, y2, y3, ALU.add).then_inc(s_y_sum, 1)
                dve.wait_ge(s_y_sum, n + 1)
                if c:
                    dve.wait_ge(s_y_normed, n)
                V_.tensor_tensor(yg, y2, sz[:, c * GW:(c + 1) * GW], ALU.mult).then_inc(s_y_gated1, 1)
                if c < LT - 2:
                    decay_sum(g, c + 2)
                variance1(g, c)
                if c == 0 and not last:
                    silu(G, 0)
                if c == 1 and not last:
                    taps_lat(G, 1)
                if c == 2 and not last:
                    silu(G, 1)
                    taps_ctx(G, 2)
            if not last:
                taps_lat(G, 2)
                silu(G, 2)
                taps_lat(G, 3)
                silu(G, 3)

        with dve.Fori(0, SSM_GROUPS - 1) as g:
            ssd(g, False)
        ssd(SSM_GROUPS - 1, True)

        for k in range(HEADS):
            dve.wait_ge(s_y_hi, HEADS + k + 1)
            V_.tensor_tensor(Y1lo[:, k, :], Y1raw[:, k % 2, :], f(Y1hi[:, k, :]), ALU.subtract).then_inc(s_y_lo, 1)
            if k == 7:
                for j in range(KT):
                    V_.tensor_scalar(dg1[:, j, :], ident[:], gcolx[:, 1, j, 0:1], None, ALU.mult).then_inc(s_gate1_diag, 1)
        out_first_half(1, Yo1)
        dve.wait_ge(s_gate1_rows_out, 1)
        dve.wait_ge(s_x1_reloaded, 16 * LT)
        out_variance(1, 0)
        for t in range(LT):
            out_scaled(1, t, Yo1, grow1[:])
            if t < LT - 1:
                out_variance(1, t + 1)
            out_added(1, t, X2, Yo1)

    @block.gpsimd
    def _(pool):
        G_.memset(half[:], -0.5).then_inc(s_y_stored, STORED)
        G_.memset(ones[:], 1.0).then_inc(s_constants_made, 1)
        G_.memset(ident[:], 0.0).then_inc(s_constants_made, 1)
        G_.memset(nothing[:], 0.0).then_inc(s_y1_stored, 16)
        pool.wait_ge(s_constants_made, 2)
        G_.affine_select(out=ident[:], in_=ident[:], compare_op=ALU.not_equal, fill=1.0, base=0,
                         pattern=[[-1, P]], channel_multiplier=1).then_inc(s_constants_made, 1)
        pool.wait_ge(s_constants_made, 3)
        G_.tensor_copy(identr[:], ident[:]).then_inc(s_constants_made, 1)

        def inv_sqrt(dst, src, n, done):
            G_.tensor_tensor(dst, src, half[:, 0:n], ALU.pow).then_inc(done, 1)

        def weight_lo(w, par, slot):
            pool.wait_ge(s_weight_hi, w + 1)
            G_.tensor_tensor(wlo[:, par], wraw[:, slot], f(whi[:, par]), ALU.subtract).then_inc(s_weight_lo, 1)

        def modulation(tile0, tile1):
            for n in range(2 * tile0, 2 * tile1):
                if n % 3 != 2:
                    continue
                j, (place, loaded, count) = n // 3, ada_slot(n // 2)
                pool.wait_ge(loaded, count)
                if j >= 2:
                    pool.wait_ge(s_modulation_product_summed, j - 1)
                G_.tensor_tensor(products[j % 2], place, csilu[:, n % 2, :], ALU.mult).then_inc(s_modulation_product, 1)

        pool.wait_ge(s_y_stored, STORED)
        pool.wait_ge(s_silu_c_step, 2)
        modulation(0, ADA_EARLY // 2 + 2)
        pool.wait_ge(s_variance, 1)
        inv_sqrt(rstd[:, 0, 0:TT], vvar[:, 0, 0:TT], TT, s_rstd)
        modulation(ADA_EARLY // 2 + 2, ADA_EARLY)
        weight_lo(0, 0, 0)
        weight_lo(1, 1, 1)
        pool.wait_ge(s_h_lo, KT)
        for m in range(2):
            sign = 1 - 2 * m
            G_.memset(T2[:, m * P:(m + 1) * P], 0.0).then_inc(s_band_masks, 1)
            pool.wait_ge(s_band_masks, 3 * m + 1)
            G_.affine_select(out=T2[:, m * P:(m + 1) * P], in_=T2[:, m * P:(m + 1) * P], compare_op=ALU.is_ge,
                             fill=MASKED, base=0, pattern=[[sign, P]], channel_multiplier=-sign).then_inc(s_band_masks, 1)
            pool.wait_ge(s_band_masks, 3 * m + 2)
            G_.tensor_copy(maskr[:, m, :], T2[:, m * P:(m + 1) * P]).then_inc(s_band_masks, 1)

        def qk_rstd(u, par):
            pool.wait_ge(s_qk_variance, u + 1)
            inv_sqrt(rq[:, par, :], vq[:], TT, s_qk_rstd)

        def q_lo(e, par):
            pool.wait_ge(s_q_hi, e + 1)
            G_.tensor_tensor(Qlo[:, par, :], QR[:], f(Qhi[:, par, :]), ALU.subtract).then_inc(s_q_lo, 1)

        modulation(ADA_EARLY, ADA_EARLY + LATE_AHEAD)
        for g in range(GROUPS):
            cut = ADA_EARLY + LATE_START[g] + LATE_SHARE[g][0]
            weight_lo(2 * g + 2, 0, 0)
            weight_lo(2 * g + 3, 1, 1)
            modulation(ADA_EARLY + LATE_START[g], cut)
            if g >= 2:
                qk_rstd(g - 2, g % 2)
            modulation(cut, ADA_EARLY + LATE_START[g + 1])
        q_lo(GROUPS, 0)
        for c in range(2):
            weight_lo(W_HEAD0 + 2 + c, c, c)

        def attention(r, last):
            for s in range(SLOTS + 3):
                n = SLOTS * r + s
                skip = lambda hs: hs is None or (last and hs == GROUPS - 1)
                if s < SLOTS and s % BLOCKS in (0, 2):
                    hs, v = s // BLOCKS, s % BLOCKS // 2
                    j = 2 * GROUPS * r + 2 * hs + v
                    if v == 0:
                        pool.wait_ge(s_raw_weights_loaded[2 + hs % 2], 16 * (USES_LAST[hs % 2] + hs // 2 + 1) + 16 * 2 * r)
                    pool.wait_ge(s_modulation_product_summed, POOL_LATE + j)
                    G_.tensor_tensor(product0[:], wraw[:, 2 + hs % 2].rearrange("p a b -> p (a b)"), csilu[:, v, :],
                                     ALU.mult).then_inc(s_modulation_product, 1)
                if not skip(hs := due(s, 4, 5)):
                    q_lo(GROUPS + GROUPS * r + hs + 1, (hs + 1) % 2)
                if not skip(hs := due(s, 5, 6)) and (hs + 1) % GROUPS >= 2:
                    qk_rstd(2 * r + hs + 1, (hs + 1) % 2)
                if not skip(hs := due(s, 4, 5)):
                    weight_lo(W_HEAD0 + 2 * (GROUPS * r + hs + 2), 0, 0)
                if not skip(hs := due(s, 7, 8)):
                    weight_lo(W_HEAD0 + 2 * (GROUPS * r + hs + 2) + 1, 1, 1)

        with pool.Fori(0, HEADS // GROUPS - 1) as r:
            attention(r, False)
        attention(HEADS // GROUPS - 1, True)
        for w in range(W_OUT0 + 2, W_OUT0 + 2 * KT):
            weight_lo(w, w % 2, (w - W_OUT0) % NR)

        def out_rstd(layer):
            for t in range(OUT_TILES[layer]):
                pool.wait_ge(s_variance, OUT_VAR[layer] + t + 2)
                inv_sqrt(rstd[:, 1 + 2 * layer, t:t + 1], vvar[:, 1 + 2 * layer, t:t + 1], 1, s_rstd)

        out_rstd(0)
        for b, (t0, t1) in enumerate(NORM_BATCHES):
            pool.wait_ge(s_variance, TT + 3 + b)
            inv_sqrt(rstd[:, 2, t0:t1], vvar[:, 2, t0:t1], t1 - t0, s_rstd)
        H2_ = 2 * SSM_HEADS
        pool.wait_ge(s_weight_hi, W_DT + 1)
        G_.tensor_tensor(wlo[:, 0, :, 0:H2_], wraw[:, NR - 1, :, 0:H2_], f(whi[:, 0, :, 0:H2_]),
                         ALU.subtract).then_inc(s_weight_lo, 1)
        weight_lo(W_SSM, 1, 0)
        pool.wait_ge(s_h_lo, KT + KT)
        G_.tensor_copy(onesr[:], ones[:]).then_inc(s_triangles, 1)
        tri = xt[:, 0, 0:P]
        n = 1
        for d in range(DIRS):
            sign = 1 - 2 * d
            for base, fill, dst in ((ones[:], 0.0, trir[:, d, :]), (None, MASKED, negr[:, d, :])):
                if base is None:
                    pool.wait_ge(s_triangles, n)
                    G_.memset(tri, 0.0).then_inc(s_triangles, 1)
                    n += 1
                    base = tri
                pool.wait_ge(s_triangles, n)
                G_.affine_select(out=tri, in_=base, compare_op=ALU.is_ge, fill=fill, base=0, pattern=[[sign, P]],
                                 channel_multiplier=-sign).then_inc(s_triangles, 1)
                pool.wait_ge(s_triangles, n + 1)
                G_.tensor_copy(dst, tri).then_inc(s_triangles, 1)
                n += 2
        for q in range(1, 6):
            weight_lo(W_SSM + q, (W_SSM + q) % 2, q % 3)

        def by_head(ap, n):
            return ap.rearrange("p (h x) -> p h x", x=n)

        def per_head(ap, n):
            return ap.unsqueeze(2).broadcast_to([P, ap.shape[1], n])

        def ssd(g, last):
            w = W_SSM + 6 + 6 * g
            G = g + 1
            pool.wait_ge(s_group_columns, g + 1)
            pool.wait_ge(s_tokens_out, 3 * g + 2)
            weighted(g, 0)
            weighted(g, 1)
            if not last:
                weight_lo(w, 1, 0)
            weighted(g, 2)
            weighted(g, 3)
            weighted(g, 4)
            if not last:
                weight_lo(w + 1, 0, 1)
            else:
                for c in range(2):
                    weight_lo(W_OUT1 + c, (W_OUT1 + c) % 2, c)
            for i in range(1, STEPS):
                state_lo(g, i)
            if not last:
                weight_lo(w + 2, 1, 2)
            for c in range(LT):
                n = LT * g + c
                if c == 0:
                    times_d(g, 0)
                if c < LT - 1:
                    times_d(g, c + 1)
                if c == 1 and not last:
                    weight_lo(w + 3, 0, 0)
                if c == 3 and not last:
                    weight_lo(w + 4, 1, 1)
                pool.wait_ge(s_y_variance, n + 1)
                inv_sqrt(yrs[:, 0:1], yvv[:, 0:1], 1, s_y_rstd)
            if not last:
                weight_lo(w + 5, 0, 2)

        def times_d(g, c):
            if c >= 2:
                pool.wait_ge(s_y_diag_d, LT * g + c - 1)
            G_.tensor_tensor(by_head(xD[:, c % 2], HD), by_head(xt[:, CT + c, :], HD), per_head(GP[:, R_D, 0, :], HD),
                             ALU.mult).then_inc(s_x_d, 1)

        def weighted(g, i):
            if i >= 2:
                pool.wait_ge(s_x_weighted_lo, STEPS * g + i - 1)
            for d, u in ((0, FWD[i]), (1, BWD[i])):
                done = G_.tensor_tensor(by_head(xw[:, i % 2, d * GW:(d + 1) * GW], HD), by_head(xt[:, u, :], HD),
                                        per_head(GP[:, R_WE + i, d, :], HD), ALU.mult)
            done.then_inc(s_x_weighted, 1)

        def state_lo(g, i):
            pool.wait_ge(s_state_hi, LT * g + i)
            G_.tensor_tensor(Hlo[:, i - 1, 0, :], hcur[:, 0:GW], f(Hhi[:, i - 1, 0, :]), ALU.subtract)
            G_.tensor_tensor(Hlo[:, LT - i, 1, :], hcur[:, GW:2 * GW], f(Hhi[:, LT - i, 1, :]),
                             ALU.subtract).then_inc(s_state_lo, 1)

        with pool.Fori(0, SSM_GROUPS - 1) as g:
            ssd(g, False)
        ssd(SSM_GROUPS - 1, True)
        for c in range(2, 2 * KT):
            weight_lo(W_OUT1 + c, (W_OUT1 + c) % 2, c % NR)
        out_rstd(1)

    @block.tensor
    def _(pe):
        def mm3(out, a_hi, a_lo, b_hi, b_lo, start, stop):
            PE_.matmul(out, a_hi, b_hi, start=start, stop=False, skip_group_check=True)
            PE_.matmul(out, a_hi, b_lo, start=False, stop=False, skip_group_check=True)
            return PE_.matmul(out, a_lo, b_hi, start=False, stop=stop, skip_group_check=True)

        pe.wait_ge(s_constants_made, 4)
        pe.wait_ge(s_x_normed, TT)
        for k in range(KT):
            ps = (psS, psT)[k % 2]
            if k >= 2:
                pe.wait_ge(s_h_scaled, k - 1)
            for t in range(TT):
                last = PE_.transpose(ps[:, t * P:(t + 1) * P], X0[:, t, k * P:(k + 1) * P], ident[:])
            last.then_inc(s_x_transposed, 1)

        def project(e, kind, part, k0, k1, w, done):
            par = kind
            toks = slice(0, CTX) if part == 0 else slice(CTX, TOK)
            out = psC[:, 0:CTX] if part == 0 else psL[kind][:, :]
            for i in range(k0, k1):
                k, m = divmod(i, 3)
                if m == 0 and kind == 0 and part == 0 and isinstance(e, int) and e == 0:
                    pe.wait_ge(s_h_lo, k + 1)
                a = (whi, whi, wlo)[m][:, par, k, :]
                b = (hhi, hlo, hhi)[m][:, k, toks]
                last = PE_.matmul(out, a, b, start=i == 0, stop=i == 3 * KT - 1, skip_group_check=True)
                if i == 3 * KT - 1:
                    last.then_inc(done, 1)

        def ctx_bank_free(e, kind):
            if kind == 0:
                if isinstance(e, int) and e <= GROUPS:
                    if e:
                        pe.wait_ge(s_tanh_ctx, e)
                else:
                    pe.wait_ge(s_gate_ctx, e - GROUPS)
            else:
                pe.wait_ge(s_q_ctx_evacuated, e + 1)

        def lat_bank_free(e, kind):
            if kind == 0:
                if not (isinstance(e, int) and e == 0):
                    pe.wait_ge(s_q_lat_evacuated, e)
            elif isinstance(e, int) and e <= GROUPS:
                if e:
                    pe.wait_ge(s_tanh_lat, e)
            else:
                pe.wait_ge(s_gate_lat, e - GROUPS)

        def tile_ready(w):
            pe.wait_ge(s_weight_hi, w + 1)
            pe.wait_ge(s_weight_lo, w + 1)

        def project_tile(e, kind, w):
            tile_ready(w)
            ctx_bank_free(e, kind)
            project(e, kind, 0, 0, 3 * KT, w, (s_q_ctx_proj, s_g_ctx_proj)[kind])
            lat_bank_free(e, kind)
            project(e, kind, 1, 0, 3 * KT, w, (s_q_lat_proj, s_g_lat_proj)[kind])

        def square_sums(u, e, pairs=None):
            pe.wait_ge(s_q_lat_evacuated, e + 1)
            if not (isinstance(u, int) and u == 0):
                pe.wait_ge(s_qk_variance, u)
            if pairs is not None:
                pe.wait_ge(s_y_gated, pairs)
            for t in range(TT):
                last = PE_.matmul(psV[:, t:t + 1], SQ[:, t * P:(t + 1) * P], ones[:, 0:1],
                                  start=True, stop=True, skip_group_check=True)
            last.then_inc(s_qk_square_sums, 1)

        def finish_kv(g):
            if g >= 2:
                square_sums(g - 2, g)
            pe.wait_ge(s_tanh_lat, g + 1)
            if g >= 1:
                pe.wait_ge(s_v_lo, g)
            if g >= 3:
                pe.wait_ge(s_k_normed, g - 2)
            for t in range(TT):
                last = PE_.transpose(psT[:, t * P:(t + 1) * P], TH[:, t * P:(t + 1) * P], ident[:])
            last.then_inc(s_v_transposed, 1)
            if g >= 2:
                pe.wait_ge(s_k_rstd_diag, g - 1)
                pe.wait_ge(s_v_lo, g + 1)
                for t in range(TT):
                    last = PE_.matmul(psT[:, t * P:(t + 1) * P], ones[:], dgk[:, t, :], start=True, stop=True,
                                      skip_group_check=True)
                last.then_inc(s_k_rstd_rows, 1)

        for e in range(GROUPS + 1):
            project_tile(e, 0, 2 * e)
            if e:
                finish_kv(e - 1)
            project_tile(e, 1, 2 * e + 1)

        def scores(r, s):
            n = SLOTS * r + s
            hs, b = s // BLOCKS, s % BLOCKS
            banded, (lo, hi, a) = hs < 2, window(b, hs < 2)
            if b == 0:
                pe.wait_ge(s_q_lo, GROUPS + GROUPS * r + hs + 1)
            if s:
                pe.wait_ge(s_probs, n)
            q = slice(b * P, (b + 1) * P)
            qh, ql = Qhi[:, hs % 2, q], Qlo[:, hs % 2, q]
            if hi > lo:
                keys = slice(CTX + lo * P, CTX + hi * P)
                i = b - CT
                mm3(psS[:, a:SEQ], qh, ql, Khi[:, hs, keys], Klo[:, hs, keys], True, not banded)
                if banded and i >= 1:
                    PE_.matmul(psS[:, a:a + P], identr[:], maskr[:, 0, :], start=False, stop=i == LT - 1,
                               skip_group_check=True)
                if banded and i < LT - 1:
                    PE_.matmul(psS[:, SEQ - P:SEQ], identr[:], maskr[:, 1, :], start=False, stop=True,
                               skip_group_check=True)
            mm3(psS[:, SEQ:TOK], qh, ql, Khi[:, hs, 0:CTX], Klo[:, hs, 0:CTX], True, True).then_inc(s_scores, 1)

        def transposes(r, s):
            n = SLOTS * r + s
            lo, hi, a = window(s % BLOCKS, s // BLOCKS < 2)
            pe.wait_ge(s_probs_normed, n + 1)
            if s:
                pe.wait_ge(s_probs_t_lo, n)
            for t in range(a // P, TT):
                last = PE_.transpose(psT[:, t * P:(t + 1) * P], PR[:, s % 2, t * P:(t + 1) * P], ident[:])
            last.then_inc(s_probs_transposed, 1)

        def values(r, pair):
            hs, q = pair // PAIRS, pair % PAIRS
            p = PAIRS * GROUPS * r + pair
            pe.wait_ge(s_probs_t_lo, 2 * p + 2)
            if pair:
                pe.wait_ge(s_y_gated, p)
            if q == 1 and hs in (1, 2):
                pe.wait_ge(s_qk_variance, 2 * r + hs + 2)
            todo = [(c, SEQ // P + c, 0, 2) for c in range(CT)]
            if q:
                b = 2 * q
                (lo0, hi0, a0), (lo1, hi1, a1) = window(b, hs < 2), window(b + 1, hs < 2)
                slot = lambda kt, lo, a: a // P + kt - lo
                for kt in range(min(lo0, lo1), max(hi0, hi1)):
                    in0, in1 = lo0 <= kt < hi0, lo1 <= kt < hi1
                    if in0 and in1 and slot(kt, lo0, a0) == slot(kt, lo1, a1):
                        todo.append((CT + kt, slot(kt, lo0, a0), 0, 2))
                    else:
                        if in0:
                            todo.append((CT + kt, slot(kt, lo0, a0), 0, 1))
                        if in1:
                            todo.append((CT + kt, slot(kt, lo1, a1), 1, 2))
            for i, (kt, sl, x0, x1) in enumerate(todo):
                x = slice(x0 * P, x1 * P)
                last = mm3(psV[:, x0 * P:x1 * P], Vhi[:, kt, hs * P:(hs + 1) * P],
                           Vlo[:, kt, hs * P:(hs + 1) * P], PThi[:, sl, x], PTlo[:, sl, x], i == 0,
                           i == len(todo) - 1)
            last.then_inc(s_pv_done, 1)

        def next_part(r, s, h, last):
            hs = min(s // BLOCKS, GROUPS - 1)
            if last and hs == GROUPS - 1:
                return
            e, w = GROUPS + GROUPS * r + hs + 1, W_HEAD0 + 2 * (GROUPS * r + hs + 1)
            at = 2 * (s - hs * BLOCKS) + h
            if hs < GROUPS - 1:
                i0, i1 = 8 * at, 8 * at + 8
            else:
                i0, i1 = (6 * at, 6 * at + 6) if at < 12 else (72 + 12 * ((at - 12) // 2), 72 + 12 * ((at - 12) // 2) + 12)
                if at >= 12 and h == 1:
                    return
            kind, part, i0 = i0 // 48, i0 // 24 % 2, i0 % 24
            i1 = i0 + (8 if hs < GROUPS - 1 else 6 if at < 12 else 12)
            if i0 == 0 and part == 0:
                tile_ready(w + kind)
                ctx_bank_free(e, kind)
            if i0 == 0 and part == 1:
                lat_bank_free(e, kind)
            project(e, kind, part, i0, i1, w + kind, ((s_q_ctx_proj, s_g_ctx_proj), (s_q_lat_proj, s_g_lat_proj))[part][kind])

        def attention(r, last):
            for s in range(SLOTS + 2):
                hs, b = s // BLOCKS, s % BLOCKS
                if s < SLOTS:
                    scores(r, s)
                if s >= 3 and s % 2 and s < SLOTS:
                    values(r, (s - 3) // 2)
                next_part(r, s, 0, last)
                if 1 <= s <= SLOTS:
                    transposes(r, s - 1)
                next_part(r, s, 1, last)
                if (h := due(s, 4, 5)) is not None and not (last and h == GROUPS - 1) and (h + 1) % GROUPS >= 2:
                    square_sums(2 * r + h + 1, GROUPS + GROUPS * r + h + 1, PAIRS * (GROUPS * r + h) + 1)
                if s == SLOTS + 1:
                    values(r, PAIRS * GROUPS - 1)

        with pe.Fori(0, HEADS // GROUPS - 1) as r:
            attention(r, False)
        attention(HEADS // GROUPS - 1, True)

        def tail(layer, w, y_hi, y_lo):
            tile_ready(w)
            for t in range(OUT_TILES[layer]):
                q = slice(t * P, (t + 1) * P)
                for i in range(4):
                    if t == 0 and i == 2:
                        tile_ready(w + 1)
                    k = HEADS - 4 + i
                    x = slice(4 * (i % 2), 4 * (i % 2) + 4)
                    wh = whi[:, (w + i // 2) % 2, x, :].rearrange("p a b -> p (a b)")
                    wl = wlo[:, (w + i // 2) % 2, x, :].rearrange("p a b -> p (a b)")
                    last = mm3(tok_bank[t], y_hi[:, k, q], y_lo[:, k, q], wh, wl, False, i == 3)
                last.then_inc(s_out_half, 1)

        for nh in range(2):
            for c in range(KT - 2 * nh):
                w = W_OUT0 + nh * KT + c
                tile_ready(w)
                for kk in range(2):
                    k = 2 * c + kk
                    wh = whi[:, w % 2, 4 * kk:4 * kk + 4, :].rearrange("p a b -> p (a b)")
                    wl = wlo[:, w % 2, 4 * kk:4 * kk + 4, :].rearrange("p a b -> p (a b)")
                    if nh == 0:
                        pe.wait_ge(s_y_lo, k + 1)
                    for t in range(TT):
                        if k == 0:
                            if nh == 0 and t == 0:
                                pe.wait_ge(s_y_gated, PAIRS * HEADS)
                                pe.wait_ge(s_probs_t_lo, BLOCKS * HEADS)
                            if nh == 1:
                                pe.wait_ge(s_out_evacuated, t + 1)
                        q = slice(t * P, (t + 1) * P)
                        last = mm3(tok_bank[t], Yhi[:, k, q], Ylo[:, k, q], wh, wl, k == 0, k == HEADS - 1)
                        if k == HEADS - 1:
                            last.then_inc(s_out_half, 1)
                if c < KT - 1:
                    last.then_inc(s_weight_used, 1)
                if nh == 0 and c in (4, 6):
                    v = (c - 4) // 2
                    if v:
                        pe.wait_ge(s_gate_rows_out, 1)
                    for k in range(KT):
                        pe.wait_ge(s_gate_diag, v * KT + k + 1)
                        last = PE_.matmul(psT[:, k * P:(k + 1) * P], ones[:], dg[:, k, :], start=True,
                                          stop=True, skip_group_check=True)
                        last.then_inc(s_gate_diag_used, 1)

        tail(0, W_OUT0 + 2 * KT - 2, Yhi, Ylo)

        pe.wait_ge(s_x_normed, TT + TT)
        for k in range(KT):
            ps = (psS, psT)[k % 2]
            if k >= 2:
                pe.wait_ge(s_h_scaled, KT + k - 1)
            for t in range(TT):
                last = PE_.transpose(ps[:, t * P:(t + 1) * P], XN[:, t, k * P:(k + 1) * P], ident[:])
            last.then_inc(s_x_transposed, 1)
        H2_ = 2 * SSM_HEADS
        tile_ready(W_DT)
        for out, toks in ((psC[0:H2_, 0:CTX], slice(0, CTX)), (psL[0][0:H2_, :], slice(CTX, TOK))):
            for k in range(KT):
                pe.wait_ge(s_h_lo, KT + k + 1)
                last = mm3(out, whi[:, 0, k, 0:H2_], wlo[:, 0, k, 0:H2_], h1hi[:, k, toks], h1lo[:, k, toks], k == 0,
                           k == KT - 1)
        last.then_inc(s_dt_projected, 1)
        pe.wait_ge(s_dt_evacuated, 1)
        for t in range(TT):
            last = PE_.transpose(psT[:, t * H2_:(t + 1) * H2_], CTH[0:H2_, t * P:(t + 1) * P], ident[0:H2_, 0:H2_])
        last.then_inc(s_dt_projected, 1)

        def project1(g, i, part, k0, k1, q2):
            toks = slice(0, CTX) if part == 0 else slice(CTX, TOK)
            out = psC[:, 0:CTX] if part == 0 else psL[i % 2][:, :]
            for j in range(k0, k1):
                k, m = divmod(j, 3)
                last = PE_.matmul(out, (whi, whi, wlo)[m][:, q2, k, :], (h1hi, h1lo, h1hi)[m][:, k, toks],
                                  start=j == 0, stop=j == 3 * KT - 1, skip_group_check=True)
            if k1 == 3 * KT:
                last.then_inc((s_tile_ctx_projected, s_tile_lat_projected)[part], 1)

        def tile_start(g, i, part, w, first):
            if part == 0 or i == 3:
                tile_ready(w)
            if part == 0:
                if not (first and i == 0):
                    pe.wait_ge(s_conv_ctx, 3 * g + i)
            elif not (first and i < 2):
                pe.wait_ge(s_conv_lat, 4 * g + i - 1)

        def running_sums():
            pe.wait_ge(s_a_split, 3)
            pe.wait_ge(s_triangles, TRI_STEPS)
            cF = psL[1][:, 0:TT * H2_].rearrange("p (t h) -> p t h", t=TT)
            for d in range(DIRS):
                h = slice(d * SSM_HEADS, (d + 1) * SSM_HEADS)
                PE_.matmul(cF[:, :, h], trir[:, d, :], ahi[:, :, h], start=True, stop=False, skip_group_check=True)
                PE_.matmul(cF[:, :, h], trir[:, d, :], alo[:, :, h], start=False, stop=True, skip_group_check=True)
            PE_.matmul(psS[:, 0:TT * H2_], onesr[:], ahi[:].rearrange("p t h -> p (t h)"), start=True, stop=False,
                       skip_group_check=True)
            PE_.matmul(psS[:, 0:TT * H2_], onesr[:], alo[:].rearrange("p t h -> p (t h)"), start=False, stop=True,
                       skip_group_check=True).then_inc(s_running_sums, 1)

        for i in range(4):
            for part in range(2):
                if i == 3 and part == 0:
                    continue
                tile_start(0, i, part, W_SSM + i, True)
                if i == 1 and part == 1:
                    pe.wait_ge(s_running_sums, 2)
                project1(0, i, part, 0, 3 * KT, (W_SSM + i) % 2)
                if i == 0 and part == 1:
                    running_sums()

        def ssd(g, last_group):
            G = g + 1
            def tokens(i):
                pe.wait_ge(s_conv_done, 4 * g + i + 1)
                if i:
                    pe.wait_ge(s_tokens_out, 3 * g + i)
                for t in range(TT):
                    last = PE_.transpose(psT[:, t * P:(t + 1) * P], U[i][:, t * P:(t + 1) * P], ident[:])
                last.then_inc(s_tokens_transposed, 1)

            def z(half, cs):
                for c in cs:
                    q = slice((CT + c) * P, (CT + c + 1) * P)
                    for kk in range(KT // 2):
                        k = half * KT // 2 + kk
                        slot = (1, 0)[half]
                        wh = whi[:, slot, 2 * kk:2 * kk + 2, :].rearrange("p a b -> p (a b)")
                        wl = wlo[:, slot, 2 * kk:2 * kk + 2, :].rearrange("p a b -> p (a b)")
                        last = mm3(psS[:, c * GW:(c + 1) * GW], h1hi[:, k, q], h1lo[:, k, q], wh, wl,
                                   k == 0 and c % 2 == 0, k == KT - 1)
                return last

            def next_part(p):
                if last_group:
                    return
                i, part = ((0, 0), (0, 1), (1, 0), (1, 1), (2, 0), (2, 1), (3, 1))[p // 2]
                if p % 2 == 0:
                    tile_start(G, i, part, W_SSM + 6 + 6 * g + i, False)
                project1(G, i, part, 12 * (p % 2), 12 * (p % 2) + 12, (1, 0, 1, 0)[i])

            def log_decays(c):
                if c == 0:
                    pe.wait_ge(s_b_tokens_lo, g + 1)
                    pe.wait_ge(s_group_a, g + 1)
                else:
                    pe.wait_ge(s_decays, LT * g + c)
                for d in range(DIRS):
                    bank = psT[:, d * 512:(d + 1) * 512]
                    PE_.matmul(bank, identr[:], negr[:, d, :].unsqueeze(1).broadcast_to([P, GH, P]), start=True,
                               stop=False, skip_group_check=True)
                    for h in range(GH):
                        for m, a in enumerate((aghi, aglo)):
                            last = PE_.matmul(bank[:, h * P:(h + 1) * P], a[:, c, d, h:h + 1].broadcast_to([P, P]),
                                              trir[:, d, :], start=False, stop=m == 1, skip_group_check=True)
                last.then_inc(s_log_decays, 1)

            def cb(c):
                q = slice(c * P, (c + 1) * P)
                mm3(ybank[1][:, 0:P], bfhi[:, 0, q], bflo[:, 0, q], bfhi[:, 1, q], bflo[:, 1, q], True,
                    True).then_inc(s_cb_done, 1)

            tile_ready(W_SSM + 4 + 6 * g)
            tokens(0)
            z(0, (0, 1))
            tokens(1)
            z(0, (2, 3)).then_inc(s_z_weight_used, 1)
            tokens(2)
            tile_ready(W_SSM + 5 + 6 * g)
            z(1, (0, 1))
            z(1, (2, 3)).then_inc(s_z_weight_used, 1)
            log_decays(0)
            pe.wait_ge(s_z_silu, g + 1)
            pe.wait_ge(s_bc_lo, g + 1)
            cb(0)
            for i in range(STEPS):
                pe.wait_ge(s_x_weighted_lo, STEPS * g + i + 1)
                if i:
                    pe.wait_ge(s_state_new, STEPS * g + i)
                for d, u in ((0, FWD[i]), (1, BWD[i])):
                    x = slice(d * GW, (d + 1) * GW)
                    last = mm3(ybank[0][:, x], bthi[:, u, :], btlo[:, u, :], xwhi[:, i % 2, x], xwlo[:, i % 2, x],
                               True, True)
                last.then_inc(s_state_added, 1)
                if i == 2:
                    log_decays(1)
                next_part(i)
            next_part(STEPS)
            pe.wait_ge(s_tokens_lo, g + 1)
            for c in range(LT):
                n = LT * g + c
                pe.wait_ge(s_cb_decayed_lo, n + 1)
                for h in range(GH):
                    x, m = slice(h * HD, (h + 1) * HD), slice(h * P, (h + 1) * P)
                    last = mm3(ybank[1][:, P + h * HD:P + (h + 1) * HD], Mhi[:, m], Mlo[:, m], xthi[:, c, x],
                               xtlo[:, c, x], True, True)
                last.then_inc(s_y_chunk, 1)
                if c == 0:
                    pe.wait_ge(s_state_new, STEPS * (g + 1))
                    pe.wait_ge(s_state_lo, LT * (g + 1))
                else:
                    pe.wait_ge(s_y_off_scaled, n)
                q = slice(c * P, (c + 1) * P)
                mm3(ybank[0], bfhi[:, 1, q], bflo[:, 1, q], Hhi[:, c].rearrange("p d x -> p (d x)"),
                    Hlo[:, c].rearrange("p d x -> p (d x)"), True, True).then_inc(s_y_off_done, 1)
                next_part(6 + 2 * c)
                if c < LT - 1:
                    pe.wait_ge(s_y_diag_d, n + 1)
                    cb(c + 1)
                if c < LT - 2:
                    log_decays(c + 2)
                if c:
                    y_transposed(g, c - 1)
                next_part(7 + 2 * c)
            y_transposed(g, LT - 1)

        def y_transposed(g, c):
            pe.wait_ge(s_y_normed, LT * g + c + 1)
            if c:
                pe.wait_ge(s_y_out, LT * g + c)
            for i in range(2):
                last = PE_.transpose(psV[:, i * P:(i + 1) * P], ynm[:, i * P:(i + 1) * P], ident[:])
            last.then_inc(s_y_transposed, 1)

        with pe.Fori(0, SSM_GROUPS - 1) as g:
            ssd(g, False)
        ssd(SSM_GROUPS - 1, True)

        for nh in range(2):
            for c in range(KT - 2 * nh):
                i = nh * KT + c
                tile_ready(W_OUT1 + i)
                for kk in range(2):
                    k = 2 * c + kk
                    sl = (W_OUT1 + i) % 2
                    wh = whi[:, sl, 4 * kk:4 * kk + 4, :].rearrange("p a b -> p (a b)")
                    wl = wlo[:, sl, 4 * kk:4 * kk + 4, :].rearrange("p a b -> p (a b)")
                    if nh == 0:
                        pe.wait_ge(s_y_lo, HEADS + k + 1)
                    for t in range(LT):
                        if k == 0 and nh == 1:
                            pe.wait_ge(s_out_evacuated, OUT_YO[1] + t + 1)
                        q = slice(t * P, (t + 1) * P)
                        last = mm3(tok_bank[t], Y1hi[:, k, q], Y1lo[:, k, q], wh, wl, k == 0, k == HEADS - 1)
                        if k == HEADS - 1:
                            last.then_inc(s_out_half, 1)
                if c < KT - 1:
                    last.then_inc(s_weight_used, 1)
                if nh == 0 and c == 4:
                    for k in range(KT):
                        pe.wait_ge(s_gate1_diag, k + 1)
                        PE_.matmul(psT[:, k * P:(k + 1) * P], ones[:], dg1[:, k, :], start=True, stop=True,
                                   skip_group_check=True).then_inc(s_gate1_rows, 1)
        tail(1, W_OUT1 + 2 * KT - 2, Y1hi, Y1lo)


def kernel(**inputs):
    import numpy as np
    import concourse.bacc as bacc
    from concourse.bass_utils import run_bass_kernel_spmd as run
    a = {k: np.asarray(v) for k, v in inputs.items()}
    f32 = mybir.dt.float32

    def tiles(w, columns):
        w = w[:, columns].reshape(KT, P, -1, P)
        return np.ascontiguousarray(w.transpose(2, 1, 0, 3))

    def colvec(v):
        return v.reshape(-1, P).T

    def out_chunks(w):
        w = w.reshape(-1, 2, P, 2, 512)
        return np.ascontiguousarray(w.transpose(3, 0, 2, 1, 4).reshape(-1, P, KT, P))

    split = np.concatenate([np.arange(0, P, 2), np.arange(1, P, 2)])
    off = dict(zip(("qa", "ka", "va", "ga", "qb", "kb", "vb", "gb"), (0, 1024, 1280, 1536, 2560, 3584, 3840, 4096)))
    order, rows_out, sinks = [], [], []
    for g in range(GROUPS):
        t = "ab"[g // 2]
        order += [off["k" + t] + (g % 2) * P + split, off["v" + t] + (g % 2) * P + np.arange(P)]
    for r in range(HEADS // GROUPS):
        for g in range(GROUPS):
            t, h = "ab"[g // 2], (g % 2) * GROUPS + r
            order += [off["q" + t] + h * P + split, off["g" + t] + h * P + np.arange(P)]
            rows_out.append((g // 2) * 1024 + h * P + np.arange(P))
            if g < 2:
                sinks.append(h)
    order, rows_out = np.concatenate(order), np.concatenate(rows_out)

    inv = 1.0 / (np.float32(10000.0) ** (np.arange(32, dtype=np.float32) / np.float32(32)))
    row = np.repeat(np.arange(SEQ // 64), 64).astype(np.float32)
    colp = np.tile(np.arange(64), SEQ // 64).astype(np.float32)
    ang = np.concatenate([row[:, None] * inv, colp[:, None] * inv], -1).astype(np.float32).T
    cos, sin = np.cos(ang).astype(np.float32), np.sin(ang).astype(np.float32)

    cw = a["ssm_conv_w"][0]
    columns = [colvec(a["b_ada"].reshape(-1)), colvec(a["norm_pre"].reshape(-1)), colvec(a["norm_post"].reshape(-1)),
               colvec(cw.reshape(-1)), colvec(a["ssm_conv_b"][0]), colvec(a["ssm_norm"][0]),
               a["attn_q_norm"][0][split][:, None], a["attn_k_norm"][0][split][:, None]]
    wi = a["ssm_w_in"][0]
    ssm = []
    for g in range(SSM_GROUPS):
        x = [tiles(wi, 2048 + 256 * g + np.arange(256)), tiles(wi, 4096 + P * g + np.arange(P)),
             tiles(wi, 5120 + P * g + np.arange(P))]
        z = wi[:, 256 * g:256 * g + 256].reshape(2, 4, P, 256).transpose(0, 2, 1, 3).reshape(2, P, KT, P)
        ssm += x + [z]
    ada = [a["w_ada"][l].T.reshape(-1, P, KT, P) for l in range(2)]
    arrays = {
        "xc": np.concatenate([a["ctx"][0], a["x"][0]]).reshape(TT, P, D_MODEL),
        "cvec": np.stack([a["c"][0], a["c_ctx"]]),
        "cols": np.concatenate(columns, 1),
        "rows": np.concatenate([a["attn_sink"][0][sinks], a["ssm_a_log"][0].reshape(-1),
                                a["ssm_dt_bias"][0].reshape(-1), a["ssm_d"][0]]),
        "w_ada": ada[0][None, :ADA_EARLY],
        "w_ada_late": np.concatenate([ada[0][ADA_EARLY:], ada[1]]),
        "w_in": tiles(a["attn_w_in"][0], order),
        "w_out0": out_chunks(a["attn_w_out"][0][rows_out]),
        "w_ssm": np.concatenate(ssm),
        "w_dt": wi[:, 6144:6208].reshape(KT, P, 64).transpose(1, 0, 2),
        "w_out1": out_chunks(a["ssm_w_out"][0]),
        "cos": np.concatenate([cos, cos]), "sin": np.concatenate([sin, -sin]),
    }
    arrays = {"in_" + k: np.ascontiguousarray(v) for k, v in arrays.items()}
    nc = bacc.Bacc("TRN2", target_bir_lowering=False, num_devices=1)
    io = {k[3:]: nc.dram_tensor(k, v.shape, f32, kind="ExternalInput").ap() for k, v in arrays.items()}
    io["out"] = nc.dram_tensor("out", (LT, P, D_MODEL), f32, kind="ExternalOutput").ap()
    io["y_spill"] = nc.dram_tensor("y_spill", (HEADS, P, TOK), f32, kind="Internal").ap()
    io["x1_spill"] = nc.dram_tensor("x1_spill", (LT, P, D_MODEL), f32, kind="Internal").ap()
    io["y1_spill"] = nc.dram_tensor("y1_spill", (SSM_GROUPS, P, 2, SEQ), f32, kind="Internal").ap()
    build(nc, io)
    r = run(nc, [arrays], core_ids=[0])
    return r.results[0]["out"].reshape(1, SEQ, D_MODEL)
```
